# Optimizing a Trainium2 kernel written in Bass

```python
import jax, jax.numpy as jnp
from jax import lax
import numpy as np

D_MODEL = 1024
BATCH = 1
SEQ = 128
DEPTH = 1
DEC_BATCH = 1
DEC_SEQ = 512
PAST_LEN = 256

GRID_W = 64
D_CONV = 512
CONV_K = 31
D_MLSTM = 512
N_HEADS = 4
HEAD_DIM = D_MLSTM // N_HEADS
CHUNK = 64
N_GROUPS = 4
EXPERTS_PER_GROUP = 4
N_EXPERTS = N_GROUPS * EXPERTS_PER_GROUP
TOP_K_IN_GROUP = 2
D_EXPERT = 256
N_ADA = 6
EPS = 1e-6
N_IN = 2 * D_CONV + 4 * D_MLSTM + 4 * N_HEADS + 2 * D_MODEL

kernel_name = 'hybrid_conv_mlstm_hmoe_diffusion_step'

def _in_splits():
    s0 = D_CONV
    s1 = 2 * D_CONV
    s2 = s1 + D_MLSTM
    s3 = s2 + D_MLSTM
    s4 = s3 + D_MLSTM
    s5 = s4 + D_MLSTM
    s6 = s5 + 4 * N_HEADS
    s7 = s6 + D_MODEL
    return [s0, s1, s2, s3, s4, s5, s6, s7]

def rms_norm(x, g):
    x32 = x.astype(jnp.float32)
    y = x32 * lax.rsqrt(jnp.mean(x32 * x32, axis=-1, keepdims=True) + EPS)
    return (y * g.astype(jnp.float32)).astype(x.dtype)

def layer_norm(x, g, b):
    x32 = x.astype(jnp.float32)
    mu = jnp.mean(x32, axis=-1, keepdims=True)
    xc = x32 - mu
    y = xc * lax.rsqrt(jnp.mean(xc * xc, axis=-1, keepdims=True) + EPS)
    return (y * g.astype(jnp.float32) + b.astype(jnp.float32)).astype(x.dtype)

def depthwise_conv(u, w, b, grid_w):
    B, T, C = u.shape
    if grid_w is not None:
        rows = T // grid_w
        u = u.reshape(B * rows, grid_w, C)
    y = lax.conv_general_dilated(
        u, w[:, None, :].astype(u.dtype), window_strides=(1,),
        padding=[(CONV_K // 2, CONV_K // 2)],
        dimension_numbers=('NWC', 'WIO', 'NWC'), feature_group_count=C)
    return (y + b.astype(y.dtype)).reshape(B, T, C)

def mlstm_dir(q, k, v, i_pre, f_pre, C0, n0, m0):
    B, H, T, Dh = q.shape
    nc = T // CHUNK
    q = q.astype(jnp.float32) * (HEAD_DIM ** -0.5)
    k = k.astype(jnp.float32)
    v = v.astype(jnp.float32)
    li = i_pre.astype(jnp.float32)
    lf = jax.nn.log_sigmoid(f_pre.astype(jnp.float32))

    def chunks(a):
        return jnp.moveaxis(a.reshape(a.shape[:2] + (nc, CHUNK) + a.shape[3:]), 2, 0)

    causal = jnp.tril(jnp.ones((CHUNK, CHUNK), dtype=bool))

    def step(carry, xs):
        C, n, m = carry
        qc, kc, vc, ic, lfc = xs
        bcum = jnp.cumsum(lfc, axis=-1)
        dmat = bcum[..., :, None] - bcum[..., None, :] + ic[..., None, :]
        dmat = jnp.where(causal, dmat, -jnp.inf)
        m_inter = bcum + m[..., None]
        m_t = jnp.maximum(m_inter, jnp.max(dmat, axis=-1))
        w_intra = jnp.exp(dmat - m_t[..., None])
        w_inter = jnp.exp(m_inter - m_t)
        s = jnp.einsum('bhtd,bhsd->bhts', qc, kc) * w_intra
        num = jnp.einsum('bhts,bhsd->bhtd', s, vc) + w_inter[..., None] * jnp.einsum('bhtd,bhde->bhte', qc, C)
        den = jnp.sum(s, axis=-1) + w_inter * jnp.einsum('bhtd,bhd->bht', qc, n)
        h = num / jnp.maximum(jnp.abs(den), jnp.exp(-m_t))[..., None]
        b_last = bcum[..., -1]
        g = b_last[..., None] - bcum + ic
        m_new = jnp.maximum(b_last + m, jnp.max(g, axis=-1))
        wk = jnp.exp(g - m_new[..., None])
        decay = jnp.exp(b_last + m - m_new)
        C_new = decay[..., None, None] * C + jnp.einsum('bhs,bhsd,bhse->bhde', wk, kc, vc)
        n_new = decay[..., None] * n + jnp.einsum('bhs,bhsd->bhd', wk, kc)
        return (C_new, n_new, m_new), h

    init = (C0.astype(jnp.float32), n0.astype(jnp.float32), m0.astype(jnp.float32))
    (C, n, m), h = lax.scan(step, init, (chunks(q), chunks(k), chunks(v), chunks(li), chunks(lf)))
    h = jnp.moveaxis(h, 0, 2).reshape(B, H, T, Dh)
    return h, (C, n, m)

def bi_mlstm(q, k, v, ig, fg, C0, n0, m0):
    hf, (Cf, nf, mf) = mlstm_dir(q, k, v, ig[:, 0], fg[:, 0], C0[:, 0], n0[:, 0], m0[:, 0])
    flip = lambda a: jnp.flip(a, axis=2)
    hb, (Cb, nb, mb) = mlstm_dir(flip(q), flip(k), flip(v), flip(ig[:, 1]), flip(fg[:, 1]),
                                 C0[:, 1], n0[:, 1], m0[:, 1])
    h = hf + flip(hb)
    return h, (jnp.stack([Cf, Cb], axis=1), jnp.stack([nf, nb], axis=1), jnp.stack([mf, mb], axis=1))

def hier_moe(h, p):
    B, T, D = h.shape
    x = h.reshape(B * T, D)
    gl = (x @ p['w_rg']).astype(jnp.float32) + p['b_rg'].astype(jnp.float32)
    gp = jax.nn.softmax(gl, axis=-1)
    gp_sel, gsel = lax.top_k(gp, 1)
    el = (x @ p['w_re']).astype(jnp.float32) + p['b_re'].astype(jnp.float32)
    el = el.reshape(-1, N_GROUPS, EXPERTS_PER_GROUP)
    el_sel = jnp.take_along_axis(el, gsel[:, :, None], axis=1)[:, 0]
    ep = jax.nn.softmax(el_sel, axis=-1)
    topv, topi = lax.top_k(ep, TOP_K_IN_GROUP)
    topv = topv / jnp.sum(topv, axis=-1, keepdims=True)
    weights = gp_sel * topv
    idx = gsel * EXPERTS_PER_GROUP + topi
    combine = jnp.einsum('nk,nke->ne', weights, jax.nn.one_hot(idx, N_EXPERTS, dtype=jnp.float32))
    combine = combine.astype(h.dtype)
    g = jnp.einsum('nd,edf->nef', x, p['w_e_gate'])
    u = jnp.einsum('nd,edf->nef', x, p['w_e_up'])
    act = jax.nn.silu(g) * u * combine[:, :, None]
    out = jnp.einsum('nef,efd->nd', act, p['w_e_down'])
    return out.reshape(B, T, D)

def trunk_layer(x, mod, C0, n0, m0, grid_w, p):
    B, T, _ = x.shape
    shift1, scale1, gate1, shift2, scale2, gate2 = (mod[:, i, None, :] for i in range(N_ADA))
    h = rms_norm(x, p['norm1_g']) * (1 + scale1) + shift1
    z = h @ p['w_in'] + p['b_in']
    a, ga, q, k, v, o, g_if, g_ma, g_mb = jnp.split(z, _in_splits(), axis=-1)
    u = a * jax.nn.sigmoid(ga)
    u = depthwise_conv(u, p['w_dw'], p['b_dw'], grid_w)
    u = jax.nn.silu(layer_norm(u, p['conv_ln_g'], p['conv_ln_b']))
    br_a = u @ p['w_conv_out']
    to_heads = lambda t: t.reshape(B, T, N_HEADS, HEAD_DIM).transpose(0, 2, 1, 3)
    g_if = (g_if.reshape(B, T, 2, 2, N_HEADS) + p['b_gates']).transpose(0, 2, 3, 4, 1)
    hm, st = bi_mlstm(to_heads(q), to_heads(k), to_heads(v), g_if[:, :, 0], g_if[:, :, 1], C0, n0, m0)
    hm = hm * lax.rsqrt(jnp.mean(hm * hm, axis=-1, keepdims=True) + EPS)
    hm = hm.transpose(0, 2, 1, 3).reshape(B, T, D_MLSTM) * p['mlstm_hn_g'].astype(jnp.float32)
    hm = (jax.nn.sigmoid(o.astype(jnp.float32)) * hm).astype(x.dtype)
    br_b = hm @ p['w_mlstm_out']
    mixed = (jax.nn.sigmoid(g_ma) * br_a + jax.nn.sigmoid(g_mb) * br_b) @ p['w_o']
    x = x + gate1 * mixed
    h2 = rms_norm(x, p['norm2_g']) * (1 + scale2) + shift2
    x = x + gate2 * hier_moe(h2, p)
    return x, st

def setup_inputs(seed: int = 0) -> dict:
    key = jax.random.key(seed)
    ks = jax.random.split(key, 32)
    nrm = lambda k, shape, s: jax.random.normal(k, shape, jnp.float32) * s
    D = D_MODEL
    f_bias = jnp.linspace(3.0, 6.0, N_HEADS, dtype=jnp.float32)
    gate_sel = jnp.array([0.0, 1.0], jnp.float32)[None, None, :, None]
    b_gates = nrm(ks[12], (DEPTH, 2, 2, N_HEADS), 0.1) + gate_sel * f_bias
    return {
        'x_prompt': nrm(ks[0], (BATCH, SEQ, D), 1.0),
        'x_sample': nrm(ks[1], (DEC_BATCH, DEC_SEQ, D), 1.0),
        'state_C': nrm(ks[2], (DEC_BATCH, DEPTH, 2, N_HEADS, HEAD_DIM, HEAD_DIM), 0.3),
        'state_n': nrm(ks[3], (DEC_BATCH, DEPTH, 2, N_HEADS, HEAD_DIM), 0.3),
        'state_m': nrm(ks[4], (DEC_BATCH, DEPTH, 2, N_HEADS), 0.5),
        'c': nrm(ks[5], (DEC_BATCH, D), 1.0),
        'c_ctx': nrm(ks[6], (D,), 1.0),
        'norm1_g': 1.0 + nrm(ks[7], (DEPTH, D), 0.05),
        'w_ada': nrm(ks[8], (DEPTH, D, N_ADA * D), 0.5 * D ** -0.5),
        'b_ada': nrm(ks[9], (DEPTH, N_ADA * D), 0.02),
        'w_in': nrm(ks[10], (DEPTH, D, N_IN), D ** -0.5),
        'b_in': nrm(ks[11], (DEPTH, N_IN), 0.02),
        'b_gates': b_gates,
        'w_dw': nrm(ks[13], (DEPTH, CONV_K, D_CONV), CONV_K ** -0.5),
        'b_dw': nrm(ks[14], (DEPTH, D_CONV), 0.02),
        'conv_ln_g': 1.0 + nrm(ks[15], (DEPTH, D_CONV), 0.05),
        'conv_ln_b': nrm(ks[16], (DEPTH, D_CONV), 0.02),
        'w_conv_out': nrm(ks[17], (DEPTH, D_CONV, D), D_CONV ** -0.5),
        'mlstm_hn_g': 1.0 + nrm(ks[18], (DEPTH, D_MLSTM), 0.05),
        'w_mlstm_out': nrm(ks[19], (DEPTH, D_MLSTM, D), D_MLSTM ** -0.5),
        'w_o': nrm(ks[20], (DEPTH, D, D), D ** -0.5),
        'norm2_g': 1.0 + nrm(ks[21], (DEPTH, D), 0.05),
        'w_rg': nrm(ks[22], (DEPTH, D, N_GROUPS), D ** -0.5),
        'b_rg': nrm(ks[23], (DEPTH, N_GROUPS), 0.01),
        'w_re': nrm(ks[24], (DEPTH, D, N_EXPERTS), D ** -0.5),
        'b_re': nrm(ks[25], (DEPTH, N_EXPERTS), 0.01),
        'w_e_gate': nrm(ks[26], (DEPTH, N_EXPERTS, D, D_EXPERT), D ** -0.5),
        'w_e_up': nrm(ks[27], (DEPTH, N_EXPERTS, D, D_EXPERT), D ** -0.5),
        'w_e_down': nrm(ks[28], (DEPTH, N_EXPERTS, D_EXPERT, D), D_EXPERT ** -0.5),
        'norm_final_g': 1.0 + nrm(ks[29], (D,), 0.05),
    }

def reference(x_prompt, x_sample, state_C, state_n, state_m, c, c_ctx, norm1_g, w_ada, b_ada,
              w_in, b_in, b_gates, w_dw, b_dw, conv_ln_g, conv_ln_b, w_conv_out, mlstm_hn_g,
              w_mlstm_out, w_o, norm2_g, w_rg, b_rg, w_re, b_re, w_e_gate, w_e_up, w_e_down,
              norm_final_g):
    B = x_prompt.shape[0]
    zC = jnp.zeros((B, 2, N_HEADS, HEAD_DIM, HEAD_DIM), jnp.float32)
    zn = jnp.zeros((B, 2, N_HEADS, HEAD_DIM), jnp.float32)
    zm = jnp.zeros((B, 2, N_HEADS), jnp.float32)
    xp, xs = x_prompt, x_sample
    new_C, new_n, new_m = [], [], []
    for l in range(DEPTH):
        p = {
            'norm1_g': norm1_g[l], 'w_in': w_in[l], 'b_in': b_in[l], 'b_gates': b_gates[l],
            'w_dw': w_dw[l], 'b_dw': b_dw[l], 'conv_ln_g': conv_ln_g[l], 'conv_ln_b': conv_ln_b[l],
            'w_conv_out': w_conv_out[l], 'mlstm_hn_g': mlstm_hn_g[l], 'w_mlstm_out': w_mlstm_out[l],
            'w_o': w_o[l], 'norm2_g': norm2_g[l], 'w_rg': w_rg[l], 'b_rg': b_rg[l], 'w_re': w_re[l],
            'b_re': b_re[l], 'w_e_gate': w_e_gate[l], 'w_e_up': w_e_up[l], 'w_e_down': w_e_down[l],
        }
        mod_ctx = (jax.nn.silu(c_ctx)[None, :] @ w_ada[l] + b_ada[l]).reshape(1, N_ADA, D_MODEL)
        mod_lat = (jax.nn.silu(c) @ w_ada[l] + b_ada[l]).reshape(-1, N_ADA, D_MODEL)
        xp, (Cl, nl, ml) = trunk_layer(xp, mod_ctx, zC, zn, zm, None, p)
        new_C.append(Cl)
        new_n.append(nl)
        new_m.append(ml)
        xs, _ = trunk_layer(xs, mod_lat, state_C[:, l], state_n[:, l], state_m[:, l], GRID_W, p)
    new_state_C = jnp.stack(new_C, axis=1)
    new_state_n = jnp.stack(new_n, axis=1)
    new_state_m = jnp.stack(new_m, axis=1)
    y_prompt = rms_norm(xp, norm_final_g)
    y_sample = rms_norm(xs, norm_final_g)
    return (y_prompt, y_sample, new_state_C, new_state_n, new_state_m)


_drawn_inputs = setup_inputs


def setup_inputs(seed=0):
    import zlib

    import numpy as np

    out = dict(_drawn_inputs(seed))
    spreads = {}
    factors = {'state_C': 8.0,
     'state_n': 8.0,
     'state_m': 8.0,
     'b_dw': 8.0,
     'conv_ln_g': 6.649,
     'conv_ln_b': 7.014,
     'mlstm_hn_g': 8.0,
     'norm2_g': 2.88,
     'b_rg': 8.0,
     'b_re': 7.197}
    for name, (base, spread) in spreads.items():
        noise = np.random.default_rng([zlib.crc32(name.encode()), seed]).standard_normal(out[name].shape)
        drawn = base * np.exp(spread * noise) if base else spread * noise
        out[name] = __import__('jax').numpy.asarray(drawn.astype(out[name].dtype))
    for name, factor in factors.items():
        out[name] = (out[name] * factor).astype(out[name].dtype)
    return out
```

```python
from contextlib import ExitStack

import concourse.bass as bass
from concourse import mybir

P = 128
D = 1024
KT = D // P
TP, TL = 128, 512
T = TP + TL
NT = T // P
HALF = T // 2
H, HD = 4, 128
DI = H * HD
CT = DI // P
CK = 31
PADW = CK // 2
GW = 64
ROWS = TL // GW
PITCH = GW + PADW
U0 = PADW
U1 = PADW + TP + PADW
UW = U1 + ROWS * PITCH
YW = UW - 2 * PADW
NE, GE, NG = 16, 4, 4
DE = 256
CAP = P
OVER = 9
NB = NE + OVER
CH = 2048
NRAW = 3
EPS = 1e-6
QS = HD ** -0.5
NEG = -1e30

F32, F32R, BF16, I32 = mybir.dt.float32, mybir.dt.float32r, mybir.dt.bfloat16, mybir.dt.int32
ALU = mybir.AluOpType
ACT = mybir.ActivationFunctionType
AX = mybir.AxisListType.X
MUL, ADD, SUB, MAX, MIN = ALU.mult, ALU.add, ALU.subtract, ALU.max, ALU.min

V_CTX, V_C, V_G1, V_BSH, V_BSC, V_BA, V_BGA, V_BQ, V_BK, V_BV, V_BO, V_BMA, V_BMB, V_BDW, V_LG, V_LB, V_HN, NV = (
    0, 8, 16, 24, 32, 40, 44, 48, 52, 56, 60, 64, 72, 80, 84, 88, 92, 96)

C_A, C_GA, C_Q, C_K, C_V, C_O, C_IF = 0, 512, 1024, 1536, 2048, 2560, 3072
C_MA, C_MB = C_IF + 16, C_IF + 16 + D


def units():
    u = [("ada", n) for n in range(8)]
    ada = iter(range(8, 24))

    def z(kind, n, with_ada=True):
        for i in range(n):
            u.append((kind, i))
            if with_ada and kind not in ("gmb",) or (with_ada and i < 2):
                k = next(ada, None)
                if k is not None:
                    u.append(("ada", k))

    for i in range(2):
        u.append(("ga", i))
        u.append(("a", i))
        u.append(("ada", next(ada)))
    for kind, n in (("v", 2), ("k", 2), ("q", 2), ("gma", 4), ("o", 2)):
        z(kind, n)
    for i in range(4):
        u.append(("gmb", i))
        k = next(ada, None)
        if k is not None:
            u.append(("ada", k))
    u += [("wc", 0), ("wm", 0), ("wc", 1), ("wm", 1)]
    u += [("wo", i) for i in range(4)]
    return u


UNITS = units()
G0 = len(UNITS)
WCOL = {"a": C_A, "ga": C_GA, "q": C_Q, "k": C_K, "v": C_V, "o": C_O, "gma": C_MA, "gmb": C_MB}
ZKINDS = tuple(WCOL)


def psum_tiles():
    out, by_unit = [], []
    for kind, i in UNITS:
        mine = []
        if kind == "ada":
            mine = [("ada", i)]
        elif kind in ZKINDS:
            mine = [(kind, 2 * i), (kind, 2 * i + 1)]
            if kind == "v" and i == 0:
                mine = [("gate", 0)] + mine
        by_unit.append([(len(out) + n, *m) for n, m in enumerate(mine)])
        out += mine
    return out, by_unit


TILES, TILES_OF = psum_tiles()
TILE_AT = {m: n for n, m in enumerate(TILES)}
UNIT_AT = {m: n for n, m in enumerate(UNITS)}


def chunk_order(first):
    return [0, 1, 2, 3, 4] if first == 0 else [0, 4, 3, 2, 1]


def build(nc, a, out):
    top = ExitStack()
    block_stack = ExitStack()

    def sem(name):
        return top.enter_context(nc.semaphore(name))

    def keep(name, shape, dt=F32):
        return top.enter_context(nc.sbuf_tensor(name, shape, dt))

    mod_d = nc.dram_tensor("mod_d", [4, 4 * D], F32, kind="Internal").ap()
    h2_d = nc.dram_tensor("h2_d", [T, D], F32, kind="Internal").ap()
    y_d = nc.dram_tensor("y_d", [NB * CAP, D], F32, kind="Internal").ap()

    ident = keep("ident", [P, P])
    identb = keep("identb", [P, P], BF16)
    ones = keep("ones", [P, P])
    onesb = keep("onesb", [P, P], BF16)
    mask = keep("mask", [P, 2, P], BF16)
    vcol = keep("vcol", [P, NV])
    taps = keep("taps", [P, CK * CT])
    cs = keep("cs", [P, 16])
    cst = keep("cst", [P, KT, 4], F32R)
    sel4 = keep("sel4", [4, 2])
    modrow = keep("modrow", [4, 256])
    mod1 = keep("mod1", [P, 16, 2])
    sh1 = keep("sh1", [P, KT, 2])
    sc1 = keep("sc1", [P, KT, 2])
    gbias = keep("gbias", [64, 4])
    m0 = keep("m0", [64, 1])
    rms = keep("rms", [P, 32])
    bqs = keep("bqs", [P, CT])
    lgs = keep("lgs", [P, CT])
    raw = keep("raw", [P, NRAW, CH])
    wh0 = keep("wh0", [P, 3, CH], F32R)
    wl0 = keep("wl0", [P, 3, CH], F32R)

    K = 1024
    spans = []

    def place(name, at, shape, dt=F32):
        with ExitStack() as s:
            if at:
                s.enter_context(nc.sbuf_tensor(f"gap_{name}", [P, int(at)], mybir.dt.uint8))
            t = s.enter_context(nc.sbuf_tensor(name, shape, dt))
        return t

    hh = place("hh", 0, [P, KT, T], F32R)
    hl = place("hl", 20 * K, [P, KT, T], F32R)
    qt = place("qt", 40 * K, [P, H, T])
    kt = place("kt", 50 * K, [P, H, T])
    ktok = place("ktok", 60 * K, [P, H, NT, HD])
    VT0 = 70 * K
    vtok = place("vtok", VT0, [P, H, NT, HD + 1])
    SG0 = 80 * K + 256
    sga = place("sga", SG0, [P, KT, T])
    CV0 = 100 * K + 256
    conv = place("conv", CV0, [P, 5, UW + 2])
    SM0 = 115 * K + 768
    rrow = place("rrow", SM0, [64, T])
    tokg = place("tokg", SM0 + 2560, [P, 3, NT, 8])
    decay = place("decay", SM0 + 3072, [P, 8, NT])
    wt = place("wt", SM0 + 3328, [P, 2, P])
    pt = place("pt", SM0 + 4352, [P, 2, P])
    kw = place("kw", SM0 + 5376, [P, 2, P])
    st = place("st", SM0 + 6400, [P, T])
    cn = place("cn", SM0 + 8960, [P, 2, HD + 1])
    inter = place("inter", SM0 + 8960 + 1056, [P, HD + 1])
    num = place("num", SM0 + 8960 + 1056 + 544, [P, NT, HD + 1])
    dn = place("dn", SM0 + 8960 + 1056 + 544 + 2592, [P, 3, NT])
    cn0 = place("cn0", SM0 + 13248, [P, 2, HD + 1])
    cout = place("cout", SM0 + 13248 + 1056, [P, HD + 1])
    gsum = place("gsum", SM0 + 13248 + 1056 + 544, [64, 2])
    mprev = place("mprev", SM0 + 13248 + 1056 + 576, [64, NT])
    mend = place("mend", SM0 + 13248 + 1056 + 608, [64, 1])
    hf = place("hf", CV0 + 3 * 4 * (UW + 2), [P, NT, HD])
    lnm = place("lnm", SM0, [P, YW])
    lnr = place("lnr", SM0 + 3072, [P, YW])
    lsq = place("lsq", SM0 + 6144, [P, 2, YW])
    hsq = place("hsq", 50 * K, [P, H * NT, HD])
    hrs = place("hrs", SM0 + 12288, [P, 3, H * NT])
    junk = place("junk", SG0, [P, NT, D])
    x5 = place("x5", 40 * K, [P, NT, D])
    vrow = place("vrow", 60 * K, [NV, P])
    drow = place("drow", 61 * K, [CK * CT, P])
    wgr = place("wgr", 62 * K, [P, KT, 16])
    wgh = place("wgh", 63 * K, [P, KT, P], F32R)
    wgl = place("wgl", 67 * K, [P, KT, P], F32R)
    xt = place("xt", SG0, [P, KT, T])
    sgt = place("sgt", 40 * K, [P, 2, T])
    at = place("at", 45 * K, [P, 2, T])
    vt = place("vt", SG0, [P, 2, T])
    gz = place("gz", SG0 + 5 * K, [P, 6, T])
    sgb = place("sgb", 40 * K, [P, KT, T])
    hmt = place("hmt", VT0, [P, H, T])
    ml = place("ml", 40 * K, [P, KT, T], F32R)
    mh = place("mh", SG0, [P, KT, T], F32R)
    mrg = place("mrg", SM0, [P, 2, 2, T])
    x2 = place("x2", 0, [P, NT, D])
    mk = place("mk", 20 * K, [5, 2, D])
    g2n = place("g2n", 28 * K, [P, D])
    tmp = place("tmp", 32 * K, [P, 2, D])
    bg1 = place("bg1", 60 * K, [P, 2, D])
    bsh = place("bsh", 68 * K, [P, 2, D])
    bsc = place("bsc", CV0, [P, 2, D])
    R0 = CV0 + 8 * K
    lg = place("lg", R0, [P, NT, 20])
    wr = place("wr", R0 + 512, [P, KT, 20])
    rb = place("rb", R0 + 1536, [P, 20])
    iota = place("iota", R0 + 2 * K, [P, P])
    upper = place("upper", R0 + 2560, [P, P], BF16)
    wgt = place("wgt", R0 + 3 * K, [P, NT, 2])
    row_i = place("row_i", R0 + 3 * K + 64, [P, NT, 2], I32)
    slot_i = place("slot_i", R0 + 3 * K + 128, [P, NB], I32)
    over_i = place("over_i", R0 + 3 * K + 256, [P, OVER], I32)
    sel5 = place("sel5", R0 + 3 * K + 320, [5, 2, P])
    h2t = place("h2t", 40 * K, [P, 2, KT, P])
    r1 = place("r1", 48 * K, [P, 20, NT * NE])
    oa = place("oa", 56 * K, [P, 2, NT, P], BF16)
    ob = place("ob", 59 * K, [P, 2, NT, 2, NB], BF16)
    obh = place("obh", 62 * K, [P, NT, NB])
    orow = place("orow", 64 * K, [P, OVER, NE])
    picks = place("picks", 65 * K, [P, NT, NE], BF16)
    h2 = place("h2", 20 * K, [P, 2, D])
    scol = place("scol", R0 + 4 * K + 512, [5, 2])
    tokcol = place("tokcol", R0 + 4 * K + 576, [P, 1])
    wh1 = place("wh1", 20 * K, [P, 3, CH], F32R)
    wl1 = place("wl1", 44 * K, [P, 3, CH], F32R)
    xh = place("xh", 68 * K, [P, 2, KT, P], F32R)
    xl = place("xl", 76 * K, [P, 2, KT, P], F32R)
    xg = place("xg", 84 * K, [P, 2, D])
    yy = place("yy", 92 * K, [P, 2, D])
    sil = place("sil", CV0, [P, DE])
    act_ = place("act", CV0 + K, [P, DE])
    ah = place("ah", CV0 + 2 * K, [P, 2, P], F32R)
    al = place("al", CV0 + 3 * K, [P, 2, P], F32R)
    bg2 = place("bg2", R0 + 5 * K, [P, 2, D])
    gfb = place("gfb", R0 + 13 * K, [P, D])
    ya = place("ya", 20 * K, [P, 2, D])
    yb = place("yb", 28 * K, [P, 2, D])
    yo = place("yo", 36 * K, [P, 2, D])
    fsq = place("fsq", 44 * K, [P, D])
    hsqr = place("hsqr", 28 * K, [P, D])
    plane = lambda n, w: r1[:, n, 0:NT * w].rearrange("p (t w) -> p t w", w=w)
    rexp = [plane(0, NG), plane(1, 1)]

    psum = top.enter_context(nc.psum_tensor("psum", [P, 8, 512], F32))
    flat = psum[:, :, :].rearrange("p b n -> p (b n)")

    x_in, vec_in, gw_in, late_in = sem("x_in"), sem("vec_in"), sem("gw_in"), sem("late_in")
    state_in = [sem(f"state_in{i}") for i in range(2)]
    raw_in = [sem(f"raw_in{i}") for i in range(NRAW)]
    consts = sem("consts")
    late_consts = sem("late_consts")
    hi_done = sem("hi_done")
    lo_done = sem("lo_done")
    z_done = sem("z_done")
    z_free = sem("z_free")
    act_step = sem("act_step")
    dve_step = sem("dve_step")
    pe_start, cols_done = sem("pe_start"), sem("cols_done")
    x_ss, x_inv, x_rstd, x_scaled = sem("x_ss"), sem("x_inv"), sem("x_rstd"), sem("x_scaled")
    xt_turned, xt_free = sem("xt_turned"), sem("xt_free")
    cs_done, cst_hi, cst_lo = sem("cs_done"), sem("cst_hi"), sem("cst_lo")
    gate_in, wg_hi, wg_lo = sem("gate_in"), sem("wg_hi"), sem("wg_lo")
    tiny_done = sem("tiny_done")
    mod_st = sem("mod_st")
    h_hi, h_lo = sem("h_hi"), sem("h_lo")
    h_mod = sem("h_mod")
    u_done = sem("u_done")
    turn_done, turn_free = sem("turn_done"), sem("turn_free")
    gsum_done = sem("gsum_done")
    gate_abs, gate_ln, gate_max = sem("gate_abs"), sem("gate_ln"), sem("gate_max")
    gate_rows, gate_pe, gate_tables = sem("gate_rows"), sem("gate_pe"), sem("gate_tables")
    r_done = sem("r_done")
    st_done, st_free = sem("st_done"), sem("st_free")
    w_done = sem("w_done")
    p_done = sem("p_done")
    mm_done = sem("mm_done")
    t_done = sem("t_done")
    num_done = sem("num_done")
    cout_st, m_st = sem("cout_st"), sem("m_st")
    hn_inv, hn_rstd, hn_scaled, hn_pe, hmt_done = (
        sem(n) for n in ("hn_inv", "hn_rstd", "hn_scaled", "hn_pe", "hmt_done"))
    o_done = sem("o_done")
    conv_step, ln_pe, ln_cent, ln_sq, ln_inv, ln_rstd, ln_norm, ln_y = (
        sem(n) for n in ("conv_step", "ln_pe", "ln_cent", "ln_sq", "ln_inv", "ln_rstd", "ln_norm", "ln_y"))
    sga_done = sem("sga_done")
    b_hi, b_lo = sem("b_hi"), sem("b_lo")
    ab_done, ab_free = sem("ab_done"), sem("ab_free")
    m_sum, m_hi, m_lo = sem("m_sum"), sem("m_hi"), sem("m_lo")
    gb_in = [sem(f"gb_in{i}") for i in range(2)]
    gb_pe, gb_free, gb_dve = sem("gb_pe"), sem("gb_free"), sem("gb_dve")
    bsc_done = sem("bsc_done")
    x2_in, x2_done = sem("x2_in"), sem("x2_done")
    wo_done, wo_free = sem("wo_done"), sem("wo_free")
    h2_ss, h2_inv, h2_rstd, h2_dve, h2_pe, h2_ev, lg_done, lg_free = (
        sem(n) for n in ("h2_ss", "h2_inv", "h2_rstd", "h2_dve", "h2_pe", "h2_ev", "lg_done", "lg_free"))
    h2_st = [sem(f"h2_st{i}") for i in range(2)]
    rt_x, rt_exp, rt_pe = sem("rt_x"), sem("rt_exp"), sem("rt_pe")
    picked, hots, tables = sem("picked"), sem("hots"), sem("tables")
    e_hi, e_lo_dve, e_lo_pool, e_used = sem("e_hi"), sem("e_lo_dve"), sem("e_lo_pool"), sem("e_used")
    xg_in = [sem(f"xg_in{i}") for i in range(2)]
    xt_done, x_hi, x_lo = sem("xt_done"), sem("x_hi"), sem("x_lo")
    gu_done, sil_done, act_done, at_done, a_hi, a_lo, dn_done = (
        sem(n) for n in ("gu_done", "sil_done", "act_done", "at_done", "a_hi", "a_lo", "dn_done"))
    y_act, y_dve = sem("y_act"), sem("y_dve")
    y_st = [sem(f"y_st{i}") for i in range(2)]
    yg_in = [sem(f"yg_in{i}") for i in range(2)]
    f_scaled, f_taken, f_sum, f_ss, f_inv, f_rstd, f_out = (
        sem(n) for n in ("f_scaled", "f_taken", "f_sum", "f_ss", "f_inv", "f_rstd", "f_out"))
    f_st = [sem(f"f_st{i}") for i in range(2)]

    VROWS = [(V_CTX, a["c_ctx"]), (V_C, a["c"][0]), (V_G1, a["norm1_g"][0]),
             (V_BSH, a["b_ada"][0, 0:2 * D]), (V_BA, a["b_in"][0, C_A:C_Q]), (V_BQ, a["b_in"][0, C_Q:C_IF]),
             (V_BMA, a["b_in"][0, C_MA:C_MB + D]), (V_BDW, a["b_dw"][0]), (V_LG, a["conv_ln_g"][0]),
             (V_LB, a["conv_ln_b"][0]), (V_HN, a["mlstm_hn_g"][0])]

    def wsrc(kind, i):
        if kind == "ada":
            return a["w_ada"][0, :, i * 256:(i + 1) * 256].rearrange("(k p) n -> p k n", p=P)
        if kind in WCOL:
            c = WCOL[kind] + i * 256
            return a["w_in"][0, :, c:c + 256].rearrange("(k p) n -> p k n", p=P)
        if kind in ("wc", "wm"):
            w = a["w_conv_out" if kind == "wc" else "w_mlstm_out"]
            return w[0, :, i * 512:(i + 1) * 512].rearrange("(k p) n -> p k n", p=P)
        return a["w_o"][0, :, i * 256:(i + 1) * 256].rearrange("(k p) n -> p k n", p=P)

    def chunk(t, slot, rows):
        return t[:, slot, :].rearrange("p (k n) -> p k n", k=rows)

    def lat(plane, width):
        return conv[:, plane, width:width + ROWS * PITCH].rearrange("p (r w) -> p r w", w=PITCH)[:, :, 0:GW]

    def accp(c):
        return 4 if c == 0 else c - 1

    CHAINS = [(h, d) for h in range(H) for d in range(2)]
    hooks = {}
    def raw_owner(g):
        return (g - G0) % 3

    def raw_landed(eng, g):
        eng.wait_ge(raw_in[g % NRAW], 16 * (g // NRAW + 1))

    VEC_IN = 16 * (len(VROWS) + 1)
    GATE_IN = 16 * 8 + 32

    def chunk_used(eng, g):
        kind, i = UNITS[g]
        if TILES_OF[g]:
            eng.wait_ge(z_done, TILES_OF[g][-1][0] + 1)
        elif kind in ("wc", "wm"):
            eng.wait_ge(ab_done, 8 * (i + 1))
        else:
            eng.wait_ge(wo_done, NT * (i + 1))

    def split_matmuls(pe, dst, pairs):
        n = 3 * len(pairs)
        k = 0
        for lh, ll, rh, rl in pairs:
            for left, right in ((lh, rh), (lh, rl), (ll, rh)):
                mm = pe.matmul(dst, left, right, start=(k == 0), stop=(k == n - 1))
                k += 1
        return mm

    def load_mod(eng, j):
        if j >= 2:
            eng.wait_ge(gb_pe, 4 * (j - 1))
        eng.dma_start(mk[0:4, j % 2, :], mod_d[:, j * D:(j + 1) * D]).then_inc(gb_in[j % 2], 16)
        eng.dma_start(mk[4:5, j % 2, :], a["b_ada"][0:1, (j + 2) * D:(j + 3) * D]).then_inc(gb_in[j % 2], 16)

    def h2_out(act, t):
        act.wait_ge(h2_dve, t + 1)
        act.dma_start(h2_d[t * P:(t + 1) * P, :], h2[:, t % 2, :]).then_inc(h2_st[t % 2], 16)
        if t >= 2:
            act.wait_ge(lg_done, t - 1)
        for q in range(2):
            act.wait_ge(h2_pe, 2 * t + q + 1)
            act.activation(h2t[:, t % 2, 4 * q:4 * q + 4, :],
                           psum[:, (2 * t + q) % 4, :].rearrange("p (k n) -> p k n", k=4), ACT.Copy).then_inc(h2_ev, 1)

    def routing(dve, then):
        four = lambda n: r1[:, n, 0:80].rearrange("p (t g e) -> p t g e", t=NT, g=NG)
        full = lambda n: r1[:, n, 0:80].rearrange("p (t e) -> p t e", t=NT)
        col = lambda n: r1[:, n, 0:NT]
        over = lambda ap, w: ap.unsqueeze(2).to_broadcast([P, NT, w])
        desc = r1[:, 19, 0:NG]
        then(dve.tensor_scalar(desc, iota[:, 0:NG], -1.0, float(NG), MUL, ADD))

        def first_max(src, top, hot, t1, t2):
            then(dve.tensor_reduce(top, src, AX, MAX))
            then(dve.tensor_tensor(t1, src, over(top, NG), ALU.is_ge))
            then(dve.tensor_tensor(t1, t1, desc.unsqueeze(1).to_broadcast([P, NT, NG]), MUL))
            then(dve.tensor_reduce(t2, t1, AX, MAX))
            then(dve.tensor_tensor(hot, t1, over(t2, NG), ALU.is_equal))

        gl, el = lg[:, :, 0:NG], lg[:, :, NG:20].rearrange("p t (g e) -> p t g e", g=NG)
        first_max(gl, col(2), plane(3, NG), plane(4, NG), col(5))
        dve.tensor_tensor(rexp[0], gl, over(col(2), NG), SUB).then_inc(rt_x, 1)
        then(dve.tensor_tensor(four(6), el, plane(3, NG).unsqueeze(3).to_broadcast([P, NT, NG, GE]), MUL))
        then(dve.tensor_reduce(plane(7, GE), four(6).rearrange("p t g e -> p t e g"), AX, ADD))
        first_max(plane(7, GE), col(8), plane(9, GE), plane(4, GE), col(5))
        then(dve.scalar_tensor_tensor(out=plane(10, GE), in0=plane(9, GE), scalar=NEG, in1=plane(7, GE), op0=MUL, op1=ADD))
        first_max(plane(10, GE), col(11), plane(12, GE), plane(4, GE), col(5))
        dve.tensor_tensor(r1[:, 1, 0:NT], col(11), col(8), SUB).then_inc(rt_x, 1)
        for n, hot in ((13, 9), (14, 12)):
            then(dve.tensor_tensor(four(n), plane(3, NG).unsqueeze(3).to_broadcast([P, NT, NG, GE]),
                                   plane(hot, GE).unsqueeze(2).to_broadcast([P, NT, NG, GE]), MUL))
        dve.tensor_tensor(picks[:, :, :], full(13), full(14), ADD).then_inc(picked, 1)
        dve.wait_ge(rt_exp, 2)
        then(dve.tensor_reduce(col(5), rexp[0], AX, ADD))
        then(dve.reciprocal(col(5), col(5)))
        then(dve.tensor_scalar(col(4), r1[:, 1, 0:NT], 1.0, None, ADD))
        then(dve.reciprocal(col(4), col(4)))
        then(dve.tensor_tensor(wgt[:, :, 0], col(4), col(5), MUL))
        then(dve.tensor_tensor(wgt[:, :, 1], wgt[:, :, 0], r1[:, 1, 0:NT], MUL))
        dve.wait_ge(rt_pe, 1)
        pos, q, cnt, ov, incl, base, blk, s = full(2), full(6), r1[:, 7, 0:NE], r1[:, 8, 0:NE], r1[:, 9, 0:NE], r1[:, 10, 0:NE], full(11), full(12)
        then(dve.tensor_copy(pos, psum[:, 5, 0:NT * NE].rearrange("p (t e) -> p t e", t=NT)))
        then(dve.tensor_copy(cnt, psum[:, 5, NT * NE:(NT + 1) * NE]))
        then(dve.tensor_scalar(q, pos, float(CAP), None, ALU.is_ge))
        then(dve.tensor_scalar(ov, cnt, float(CAP), None, ALU.is_gt))
        for k in range(2, -(-T // CAP)):
            then(dve.scalar_tensor_tensor(out=q, in0=pos, scalar=float(k * CAP), in1=q, op0=ALU.is_ge, op1=ADD))
            then(dve.scalar_tensor_tensor(out=ov, in0=cnt, scalar=float(k * CAP), in1=ov, op0=ALU.is_gt, op1=ADD))
        then(dve.tensor_tensor_scan(incl, ones[:, 0:NE], ov, 0.0, MUL, ADD))
        then(dve.tensor_tensor(base, incl, ov, SUB))
        then(dve.scalar_tensor_tensor(out=base, in0=base, scalar=float(NE - 1), in1=iota[:, 0:NE], op0=ADD, op1=SUB))
        wide = lambda ap: ap.unsqueeze(1).to_broadcast([P, NT, NE])
        then(dve.tensor_tensor(blk, q, wide(base), ADD))
        then(dve.tensor_scalar(full(15), q, 0.0, None, ALU.is_gt))
        then(dve.tensor_tensor(blk, blk, full(15), MUL))
        then(dve.tensor_tensor(blk, blk, wide(iota[:, 0:NE]), ADD))
        then(dve.scalar_tensor_tensor(out=s, in0=q, scalar=-float(CAP), in1=pos, op0=MUL, op1=ADD))
        for i, hot in enumerate((13, 14)):
            then(dve.tensor_tensor(full(15), full(hot), blk, MUL))
            then(dve.tensor_reduce(col(16), full(15), AX, ADD))
            then(dve.tensor_tensor(full(15), full(hot), s, MUL))
            then(dve.tensor_reduce(col(17), full(15), AX, ADD))
            then(dve.scalar_tensor_tensor(out=col(18), in0=col(16), scalar=float(CAP), in1=col(17), op0=MUL, op1=ADD))
            then(dve.tensor_copy(row_i[:, :, i], col(18)))
            then(dve.tensor_tensor(oa[:, i, :, :], iota[:, :].unsqueeze(1).to_broadcast([P, NT, P]), over(col(17), P),
                                   ALU.is_equal))
            then(dve.tensor_tensor(obh[:, :, :], iota[:, 0:NB].unsqueeze(1).to_broadcast([P, NT, NB]), over(col(16), NB),
                                   ALU.is_equal))
            then(dve.tensor_scalar(ob[:, i, :, 0, :], obh[:, :, :], tokcol[:, :], None, MUL))
            ins = dve.tensor_tensor(ob[:, i, :, 1, :], obh[:, :, :], over(iota[:, 0:NT], NB), MUL)
            if i == 0:
                then(ins)
        ins.then_inc(hots, 1)
        eo = obh[:, :, :].rearrange("p t n -> p (t n)")
        dve.wait_ge(hots, 1)
        big = orow[:, :, :]
        then(dve.tensor_tensor(big, iota[:, 0:OVER].unsqueeze(2).to_broadcast([P, OVER, NE]),
                               incl.unsqueeze(1).to_broadcast([P, OVER, NE]), ALU.is_ge))
        then(dve.tensor_reduce(r1[:, 17, 0:OVER], big, AX, ADD))
        then(dve.tensor_scalar(r1[:, 17, 0:OVER], r1[:, 17, 0:OVER], float(NE - 1), None, MIN))
        then(dve.tensor_copy(over_i[:, :], r1[:, 17, 0:OVER]))
        dve.wait_ge(rt_pe, 2)
        then(dve.tensor_copy(r1[:, 16, 0:2 * NB], psum[:, 6, 0:2 * NB]))
        then(dve.scalar_tensor_tensor(out=r1[:, 17, 0:NB], in0=r1[:, 16, NB:2 * NB], scalar=float(P), in1=r1[:, 16, 0:NB],
                                      op0=MUL, op1=ADD))
        dve.tensor_copy(slot_i[:, :], r1[:, 17, 0:NB]).then_inc(tables, 1)

    def experts_pool(pool):
        pool.wait_ge(h2_st[0], 16 * 3)
        pool.wait_ge(h2_st[1], 16 * 2)
        pool.wait_ge(tables, 1)
        for b in range(NB + 1):
            if b < NB:
                if b >= 2:
                    pool.wait_ge(xt_done, 2 * (b - 1))
                else:
                    pool.wait_ge(wo_done, 4 * NT)
                pool.indirect_dma_start(out=xg[:, b % 2, :], out_offset=None, in_=h2_d,
                                        in_offset=bass.IndirectOffsetOnAxis(ap=slot_i[:, b:b + 1], axis=0),
                                        bounds_check=T - 1).then_inc(xg_in[b % 2], 16)
            if b >= 1:
                pool.wait_ge(e_hi, 3 * b)
                n = b - 1
                pool.tensor_tensor((wl0, wl1)[n % 2][:, 2, :], raw[:, (G0 + 3 * n + 2) % NRAW, :],
                                   (wh0, wh1)[n % 2][:, 2, :].bitcast(F32), SUB).then_inc(e_lo_pool, 1)
        for i in range(2):
            pool.wait_ge(y_st[i], 16 * (-(-(NB - i) // 2)))
        for t in range(NT):
            if t >= 2:
                pool.wait_ge(f_taken, t - 1)
            for i, buf in enumerate((ya, yb)):
                pool.indirect_dma_start(out=buf[:, t % 2, :], out_offset=None, in_=y_d,
                                        in_offset=bass.IndirectOffsetOnAxis(ap=row_i[:, t, i:i + 1], axis=0),
                                        bounds_check=NB * CAP - 1).then_inc(yg_in[t % 2], 16)

    block = top.enter_context(nc.Block())

    @block.sync
    def _(sp):
        for t in range(NT):
            src = a["x_prompt"][0] if t == 0 else a["x_sample"][0, (t - 1) * P:t * P, :]
            sp.dma_start(x5[:, t, :], src).then_inc(x_in, 16)
        for g, (kind, i) in enumerate(UNITS):
            if g >= NRAW:
                sp.wait_ge(lo_done, g - NRAW + 1)
            src = wsrc(kind, i)
            sp.dma_start(chunk(raw, g % NRAW, src.shape[1]), src).then_inc(raw_in[g % NRAW], 16)
        for b in range(NB):
            if b >= NE:
                if b == NE:
                    sp.wait_ge(tables, 1)
                e = sp.value_load(over_i[0:1, b - NE:b - NE + 1], min_val=0, max_val=NE - 1)
                pick = lambda w: w[0, bass.ds(e, 1), :, :].rearrange("a (k p) n -> p (a k) n", p=P)
            else:
                pick = lambda w: w[0, b, :, :].rearrange("(k p) n -> p k n", p=P)
            for c, name in enumerate(("w_e_gate", "w_e_up", "w_e_down")):
                g = G0 + 3 * b + c
                if b == 0:
                    sp.wait_ge(lo_done, g - NRAW + 1)
                elif raw_owner(g) == 2:
                    sp.wait_ge(e_lo_pool, b)
                else:
                    sp.wait_ge(e_lo_dve, 2 * (b - 1) + c + 1)
                src = pick(a[name])
                sp.dma_start(chunk(raw, g % NRAW, src.shape[1]), src).then_inc(raw_in[g % NRAW], 16)

    @block.gpsimd
    def _(pool):
        pool.memset(ident[:, :], 0.0).then_inc(consts, 1)
        pool.memset(identb[:, :], 0.0).then_inc(consts, 1)
        pool.memset(ones[:, :], 1.0).then_inc(consts, 1)
        pool.memset(onesb[:, :], 1.0).then_inc(consts, 1)
        pool.memset(mask[:, :, :], 0.0).then_inc(consts, 1)
        pool.memset(conv[:, :, :], 0.0).then_inc(consts, 1)
        pool.memset(wgh[:, :, :].bitcast(F32), 0.0).then_inc(consts, 1)
        pool.memset(wgl[:, :, :].bitcast(F32), 0.0).then_inc(consts, 1)
        pool.memset(gbias[:, :], 0.0).then_inc(consts, 1)
        pool.memset(m0[:, :], 0.0).then_inc(consts, 1)
        pool.wait_ge(consts, 10)
        for t in (ident, identb):
            pool.affine_select(out=t[:, :], in_=t[:, :], compare_op=ALU.not_equal, fill=1.0, base=0,
                               pattern=[[-1, P]], channel_multiplier=1).then_inc(consts, 1)
        pool.affine_select(out=mask[:, 0, :], in_=mask[:, 0, :], compare_op=ALU.is_ge, fill=NEG, base=0,
                           pattern=[[1, P]], channel_multiplier=-1).then_inc(consts, 1)
        pool.affine_select(out=mask[:, 1, :], in_=mask[:, 1, :], compare_op=ALU.is_ge, fill=NEG, base=0,
                           pattern=[[-1, P]], channel_multiplier=1).then_inc(consts, 1)
        for g in range(G0):
            if g == UNIT_AT["v", 0] - 1:
                pool.wait_ge(h_lo, KT)
                pool.memset(gz[0:64, 5, :], 1.0).then_inc(consts, 1)
                pool.wait_ge(consts, 15)
                pool.memset(gz[0:32, 5, 0:T:P], 0.0).then_inc(consts, 1)
                pool.memset(gz[32:64, 5, P - 1:T:P], 0.0).then_inc(consts, 1)
                pool.wait_ge(consts, 17)
            pool.wait_ge(hi_done, g + 1)
            pool.tensor_tensor(wl0[:, g % 3, :], raw[:, g % NRAW, :], wh0[:, g % 3, :].bitcast(F32),
                               SUB).then_inc(lo_done, 1)
        experts_pool(pool)

    @block.tensor
    def _(pe):
        def turn(dst, src, n=P):
            return pe.transpose(dst, src, ident[0:n, 0:n])

        pe.wait_ge(consts, 14)
        pe.wait_ge(vec_in, VEC_IN)
        turn(psum[:, 4, 0:NV], vrow[:, :], NV)
        turn(psum[:, 4, 128:128 + CK * CT], drow[:, :], CK * CT).then_inc(pe_start, 1)
        for t in range(NT):
            pe.wait_ge(x_scaled, t + 1)
            for q in range(2):
                n = 2 * t + q
                if n >= 4:
                    pe.wait_ge(xt_free, n - 3)
                for k in range(4):
                    mm = turn(psum[:, n % 4, k * P:(k + 1) * P], x5[:, t, (4 * q + k) * P:(4 * q + k + 1) * P])
                mm.then_inc(xt_turned, 1)
        pe.wait_ge(xt_free, 2 * NT)
        pe.wait_ge(cst_lo, 1)

        def tiny(n):
            pe.wait_ge(z_free, TILE_AT["ada", n] + 1)
            for j in range(2):
                mm = pe.matmul(psum[:, 6, 4 * n + 2 * j:4 * n + 2 * j + 2], modrow[:, j * P:(j + 1) * P], sel4[:, :],
                               start=True, stop=True)
            mm.then_inc(tiny_done, 1)

        def open_tile(tile):
            if tile >= 2:
                pe.wait_ge(z_free, tile - 1)
            return 2 * (tile % 2)

        def gemm(tile, wh, wl, hook=None):
            p = open_tile(tile)
            for k in range(KT):
                pe.wait_ge(h_lo, k + 1)
                for x, (w, r) in enumerate(((wh(k), hh), (wh(k), hl), (wl(k), hh))):
                    for q in range(2):
                        mm = pe.matmul(psum[:, p + q, 0:HALF], w, r[:, k, q * HALF:(q + 1) * HALF],
                                       start=(k == 0 and x == 0), stop=(k == KT - 1 and x == 2))
                if hook:
                    hook(k)
            mm.then_inc(z_done, 1)

        def turn_tokens(kind, h):
            pe.wait_ge(z_free, TILE_AT[kind, h] + 1)
            n = h if kind == "v" else H + h
            if n:
                pe.wait_ge(turn_free, n)
            src = vt[:, h % 2, :] if kind == "v" else kt[:, h, :]
            for t in range(NT):
                mm = turn(flat[:, 4 * 512 + t * P:4 * 512 + (t + 1) * P], src[:, t * P:(t + 1) * P])
            mm.then_inc(turn_done, 1)

        def gates_turn():
            pe.wait_ge(gate_rows, 1)
            pe.wait_ge(turn_free, 2 * H)
            for t in range(NT):
                turn(flat[:, 4 * 512 + t * P:4 * 512 + (t + 1) * P], gz[:, 4, t * P:(t + 1) * P])
            for t in range(NT):
                turn(psum[:, 6, t * 64:(t + 1) * 64], gz[0:64, 3, t * P:(t + 1) * P], 64)
            for ci, (h, d) in enumerate(CHAINS):
                col = 64 + 32 * d + h
                mm = pe.matmul(psum[:, 7, ci * NT:(ci + 1) * NT], ident[64:128, col:col + 1].to_broadcast([64, P]),
                               gz[64:128, 4, (0 if d else P - 1):T:P], start=True, stop=True)
            mm.then_inc(gate_pe, 1)

        def exponents(ci):
            h, d = CHAINS[ci]
            if ci:
                pe.wait_ge(w_done, NT * ci)
            row = ident[0:64, 32 * d + h:32 * d + h + 1].to_broadcast([64, P])
            pe.matmul(psum[:, 4, :], row, rrow[:, P:T], start=True, stop=False)
            pe.matmul(psum[:, 4, :], identb[:, :], mask[:, d:d + 1, :].to_broadcast([P, 4, P]), start=False, stop=True)
            pe.matmul(psum[:, 5, 0:P], row, rrow[:, 0:P], start=True, stop=False)
            pe.matmul(psum[:, 5, 0:P], identb[:, :], mask[:, d, :], start=False, stop=True).then_inc(r_done, 1)

        def scores(ci):
            h, _ = CHAINS[ci]
            if ci:
                pe.wait_ge(num_done, NT * ci)
            for t in range(NT):
                mm = pe.matmul(flat[:, 6 * 512 + t * P:6 * 512 + (t + 1) * P], kt[:, h, t * P:(t + 1) * P],
                               qt[:, h, t * P:(t + 1) * P], start=True, stop=True)
            mm.then_inc(st_done, 1)

        def step(ci, i):
            h, d = CHAINS[ci]
            n = NT * ci + i
            c = chunk_order(d)[i]
            pe.wait_ge(p_done, n + 1)
            if n:
                pe.wait_ge(num_done, n)
            mm = pe.matmul(psum[:, 6, 0:HD + 1], pt[:, n % 2, :], vtok[:, h, c, :], start=True, stop=True)
            if i < NT - 1:
                mm = pe.matmul(psum[:, 6, 256:256 + HD + 1], kw[:, n % 2, :], vtok[:, h, c, :], start=True, stop=True)
            if i:
                if i == 1:
                    pe.wait_ge(state_in[ci % 2], 32 * (ci // 2 + 1))
                state = cn0[:, ci % 2, :] if i == 1 else cn[:, i % 2, :]
                mm = pe.matmul(psum[:, 7, 0:HD + 1], qt[:, h, c * P:(c + 1) * P], state, start=True, stop=True)
            mm.then_inc(mm_done, 1)

        def chain_hook(ci):
            def run(k):
                if k == 0:
                    exponents(ci)
                    if CHAINS[ci][1] == 0:
                        scores(ci)
                elif k >= 3:
                    step(ci, k - 3)
            return run

        def heads_turn():
            pe.wait_ge(hn_scaled, 1)
            pe.wait_ge(num_done, NT * len(CHAINS))
            for h in range(H):
                if h:
                    pe.wait_ge(hmt_done, h)
                for t in range(NT):
                    mm = turn(flat[:, 6 * 512 + t * P:6 * 512 + (t + 1) * P], ktok[:, h, t, :])
                mm.then_inc(hn_pe, 1)

        def channel_sums(n):
            for c in range(CT):
                if n == 0:
                    pe.wait_ge(conv_step, CK * CT)
                    src = conv[:, accp(c), 0:YW]
                else:
                    pe.wait_ge(ln_sq, c + 1)
                    src = lsq[:, c % 2, :]
                for q in range(2):
                    mm = pe.matmul(psum[:, 4 + q, 0:YW // 2], ones[:, :], src[:, q * (YW // 2):(q + 1) * (YW // 2)],
                                   start=(c == 0), stop=(c == CT - 1))
                if n == 1:
                    mm.then_inc(ln_pe, 1)
            if n == 0:
                mm.then_inc(ln_pe, 1)

        for g, (kind, i) in enumerate(UNITS):
            if kind in ("wc", "wm", "wo"):
                continue
            pe.wait_ge(lo_done, g + 1)
            hi, lo = wh0[:, g % 3, :], wl0[:, g % 3, :]
            if kind == "v" and i == 0:
                pe.wait_ge(wg_lo, 4)
                gemm(TILE_AT["gate", 0], lambda k: wgh[:, k, :], lambda k: wgl[:, k, :])
            if kind == "ada":
                tile = TILE_AT[kind, i]
                p = open_tile(tile)
                for k in range(KT):
                    for j, w in enumerate((hi, lo)):
                        mm = pe.matmul(psum[0:4, p, 0:256], cst[:, k, :], w[:, k * 256:(k + 1) * 256],
                                       start=(k == 0 and j == 0), stop=(k == KT - 1 and j == 1))
                mm.then_inc(z_done, 1)
                if 1 <= i < 8:
                    tiny(i - 1)
                if i == 7:
                    tiny(7)
            else:
                for j in range(2):
                    n = 2 * i + j
                    hook = chain_hook(n) if kind == "gma" else None
                    if kind == "gma" and n == 0:
                        gates_turn()
                        pe.wait_ge(gate_tables, 1)
                    w = lambda t: (lambda k: t[:, k * 256 + j * P:k * 256 + (j + 1) * P])
                    gemm(TILE_AT[kind, n], w(hi), w(lo), hook)
                    if kind in ("v", "k") and n:
                        turn_tokens(kind, n - 1)
                    if (kind, n) == ("k", 0):
                        turn_tokens("v", H - 1)
                    if (kind, n) == ("q", 0):
                        turn_tokens("k", H - 1)
                    if (kind, n) == ("o", 1):
                        heads_turn()
                    if (kind, n) == ("o", 3):
                        channel_sums(0)
                    if (kind, n) == ("gmb", 1):
                        channel_sums(1)

        for half in range(2):
            g = UNIT_AT["wc", half]
            pe.wait_ge(lo_done, g + 2)
            pe.wait_ge(b_lo, 8)
            for m in range(4):
                for br in range(2):
                    n = 8 * half + 2 * m + br
                    if n >= 2:
                        pe.wait_ge(ab_free, n - 1)
                    else:
                        pe.wait_ge(z_free, len(TILES))
                    p = 2 * (n % 2)
                    slot = (g + br) % 3
                    for k in range(4):
                        cols = slice(k * 512 + m * P, k * 512 + (m + 1) * P)
                        hi, lo = wh0[:, slot, cols], wl0[:, slot, cols]
                        for x, (w, r) in enumerate(((hi, hh), (hi, hl), (lo, hh))):
                            for q in range(2):
                                mm = pe.matmul(psum[:, p + q, 0:HALF], w, r[:, 4 * br + k, q * HALF:(q + 1) * HALF],
                                               start=(k == 0 and x == 0), stop=(k == 3 and x == 2))
                    mm.then_inc(ab_done, 1)

        def broadcast(j):
            pe.wait_ge(gb_in[j % 2], 32 * (j // 2 + 1))
            pe.wait_ge(gb_dve, 1)
            if j:
                pe.wait_ge(gb_free, 4 * j)
            for v in range(2):
                for q in range(2):
                    pe.matmul(psum[:, 4 + 2 * v + q, :], sel5[:, v, :], mk[:, j % 2, q * 512:(q + 1) * 512],
                              start=True, stop=True).then_inc(gb_pe, 1)

        for j in range(4):
            broadcast(j)
        for i in range(4):
            g = UNIT_AT["wo", i]
            pe.wait_ge(lo_done, g + 1)
            for t in range(NT):
                n = NT * i + t
                if n >= 4:
                    pe.wait_ge(wo_free, n - 3)
                elif n < 2:
                    pe.wait_ge(ab_free, 16)
                for k in range(KT):
                    if i == 0 and t == 0:
                        pe.wait_ge(m_lo, k + 1)
                    l_hi, l_lo = mh[:, k, t * P:(t + 1) * P], ml[:, k, t * P:(t + 1) * P]
                    w_hi, w_lo = (w[:, g % 3, k * 256:(k + 1) * 256] for w in (wh0, wl0))
                    for x, (l, r) in enumerate(((l_hi, w_hi), (l_hi, w_lo), (l_lo, w_hi))):
                        mm = pe.matmul(psum[:, n % 4, 0:256], l, r, start=(k == 0 and x == 0),
                                       stop=(k == KT - 1 and x == 2))
                mm.then_inc(wo_done, 1)
        for t in range(NT):
            pe.wait_ge(h2_dve, t + 1)
            for q in range(2):
                n = 2 * t + q
                if n >= 4:
                    pe.wait_ge(h2_ev, n - 3)
                elif n == 0:
                    pe.wait_ge(wo_free, 4 * NT)
                for k in range(4):
                    mm = turn(psum[:, n % 4, k * P:(k + 1) * P], h2[:, t % 2, (4 * q + k) * P:(4 * q + k + 1) * P])
                mm.then_inc(h2_pe, 1)
            pe.wait_ge(h2_ev, 2 * t + 2)
            if t == 0:
                pe.wait_ge(gb_free, 16)
            else:
                pe.wait_ge(lg_free, t)
            for k in range(KT):
                mm = pe.matmul(psum[:, 4, 0:20], h2t[:, t % 2, k, :], wr[:, k, :], start=(k == 0), stop=(k == KT - 1))
            mm.then_inc(lg_done, 1)
        pe.wait_ge(picked, 1)
        for t in range(NT):
            for s in range(t):
                pe.matmul(psum[:, 5, t * NE:(t + 1) * NE], onesb[:, :], picks[:, s, :], start=(s == 0), stop=False)
            pe.matmul(psum[:, 5, t * NE:(t + 1) * NE], upper[:, :], picks[:, t, :], start=(t == 0), stop=True)
        for t in range(NT):
            mm = pe.matmul(psum[:, 5, NT * NE:(NT + 1) * NE], onesb[:, :], picks[:, t, :], start=(t == 0),
                           stop=(t == NT - 1))
        mm.then_inc(rt_pe, 1)
        pe.wait_ge(hots, 1)
        for n in range(2 * NT):
            mm = pe.matmul(psum[:, 6, 0:2 * NB], oa[:, n // NT, n % NT, :], ob[:, n // NT, n % NT, :, :],
                           start=(n == 0), stop=(n == 2 * NT - 1))
        mm.then_inc(rt_pe, 1)

        def turn_rows(b, q):
            if q == 0:
                pe.wait_ge(xg_in[b % 2], 16 * (b // 2 + 1))
            if b:
                pe.wait_ge(x_lo, 2 * (b - 1) + q + 1)
            for k in range(4):
                mm = turn(psum[:, 2 + q, k * P:(k + 1) * P], xg[:, b % 2, (4 * q + k) * P:(4 * q + k + 1) * P])
            mm.then_inc(xt_done, 1)

        pe.wait_ge(h2_ev, 2 * NT)
        pe.wait_ge(gb_free, 16)
        turn_rows(0, 0)
        turn_rows(0, 1)
        for b in range(NB):
            wh, wl = (wh0, wh1)[b % 2], (wl0, wl1)[b % 2]
            pe.wait_ge(e_lo_dve, 2 * (b + 1))
            pe.wait_ge(x_lo, 2 * (b + 1))
            if b >= 2:
                pe.wait_ge(act_done, b - 1)
            both = lambda w, k: w[:, 0:2, k * DE:(k + 1) * DE]
            pairs = [(xh[:, b % 2, k, :], xl[:, b % 2, k, :], both(wh, k), both(wl, k)) for k in range(KT)]
            split_matmuls(pe, psum[:, b % 2, :], pairs).then_inc(gu_done, 1)
            if b + 1 < NB:
                turn_rows(b + 1, 0)
            pe.wait_ge(act_done, b + 1)
            if b:
                pe.wait_ge(a_lo, b)
            turn(psum[:, 4, 0:P], act_[:, 0:P])
            turn(psum[:, 4, P:2 * P], act_[:, P:2 * P]).then_inc(at_done, 1)
            if b + 1 < NB:
                turn_rows(b + 1, 1)
            pe.wait_ge(a_lo, b + 1)
            pe.wait_ge(e_lo_pool, b + 1)
            if b:
                pe.wait_ge(y_act, b)
                pe.wait_ge(y_dve, b)
            for q in range(2):
                cols = lambda w, j: w[:, 2, j * D + q * 512:j * D + (q + 1) * 512]
                mm = split_matmuls(pe, psum[:, 5 + q, :],
                                   [(ah[:, j, :], al[:, j, :], cols(wh, j), cols(wl, j)) for j in range(2)])
            mm.then_inc(e_used, 1)

    @block.scalar
    def _(act):
        def raw_hi(g):
            raw_landed(act, g)
            if g >= 3:
                chunk_used(act, g - 3)
            act.activation(wh0[:, g % 3, :], raw[:, g % NRAW, :], ACT.Copy).then_inc(hi_done, 1)

        pair = lambda tile, rows=slice(0, P): psum[rows, 2 * (tile % 2):2 * (tile % 2) + 2, 0:HALF]
        halves = lambda ap: ap.rearrange("p (q n) -> p q n", q=2)

        for row, src in VROWS:
            n = src.shape[0] // P
            act.dma_start(vrow[row:row + n, :], src.rearrange("(r p) -> r p", p=P)).then_inc(vec_in, 16)
        act.dma_start(drow[:, :], a["w_dw"][0].rearrange("k (c p) -> (k c) p", p=P)).then_inc(vec_in, 16)
        act.dma_start(wgr[:, :, :], a["w_in"][0, :, C_IF:C_MA].rearrange("(k p) n -> p k n", p=P)).then_inc(gw_in, 16)
        act.wait_ge(consts, 10)
        for d in range(2):
            for f in range(2):
                rows = slice(32 * d, 32 * d + H)
                c = C_IF + 8 * d + 4 * f
                act.dma_start(gbias[rows, 2 * f:2 * f + 1], a["b_in"][0, c:c + H].rearrange("(h o) -> h o", o=1)).then_inc(gate_in, 16)
                act.dma_start(gbias[rows, 2 * f + 1:2 * f + 2], a["b_gates"][0, d, f].rearrange("(h o) -> h o", o=1)).then_inc(gate_in, 16)
            act.dma_start(m0[rows, :], a["state_m"][0, 0, d].rearrange("(h o) -> h o", o=1)).then_inc(gate_in, 16)
        act.wait_ge(x_in, 16 * NT)
        for t in range(NT):
            act.activation(junk[:, t, :], x5[:, t, :], ACT.Square, accum_out=rms[:, t:t + 1]).then_inc(x_ss, 1)
        act.wait_ge(x_inv, 1)
        act.activation(rms[:, 8:8 + NT], rms[:, 8:8 + NT], ACT.Sqrt).then_inc(x_rstd, 1)
        act.wait_ge(cols_done, 1)
        act.activation(cs[:, :], vcol[:, 0:16], ACT.Silu).then_inc(cs_done, 1)
        act.wait_ge(cs_done, 1)
        act.activation(cst[:, :, 0:2], cs[:, :].rearrange("p (v k) -> p k v", v=2), ACT.Copy).then_inc(cst_hi, 1)
        raw_hi(0)
        raw_hi(1)
        for n in range(2 * NT):
            t, q = n // 2, n % 2
            act.wait_ge(xt_turned, n + 1)
            act.activation(xt[:, 4 * q:4 * q + 4, t * P:(t + 1) * P], psum[:, n % 4, :].rearrange("p (k n) -> p k n", k=4),
                           ACT.Copy).then_inc(xt_free, 1)
        act.wait_ge(gw_in, 16)
        for d in range(2):
            for f in range(2):
                act.activation(wgh[:, :, 64 * f + 32 * d:64 * f + 32 * d + H], wgr[:, :, 8 * d + 4 * f:8 * d + 4 * f + H],
                               ACT.Copy).then_inc(wg_hi, 1)

        def load_state(ci):
            h, d = CHAINS[ci]
            if ci >= 2:
                act.wait_ge(num_done, NT * (ci - 2) + 2)
            act.dma_start(cn0[:, ci % 2, 0:HD], a["state_C"][0, 0, d, h]).then_inc(state_in[ci % 2], 16)
            act.dma_start(cn0[:, ci % 2, HD:HD + 1], a["state_n"][0, 0, d, h].rearrange("(p o) -> p o", o=1)).then_inc(state_in[ci % 2], 16)

        def turned(kind, h):
            n = h if kind == "v" else H + h
            act.wait_ge(turn_done, n + 1)
            src = flat[:, 4 * 512:4 * 512 + T].rearrange("p (t n) -> p t n", t=NT)
            dst = vtok[:, h, :, 0:HD] if kind == "v" else ktok[:, h, :, :]
            act.activation(dst, src, ACT.Copy).then_inc(turn_free, 1)

        def gates():
            act.wait_ge(gate_abs, 1)
            act.activation(gz[0:64, 2, :], gz[0:64, 2, :], ACT.Exp, scale=-1.0).then_inc(act_step, 1)
            act.wait_ge(act_step, 1)
            act.activation(gz[0:64, 2, :], gz[0:64, 2, :], ACT.Ln, bias=1.0).then_inc(gate_ln, 1)

        def gates2():
            act.wait_ge(gate_max, 1)
            for d in range(2):
                act.dma_start(out["new_m"][0, 0, d].rearrange("(h o) -> h o", o=1),
                              mend[32 * d:32 * d + H, :]).then_inc(m_st, 16)
            act.activation(gz[64:128, 4, :], gz[0:64, 1, :], ACT.Exp)
            act.activation(gz[0:64, 3, :], gz[0:64, 3, :], ACT.Exp, scale=-1.0).then_inc(gate_rows, 1)

        def chain(ci):
            h, d = CHAINS[ci]
            order = chunk_order(d)
            col = 4 * d + h

            def weights(i):
                n, c = NT * ci + i, order[i]
                if n >= 2:
                    act.wait_ge(p_done, n - 1)
                src = psum[:, 4, (c - 1) * P:c * P] if c else psum[:, 5, 0:P]
                act.activation(wt[:, n % 2, :], src, ACT.Exp, bias=tokg[:, 0, c, col:col + 1]).then_inc(w_done, 1)

            if ci + 1 < len(CHAINS):
                load_state(ci + 1)
            act.wait_ge(r_done, ci + 1)
            if d == 0:
                act.wait_ge(st_done, h + 1)
                if h:
                    act.wait_ge(p_done, 2 * NT * h)
                act.activation(st[:, :], flat[:, 6 * 512:6 * 512 + T], ACT.Copy).then_inc(st_free, 1)
            weights(0)
            weights(1)
            for i in range(NT):
                n, c = NT * ci + i, order[i]
                if i:
                    act.wait_ge(mm_done, n + 1)
                    act.wait_ge(num_done, n)
                    if i == 1:
                        act.dma_start(out["new_C"][0, 0, d, h], cout[:, 0:HD]).then_inc(cout_st, 16)
                        act.dma_start(out["new_n"][0, 0, d, h].rearrange("(p o) -> p o", o=1),
                                      cout[:, HD:HD + 1]).then_inc(cout_st, 16)
                    act.activation(inter[:, :], psum[:, 7, 0:HD + 1], ACT.Copy,
                                   scale=tokg[:, 1, c, col:col + 1]).then_inc(t_done, 1)
                if i + 2 < NT:
                    weights(i + 2)

        def evacuate(tile, kind, i):
            if kind == "gma":
                if i == 0:
                    load_state(0)
                    act.wait_ge(gate_tables, 1)
                chain(i)
            act.wait_ge(z_done, tile + 1)
            bias = lambda base: vcol[:, base + i:base + i + 1]

            def z(dst, func, base, **more):
                act.activation(halves(dst), pair(tile), func, bias=bias(base), **more).then_inc(z_free, 1)

            if kind == "ada":
                if 1 <= i <= 8:
                    act.wait_ge(tiny_done, i)
                elif i:
                    act.wait_ge(mod_st, 16 * (i - 8))
                act.activation(modrow[:, :], psum[0:4, 2 * (tile % 2), 0:256], ACT.Copy).then_inc(z_free, 1)
                if i >= 8:
                    act.wait_ge(z_free, tile + 1)
                    act.dma_start(mod_d[:, (i - 8) * 256:(i - 7) * 256], modrow[:, :]).then_inc(mod_st, 16)
            elif kind == "ga":
                if i >= 2:
                    act.wait_ge(u_done, i - 1)
                z(sgt[:, i % 2, :], ACT.Sigmoid, V_BGA)
            elif kind == "a":
                z(at[:, i % 2, :], ACT.Identity, V_BA)
            elif kind == "gate":
                act.wait_ge(h_lo, KT)
                act.wait_ge(gsum_done, 1)
                act.activation(halves(gz[0:64, 0, :]), pair(tile, slice(0, 64)), ACT.Identity, bias=gsum[:, 0:1])
                act.activation(halves(gz[0:64, 1, :]), pair(tile, slice(64, P)), ACT.Identity,
                               bias=gsum[:, 1:2]).then_inc(z_free, 1)
                act.activation(vtok[:, :, :, HD], ones[:, 0:H * NT].rearrange("p (h t) -> p h t", h=H), ACT.Copy)
            elif kind == "v":
                if i >= 2:
                    act.wait_ge(turn_done, i - 1)
                z(vt[:, i % 2, :], ACT.Identity, V_BV)
                if i:
                    turned("v", i - 1)
            elif kind == "k":
                z(kt[:, i, :], ACT.Identity, V_BK)
                turned("k", i - 1) if i else turned("v", H - 1)
                if i == 0:
                    gates()
            elif kind == "q":
                act.wait_ge(u_done, CT)
                act.activation(halves(qt[:, i, :]), pair(tile), ACT.Identity, bias=bqs[:, i:i + 1],
                               scale=QS).then_inc(z_free, 1)
                if i == 0:
                    turned("k", H - 1)
                    gates2()
            elif kind == "gma":
                z(sga[:, i, :], ACT.Identity, V_BMA)
            elif kind == "o":
                if i >= 2:
                    act.wait_ge(o_done, i - 1)
                z(sgt[:, i % 2, :], ACT.Sigmoid, V_BO)
                if i == 1:
                    act.wait_ge(hn_inv, 1)
                    act.activation(hrs[:, 1, :], hrs[:, 1, :], ACT.Sqrt).then_inc(hn_rstd, 1)
                    for h in range(H):
                        act.wait_ge(hn_pe, h + 1)
                        act.activation(hmt[:, h, :], flat[:, 6 * 512:6 * 512 + T], ACT.Copy,
                                       scale=vcol[:, V_HN + h:V_HN + h + 1]).then_inc(hmt_done, 1)
                if i == 3:
                    act.activation(sga[:, :, :], sga[:, :, :], ACT.Sigmoid).then_inc(sga_done, 1)
            elif kind == "gmb":
                act.wait_ge(o_done, H)
                z(sgb[:, i, :], ACT.Sigmoid, V_BMB)
                if i == 0:
                    act.wait_ge(ln_cent, CT)
                    for c in range(CT):
                        if c >= 2:
                            act.wait_ge(ln_pe, c)
                        act.activation(lsq[:, c % 2, :], conv[:, accp(c), 0:YW], ACT.Square).then_inc(ln_sq, 1)
                if i == 3:
                    act.wait_ge(ln_inv, 1)
                    act.activation(lnr[:, :], lnr[:, :], ACT.Sqrt).then_inc(ln_rstd, 1)
                    for c in range(CT):
                        act.wait_ge(ln_norm, c + 1)
                        act.activation(conv[:, accp(c), 0:YW], conv[:, accp(c), 0:YW], ACT.Silu,
                                       bias=vcol[:, V_LB + c:V_LB + c + 1], scale=vcol[:, V_LG + c:V_LG + c + 1]).then_inc(ln_y, 1)

        for g, (kind, i) in enumerate(UNITS):
            if g + 2 < G0 and kind != "wm":
                raw_hi(g + 2)
            for tile, k, n in TILES_OF[g]:
                evacuate(tile, k, n)
            if (kind, i) == ("ada", 7):
                for k in range(KT):
                    act.wait_ge(h_mod, k + 1)
                    act.activation(hh[:, k, :], xt[:, k, :], ACT.Copy).then_inc(h_hi, 1)
            if (kind, i) == ("wc", 0):
                act.wait_ge(ln_y, CT)
                act.wait_ge(o_done, H)
                act.wait_ge(z_done, len(TILES))
                for c in range(CT):
                    act.activation(hh[:, c, 0:TP], conv[:, accp(c), 0:TP], ACT.Copy)
                    act.activation(hh[:, c, TP:T].rearrange("p (r w) -> p r w", w=GW), lat(accp(c), U1 - U0), ACT.Copy).then_inc(b_hi, 1)
                for h in range(H):
                    act.activation(hh[:, CT + h, :], hmt[:, h, :], ACT.Copy).then_inc(b_hi, 1)
            if kind == "wc":
                for m in range(4 * i, 4 * i + 4):
                    act.wait_ge(m_sum, m + 1)
                    act.activation(mh[:, m, :], mrg[:, m % 2, 0, :], ACT.Copy).then_inc(m_hi, 1)
                if i == 1:
                    act.wait_ge(ab_done, 16)
                    act.wait_ge(m_lo, KT)
                    act.wait_ge(mod_st, 16 * 16)
                    for j in range(2):
                        load_mod(act, j)
                    for t in range(NT):
                        src = a["x_prompt"][0] if t == 0 else a["x_sample"][0, (t - 1) * P:t * P, :]
                        act.dma_start(x2[:, t, :], src).then_inc(x2_in, 16)
                    act.dma_start(g2n[:, :], a["norm2_g"][0:1, :].to_broadcast([P, D])).then_inc(late_in, 16)
                    act.dma_start(gfb[:, :], a["norm_final_g"].rearrange("(o n) -> o n", o=1).to_broadcast([P, D])).then_inc(late_in, 16)
                    act.dma_start(wr[:, :, 0:NG], a["w_rg"][0].rearrange("(k p) n -> p k n", p=P)).then_inc(late_in, 16)
                    act.dma_start(wr[:, :, NG:20], a["w_re"][0].rearrange("(k p) n -> p k n", p=P)).then_inc(late_in, 16)
                    act.dma_start(rb[:, 0:NG], a["b_rg"][0:1, :].to_broadcast([P, NG])).then_inc(late_in, 16)
                    act.dma_start(rb[:, NG:20], a["b_re"][0:1, :].to_broadcast([P, NE])).then_inc(late_in, 16)
                raw_hi(g + 3)
            if (kind, i) == ("wm", 1):
                for j, dst in enumerate((bg1, bsh, bsc, bg2)):
                    for n in range(4):
                        act.wait_ge(gb_pe, 4 * j + n + 1)
                        act.activation(dst[:, n // 2, (n % 2) * 512:(n % 2 + 1) * 512], psum[:, 4 + n, :], ACT.Copy,
                                       bias=1.0 if j == 2 else 0.0).then_inc(gb_free, 1)
                    if j < 2:
                        load_mod(act, j + 2)
        for t in range(NT):
            act.wait_ge(x2_done, t + 1)
            act.activation(hsqr[:, :], x2[:, t, :], ACT.Square, accum_out=rms[:, 16 + t:17 + t]).then_inc(h2_ss, 1)
            act.wait_ge(h2_inv, t + 1)
            act.activation(rms[:, 24 + t:25 + t], rms[:, 24 + t:25 + t], ACT.Sqrt).then_inc(h2_rstd, 1)
            if t:
                h2_out(act, t - 1)
        h2_out(act, NT - 1)
        for n in range(2):
            act.wait_ge(rt_x, n + 1)
            src = rexp[n]
            act.activation(src, src, ACT.Exp).then_inc(rt_exp, 1)

        def w_hi(b, c):
            g = G0 + 3 * b + c
            raw_landed(act, g)
            if b >= 2:
                act.wait_ge(e_used, b - 1)
            elif b == 1:
                act.wait_ge(tables, 1)
            else:
                act.wait_ge(wo_done, 4 * NT)
            act.activation((wh0, wh1)[b % 2][:, c, :], raw[:, g % NRAW, :], ACT.Copy).then_inc(e_hi, 1)

        def x_high(b, q):
            act.wait_ge(xt_done, 2 * b + q + 1)
            if b >= 2:
                act.wait_ge(gu_done, b - 1)
            act.activation(xh[:, b % 2, 4 * q:4 * q + 4, :], psum[:, 2 + q, :].rearrange("p (k n) -> p k n", k=4),
                           ACT.Copy).then_inc(x_hi, 1)

        def store_y(b):
            act.wait_ge(y_act, b + 1)
            act.wait_ge(y_dve, b + 1)
            act.dma_start(y_d[b * CAP:(b + 1) * CAP, :], yy[:, b % 2, :]).then_inc(y_st[b % 2], 16)

        for c in range(3):
            w_hi(0, c)
        x_high(0, 0)
        x_high(0, 1)
        for b in range(NB):
            if b + 1 < NB:
                w_hi(b + 1, 0)
                w_hi(b + 1, 1)
            act.wait_ge(gu_done, b + 1)
            if b:
                act.wait_ge(act_done, b)
            act.activation(sil[:, :], psum[:, b % 2, 0:DE], ACT.Silu).then_inc(sil_done, 1)
            if b:
                store_y(b - 1)
            if b + 1 < NB:
                x_high(b + 1, 0)
            act.wait_ge(at_done, b + 1)
            if b:
                act.wait_ge(e_used, b)
            act.activation(ah[:, :, :], psum[:, 4, 0:DE].rearrange("p (j n) -> p j n", j=2), ACT.Copy).then_inc(a_hi, 1)
            if b + 1 < NB:
                x_high(b + 1, 1)
                w_hi(b + 1, 2)
            act.wait_ge(e_used, b + 1)
            if b >= 2:
                act.wait_ge(y_st[b % 2], 16 * (b // 2))
            act.activation(yy[:, b % 2, 0:512], psum[:, 5, :], ACT.Copy).then_inc(y_act, 1)
        store_y(NB - 1)
        for t in range(NT):
            act.wait_ge(yg_in[t % 2], 32 * (t // 2 + 1))
            act.activation(ya[:, t % 2, :], ya[:, t % 2, :], ACT.Copy, scale=wgt[:, t, 0:1]).then_inc(f_scaled, 1)
            act.wait_ge(f_sum, t + 1)
            act.activation(fsq[:, :], yo[:, t % 2, :], ACT.Square, accum_out=rms[:, t:t + 1]).then_inc(f_ss, 1)
            act.wait_ge(f_inv, t + 1)
            act.activation(rms[:, 8 + t:9 + t], rms[:, 8 + t:9 + t], ACT.Sqrt).then_inc(f_rstd, 1)
            act.wait_ge(f_out, t + 1)
            dst = out["y_prompt"][0] if t == 0 else out["y_sample"][0, (t - 1) * P:t * P, :]
            act.dma_start(dst, yo[:, t % 2, :]).then_inc(f_st[t % 2], 16)
        act.wait_ge(f_st[0], 16 * 3)
        act.wait_ge(f_st[1], 16 * 2)
        act.wait_ge(cout_st, 32 * len(CHAINS))
        act.wait_ge(m_st, 32)

    @block.vector
    def _(dve):
        steps = [0]

        def then(ins):
            steps[0] += 1
            ins.then_inc(dve_step, 1)
            dve.wait_ge(dve_step, steps[0])

        dve.wait_ge(consts, 14)
        then(dve.tensor_tensor(sel4[:, :], ident[0:4, 0:2], ident[0:4, 2:4], ADD))
        dve.wait_ge(pe_start, 1)
        dve.tensor_copy(vcol[:, :], psum[:, 4, 0:NV])
        dve.tensor_copy(taps[:, :], psum[:, 4, 128:128 + CK * CT]).then_inc(cols_done, 1)
        dve.wait_ge(cols_done, 1)
        dve.tensor_scalar(bqs[:, :], vcol[:, V_BQ:V_BQ + CT], QS, None, MUL)
        dve.wait_ge(gate_in, GATE_IN)
        dve.tensor_tensor(gsum[:, :], gbias[:, 0:4:2], gbias[:, 1:4:2], ADD).then_inc(gsum_done, 1)
        dve.wait_ge(x_ss, NT)
        then(dve.tensor_scalar(rms[:, 8:8 + NT], rms[:, 0:NT], 1.0 / D, EPS, MUL, ADD))
        dve.reciprocal(rms[:, 8:8 + NT], rms[:, 8:8 + NT]).then_inc(x_inv, 1)
        dve.wait_ge(x_rstd, 1)
        for t in range(NT):
            dve.tensor_scalar(x5[:, t, :], x5[:, t, :], rms[:, 8 + t:9 + t], None, MUL).then_inc(x_scaled, 1)
        dve.wait_ge(cst_hi, 1)
        dve.tensor_tensor(cst[:, :, 2:4], cs[:, :].rearrange("p (v k) -> p k v", v=2), cst[:, :, 0:2].bitcast(F32),
                          SUB).then_inc(cst_lo, 1)
        dve.wait_ge(wg_hi, 4)
        for d in range(2):
            for f in range(2):
                dst = slice(64 * f + 32 * d, 64 * f + 32 * d + H)
                dve.tensor_tensor(wgl[:, :, dst], wgr[:, :, 8 * d + 4 * f:8 * d + 4 * f + H],
                                  wgh[:, :, dst].bitcast(F32), SUB).then_inc(wg_lo, 1)
        dve.wait_ge(tiny_done, 8)
        then(dve.tensor_copy(mod1[:, :, :], psum[:, 6, 0:32].rearrange("p (k v) -> p k v", v=2)))
        for v in range(2):
            then(dve.tensor_tensor(sh1[:, :, v], mod1[:, 0:KT, v], vcol[:, V_BSH:V_BSH + KT], ADD))
            then(dve.tensor_tensor(sc1[:, :, v], mod1[:, KT:2 * KT, v], vcol[:, V_BSC:V_BSC + KT], ADD))
            then(dve.scalar_tensor_tensor(out=sc1[:, :, v], in0=sc1[:, :, v], scalar=1.0, in1=vcol[:, V_G1:V_G1 + KT],
                                          op0=ADD, op1=MUL))
        dve.wait_ge(xt_free, 2 * NT)
        for k in range(KT):
            for v, cols in ((0, slice(0, TP)), (1, slice(TP, T))):
                ins = dve.tensor_scalar(xt[:, k, cols], xt[:, k, cols], sc1[:, k, v:v + 1], sh1[:, k, v:v + 1], MUL, ADD)
            ins.then_inc(h_mod, 1)
            dve.wait_ge(h_hi, k + 1)
            dve.tensor_tensor(hl[:, k, :], xt[:, k, :], hh[:, k, :].bitcast(F32), SUB).then_inc(h_lo, 1)

        def conv_input(c):
            dve.wait_ge(z_free, TILE_AT["a", c] + 1)
            dve.tensor_tensor(conv[:, c, U0:U0 + TP], at[:, c % 2, 0:TP], sgt[:, c % 2, 0:TP], MUL)
            dve.tensor_tensor(lat(c, U1), at[:, c % 2, TP:T].rearrange("p (r w) -> p r w", w=GW),
                              sgt[:, c % 2, TP:T].rearrange("p (r w) -> p r w", w=GW), MUL).then_inc(u_done, 1)

        taken = [0]

        def conv_taps(tiles, first, last):
            for c in tiles:
                for k in range(first, last):
                    acc, src = conv[:, accp(c), 0:YW], conv[:, c, k:k + YW]
                    w = taps[:, k * CT + c:k * CT + c + 1]
                    if taken[0]:
                        dve.wait_ge(conv_step, taken[0])
                    if k == 0:
                        ins = dve.tensor_scalar(acc, src, w, vcol[:, V_BDW + c:V_BDW + c + 1], MUL, ADD)
                    else:
                        ins = dve.scalar_tensor_tensor(out=acc, in0=src, scalar=w, in1=acc, op0=MUL, op1=ADD)
                    taken[0] += 1
                    ins.then_inc(conv_step, 1)

        for c in range(2):
            conv_input(c)
        dve.wait_ge(u_done, 2)
        conv_taps((0,), 0, 16)
        conv_input(2)
        conv_input(3)
        conv_taps((0,), 16, CK)
        conv_taps((1,), 0, CK)
        dve.wait_ge(z_free, TILE_AT["gate", 0] + 1)
        dve.scalar_tensor_tensor(out=gz[0:64, 2, :], in0=gz[0:64, 1, :], scalar=-1.0, in1=gz[0:64, 1, :], op0=MUL,
                                 op1=MAX).then_inc(gate_abs, 1)
        dve.wait_ge(u_done, CT)
        conv_taps((2,), 0, CK)
        dve.wait_ge(gate_ln, 1)
        dve.wait_ge(consts, 17)
        then(dve.scalar_tensor_tensor(out=gz[0:64, 1, :], in0=gz[0:64, 1, :], scalar=0.0, in1=gz[0:64, 2, :], op0=MIN,
                                      op1=SUB))
        fwd = lambda n, a0, a1: gz[0:32, n, a0:a1]
        bwd = lambda n, a0, a1: gz[32:64, n, a1 - 1:(a0 - 1 if a0 else None):-1]
        for dirn in (fwd, bwd):
            dve.tensor_tensor_scan(dirn(2, 0, T), dirn(5, 0, T), dirn(1, 0, T), 0.0, MUL, ADD)
            dve.tensor_tensor_scan(dirn(3, 0, TP), dirn(1, 0, TP), dirn(0, 0, TP), 0.0, ADD, MAX)
            start = m0[0:32, :] if dirn is fwd else m0[32:64, :]
            ins = dve.tensor_tensor_scan(dirn(3, TP, T), dirn(1, TP, T), dirn(0, TP, T), start, ADD, MAX)
        then(ins)
        dve.tensor_tensor(gz[0:64, 4, :], gz[0:64, 0, :], gz[0:64, 2, :], SUB)
        dve.memset(mprev[:, :], 0.0)
        then(dve.tensor_tensor(rrow[:, :], gz[0:64, 2, :], gz[0:64, 3, :], SUB))
        dve.tensor_copy(mprev[0:32, 1:2], m0[0:32, :])
        dve.tensor_copy(mprev[32:64, NT - 1:NT], m0[32:64, :])
        dve.tensor_copy(mprev[0:32, 2:NT], gz[0:32, 3, 2 * P - 1:T - P:P])
        dve.tensor_copy(mprev[32:64, 1:NT - 1], gz[32:64, 3, 2 * P:T:P])
        dve.tensor_copy(mend[0:32, :], gz[0:32, 3, P - 1:P])
        then(dve.tensor_copy(mend[32:64, :], gz[32:64, 3, 0:1]))
        dve.tensor_tensor(gz[0:64, 1, :].rearrange("p (t n) -> p t n", t=NT), rrow[:, :].rearrange("p (t n) -> p t n", t=NT),
                          mprev[:, :].unsqueeze(2).to_broadcast([64, NT, P]), ADD).then_inc(gate_max, 1)
        conv_taps((3,), 0, CK)
        dve.wait_ge(conv_step, taken[0])
        dve.wait_ge(gate_pe, 1)
        turned = flat[:, 4 * 512:4 * 512 + T].rearrange("p (t n) -> p t n", t=NT)
        em = psum[:, 6, 0:NT * 64].rearrange("p (t n) -> p t n", t=NT)
        for d in range(2):
            cols = slice(4 * d, 4 * d + H)
            dve.tensor_copy(tokg[:, 0, :, cols], turned[:, :, 32 * d:32 * d + H])
            dve.tensor_copy(tokg[:, 1, :, cols], turned[:, :, 64 + 32 * d:64 + 32 * d + H])
            dve.tensor_copy(tokg[:, 2, :, cols], em[:, :, 32 * d:32 * d + H])
        dve.tensor_copy(decay[:, :, :], psum[:, 7, 0:8 * NT].rearrange("p (c t) -> p c t", t=NT)).then_inc(gate_tables, 1)
        dve.wait_ge(gate_tables, 1)

        NSTEP = NT * len(CHAINS)
        where = [(ci, i, chunk_order(CHAINS[ci][1])[i]) for ci in range(len(CHAINS)) for i in range(NT)]

        def weigh(n):
            ci, i, c = where[n]
            h, d = CHAINS[ci]
            dve.wait_ge(w_done, n + 1)
            dve.wait_ge(st_free, h + 1)
            if n >= 2:
                dve.wait_ge(mm_done, n - 1)
            last = 0 if d else P - 1
            ins = dve.tensor_tensor(pt[:, n % 2, :], st[:, c * P:(c + 1) * P], wt[:, n % 2, :], MUL)
            if i < NT - 1:
                ins = dve.tensor_scalar(kw[:, n % 2, :], ktok[:, h, c, :], wt[:, n % 2, last:last + 1], None, MUL)
            ins.then_inc(p_done, 1)

        for n in range(NSTEP):
            ci, i, c = where[n]
            h, d = CHAINS[ci]
            if i == 0:
                weigh(n)
            if i < NT - 1:
                weigh(n + 1)
            dve.wait_ge(mm_done, n + 1)
            upd = psum[:, 6, 256:256 + HD + 1]
            if i == 0:
                if ci:
                    dve.wait_ge(cout_st, 32 * ci)
                dve.tensor_copy(num[:, c, :], psum[:, 6, 0:HD + 1])
                dve.tensor_copy(cout[:, :], upd).then_inc(num_done, 1)
            else:
                dve.wait_ge(t_done, (NT - 1) * ci + i)
                ins = dve.tensor_tensor(num[:, c, :], psum[:, 6, 0:HD + 1], inter[:, :], ADD)
                if i < NT - 1:
                    before = cn0[:, ci % 2, :] if i == 1 else cn[:, i % 2, :]
                    ins = dve.scalar_tensor_tensor(out=cn[:, (i + 1) % 2, :], in0=before,
                                                   scalar=decay[:, ci, c:c + 1], in1=upd, op0=MUL, op1=ADD)
                ins.then_inc(num_done, 1)
            if i == NT - 1:
                dve.wait_ge(num_done, n + 1)
                den = num[:, :, HD]
                then(dve.scalar_tensor_tensor(out=dn[:, 0, :], in0=den, scalar=-1.0, in1=den, op0=MUL, op1=MAX))
                then(dve.tensor_tensor(dn[:, 1, :], dn[:, 0, :], tokg[:, 2, :, 4 * d + h], MAX))
                then(dve.reciprocal(dn[:, 2, :], dn[:, 1, :]))
                if d == 0:
                    then(dve.tensor_tensor(hf[:, :, :], num[:, :, 0:HD], dn[:, 2, :].unsqueeze(2).to_broadcast([P, NT, HD]), MUL))
                else:
                    for t in range(NT):
                        ins = dve.scalar_tensor_tensor(out=ktok[:, h, t, :], in0=num[:, t, 0:HD], scalar=dn[:, 2, t:t + 1],
                                                       in1=hf[:, t, :], op0=MUL, op1=ADD)
                    then(ins)
        heads = ktok[:, :, :, :].rearrange("p h t n -> p (h t) n")
        dve.wait_ge(mm_done, NSTEP)
        then(dve.tensor_tensor(hsq[:, :, :], heads, heads, MUL))
        then(dve.tensor_reduce(hrs[:, 0, :], hsq[:, :, :], AX, ADD))
        then(dve.tensor_scalar(hrs[:, 0, :], hrs[:, 0, :], 1.0 / HD, EPS, MUL, ADD))
        dve.reciprocal(hrs[:, 1, :], hrs[:, 0, :]).then_inc(hn_inv, 1)
        dve.wait_ge(hn_rstd, 1)
        dve.tensor_tensor(heads, heads, hrs[:, 1, :].unsqueeze(2).to_broadcast([P, H * NT, HD]), MUL).then_inc(hn_scaled, 1)
        for h in range(H):
            dve.wait_ge(hmt_done, H)
            dve.wait_ge(z_free, TILE_AT["o", h] + 1)
            dve.tensor_tensor(hmt[:, h, :], hmt[:, h, :], sgt[:, h % 2, :], MUL).then_inc(o_done, 1)
        dve.wait_ge(ln_pe, 1)
        sums = psum[:, 4:6, 0:YW // 2]
        two = lambda t: t.rearrange("p (q n) -> p q n", q=2)
        then(dve.tensor_scalar(two(lnm[:, :]), sums, 1.0 / DI, None, MUL))
        for c in range(CT):
            dve.tensor_tensor(conv[:, accp(c), 0:YW], conv[:, accp(c), 0:YW], lnm[:, :], SUB).then_inc(ln_cent, 1)
        dve.wait_ge(ln_pe, 1 + CT)
        then(dve.tensor_scalar(two(lnr[:, :]), sums, 1.0 / DI, EPS, MUL, ADD))
        dve.reciprocal(lnr[:, :], lnr[:, :]).then_inc(ln_inv, 1)
        dve.wait_ge(ln_rstd, 1)
        for c in range(CT):
            dve.tensor_tensor(conv[:, accp(c), 0:YW], conv[:, accp(c), 0:YW], lnr[:, :], MUL).then_inc(ln_norm, 1)
        for c in range(CT):
            dve.wait_ge(b_hi, c + 1)
            dve.tensor_tensor(hl[:, c, 0:TP], conv[:, accp(c), 0:TP], hh[:, c, 0:TP].bitcast(F32), SUB)
            dve.tensor_tensor(hl[:, c, TP:T].rearrange("p (r w) -> p r w", w=GW), lat(accp(c), U1 - U0),
                              hh[:, c, TP:T].bitcast(F32).rearrange("p (r w) -> p r w", w=GW), SUB).then_inc(b_lo, 1)
        for h in range(H):
            dve.wait_ge(b_hi, CT + h + 1)
            dve.tensor_tensor(hl[:, CT + h, :], hmt[:, h, :], hh[:, CT + h, :].bitcast(F32), SUB).then_inc(b_lo, 1)
        dve.wait_ge(sga_done, 1)

        def merged_low(m):
            dve.wait_ge(m_hi, m + 1)
            dve.tensor_tensor(ml[:, m, :], mrg[:, m % 2, 0, :], mh[:, m, :].bitcast(F32), SUB).then_inc(m_lo, 1)

        for m in range(KT):
            if m >= 2:
                merged_low(m - 2)
            for br, gate in enumerate((sga, sgb)):
                n = 2 * m + br
                if m >= 2 and br == 0:
                    dve.wait_ge(m_lo, m - 1)
                dve.wait_ge(ab_done, n + 1)
                dve.tensor_tensor(two(mrg[:, m % 2, br, :]), psum[:, 2 * (n % 2):2 * (n % 2) + 2, 0:HALF],
                                  two(gate[:, m, :]), MUL).then_inc(ab_free, 1)
            dve.wait_ge(ab_free, 2 * m + 2)
            dve.tensor_tensor(mrg[:, m % 2, 0, :], mrg[:, m % 2, 0, :], mrg[:, m % 2, 1, :], ADD).then_inc(m_sum, 1)
        merged_low(KT - 2)
        merged_low(KT - 1)
        for v in range(2):
            then(dve.tensor_tensor(scol[:, v:v + 1], ident[0:5, v:v + 1], ident[0:5, v + 2:v + 3], ADD))
            then(dve.tensor_tensor(scol[:, v:v + 1], scol[:, v:v + 1], ident[0:5, 4:5], ADD))
            ins = dve.tensor_scalar(sel5[:, v, :], ones[0:5, :], scol[:, v:v + 1], None, MUL)
        ins.then_inc(gb_dve, 1)
        dve.wait_ge(gb_free, 12)
        dve.wait_ge(late_in, 16 * 6)
        for v in range(2):
            ins = dve.tensor_tensor(bsc[:, v, :], bsc[:, v, :], g2n[:, :], MUL)
        then(ins)
        then(dve.tensor_tensor_scan(iota[:, :], ones[:, :], ones[:, :], -1.0, MUL, ADD))
        then(dve.tensor_tensor(tmp[:, 0, 0:P], ident[:, :], iota[:, :], MUL))
        then(dve.tensor_reduce(tokcol[:, :], tmp[:, 0, 0:P], AX, ADD))
        then(dve.tensor_scalar(upper[:, :], iota[:, :], tokcol[:, :], None, ALU.is_gt))
        dve.wait_ge(x2_in, 16 * NT)
        for n in range(4 * NT):
            i, t = n // NT, n % NT
            v, cols = min(t, 1), slice(i * 256, (i + 1) * 256)
            dve.wait_ge(wo_done, n + 1)
            dve.tensor_tensor(tmp[:, n % 2, 0:256], psum[:, n % 4, 0:256], bg1[:, v, cols], MUL).then_inc(wo_free, 1)
            dve.wait_ge(wo_free, n + 1)
            ins = dve.tensor_tensor(x2[:, t, cols], x2[:, t, cols], tmp[:, n % 2, 0:256], ADD)
            if i == 3:
                ins.then_inc(x2_done, 1)
        for t in range(NT + 1):
            if t < NT:
                v = min(t, 1)
                dve.wait_ge(h2_ss, t + 1)
                then(dve.tensor_scalar(rms[:, 24 + t:25 + t], rms[:, 16 + t:17 + t], 1.0 / D, EPS, MUL, ADD))
                dve.reciprocal(rms[:, 24 + t:25 + t], rms[:, 24 + t:25 + t]).then_inc(h2_inv, 1)
                dve.wait_ge(h2_rstd, t + 1)
                if t >= 2:
                    dve.wait_ge(h2_st[t % 2], 16 * (t // 2))
                    dve.wait_ge(h2_pe, 2 * (t - 1))
                then(dve.scalar_tensor_tensor(out=h2[:, t % 2, :], in0=x2[:, t, :], scalar=rms[:, 24 + t:25 + t],
                                              in1=bsc[:, v, :], op0=MUL, op1=MUL))
                dve.tensor_tensor(h2[:, t % 2, :], h2[:, t % 2, :], bsh[:, v, :], ADD).then_inc(h2_dve, 1)
            if t:
                dve.wait_ge(lg_done, t)
                dve.tensor_tensor(lg[:, t - 1, :], psum[:, 4, 0:20], rb[:, :], ADD).then_inc(lg_free, 1)
        routing(dve, then)
        def w_lo(b, c):
            g = G0 + 3 * b + c
            dve.wait_ge(e_hi, 3 * b + c + 1)
            dve.tensor_tensor((wl0, wl1)[b % 2][:, c, :], raw[:, g % NRAW, :], (wh0, wh1)[b % 2][:, c, :].bitcast(F32),
                              SUB).then_inc(e_lo_dve, 1)

        def x_low(b, q):
            dve.wait_ge(x_hi, 2 * b + q + 1)
            dve.tensor_tensor(xl[:, b % 2, 4 * q:4 * q + 4, :], psum[:, 2 + q, :].rearrange("p (k n) -> p k n", k=4),
                              xh[:, b % 2, 4 * q:4 * q + 4, :].bitcast(F32), SUB).then_inc(x_lo, 1)

        w_lo(0, 0)
        w_lo(0, 1)
        x_low(0, 0)
        x_low(0, 1)
        for b in range(NB):
            if b + 1 < NB:
                w_lo(b + 1, 0)
                w_lo(b + 1, 1)
            dve.wait_ge(sil_done, b + 1)
            if b:
                dve.wait_ge(at_done, b)
            dve.tensor_tensor(act_[:, :], psum[:, b % 2, DE:2 * DE], sil[:, :], MUL).then_inc(act_done, 1)
            if b + 1 < NB:
                x_low(b + 1, 0)
            dve.wait_ge(a_hi, b + 1)
            dve.tensor_tensor(al[:, :, :], psum[:, 4, 0:DE].rearrange("p (j n) -> p j n", j=2), ah[:, :, :].bitcast(F32),
                              SUB).then_inc(a_lo, 1)
            if b + 1 < NB:
                x_low(b + 1, 1)
            dve.wait_ge(e_used, b + 1)
            if b >= 2:
                dve.wait_ge(y_st[b % 2], 16 * (b // 2))
            dve.tensor_copy(yy[:, b % 2, 512:D], psum[:, 6, :]).then_inc(y_dve, 1)
        for t in range(NT):
            v = min(t, 1)
            dve.wait_ge(f_scaled, t + 1)
            if t >= 2:
                dve.wait_ge(f_st[t % 2], 16 * (t // 2))
            dve.scalar_tensor_tensor(out=yo[:, t % 2, :], in0=yb[:, t % 2, :], scalar=wgt[:, t, 1:2], in1=ya[:, t % 2, :],
                                     op0=MUL, op1=ADD).then_inc(f_taken, 1)
            dve.wait_ge(f_taken, t + 1)
            then(dve.tensor_tensor(yo[:, t % 2, :], yo[:, t % 2, :], bg2[:, v, :], MUL))
            dve.tensor_tensor(yo[:, t % 2, :], yo[:, t % 2, :], x2[:, t, :], ADD).then_inc(f_sum, 1)
            dve.wait_ge(f_ss, t + 1)
            then(dve.tensor_scalar(rms[:, 8 + t:9 + t], rms[:, t:t + 1], 1.0 / D, EPS, MUL, ADD))
            dve.reciprocal(rms[:, 8 + t:9 + t], rms[:, 8 + t:9 + t]).then_inc(f_inv, 1)
            dve.wait_ge(f_rstd, t + 1)
            dve.scalar_tensor_tensor(out=yo[:, t % 2, :], in0=yo[:, t % 2, :], scalar=rms[:, 8 + t:9 + t], in1=gfb[:, :],
                                     op0=MUL, op1=MUL).then_inc(f_out, 1)

    top.close()


_INS = ["x_prompt", "x_sample", "state_C", "state_n", "state_m", "c", "c_ctx", "norm1_g", "w_ada", "b_ada", "w_in", "b_in",
        "b_gates", "w_dw", "b_dw", "conv_ln_g", "conv_ln_b", "w_conv_out", "mlstm_hn_g", "w_mlstm_out", "w_o", "norm2_g",
        "w_rg", "b_rg", "w_re", "b_re", "w_e_gate", "w_e_up", "w_e_down", "norm_final_g"]
_OUTS = [("y_prompt", (1, TP, D)), ("y_sample", (1, TL, D)), ("new_C", (1, 1, 2, H, HD, HD)), ("new_n", (1, 1, 2, H, HD)),
         ("new_m", (1, 1, 2, H))]


def kernel(**inputs):
    import numpy as np
    import concourse.bacc as bacc
    from concourse.bass_utils import run_bass_kernel_spmd

    nc = bacc.Bacc("TRN2", target_bir_lowering=False, num_devices=1)
    arrays, a, out = {}, {}, {}
    for name in _INS:
        x = np.ascontiguousarray(inputs[name])
        arrays[f"in_{name}"] = x
        a[name] = nc.dram_tensor(f"in_{name}", x.shape, mybir.dt.from_np(x.dtype), kind="ExternalInput").ap()
    for name, shape in _OUTS:
        out[name] = nc.dram_tensor(f"out_{name}", shape, F32, kind="ExternalOutput").ap()
    build(nc, a, out)
    r = run_bass_kernel_spmd(nc, [arrays], core_ids=[0])
    return tuple(r.results[0][f"out_{name}"] for name, _ in _OUTS)
```

```python
from contextlib import ExitStack

import concourse.bass as bass
from concourse import mybir

P = 128
D = 1024
KT = D // P
TP, TL = 128, 512
T = TP + TL
NT = T // P
HALF = T // 2
H, HD = 4, 128
DI = H * HD
CT = DI // P
CK = 31
PADW = CK // 2
GW = 64
ROWS = TL // GW
PITCH = GW + PADW
U0 = PADW
U1 = PADW + TP + PADW
UW = U1 + ROWS * PITCH
YW = UW - 2 * PADW
NE, GE, NG = 16, 4, 4
DE = 256
CAP = P
OVER = 9
NB = NE + OVER
NS = NB + NB % 2
FILL = (NS - NE) // 2
CH = 2048
NRAW = 3
EPS = 1e-6
QS = HD ** -0.5
NEG = -1e30

F32, F32R, BF16, I32 = mybir.dt.float32, mybir.dt.float32r, mybir.dt.bfloat16, mybir.dt.int32
ALU = mybir.AluOpType
ACT = mybir.ActivationFunctionType
AX = mybir.AxisListType.X
MUL, ADD, SUB, MAX, MIN = ALU.mult, ALU.add, ALU.subtract, ALU.max, ALU.min

V_CTX, V_C, V_G1, V_BSH, V_BSC, V_BA, V_BGA, V_BQ, V_BK, V_BV, V_BO, V_BMA, V_BMB, V_BDW, V_LG, V_LB, V_HN, NV = (
    0, 8, 16, 24, 32, 40, 44, 48, 52, 56, 60, 64, 72, 80, 84, 88, 92, 96)

C_A, C_GA, C_Q, C_K, C_V, C_O, C_IF = 0, 512, 1024, 1536, 2048, 2560, 3072
C_MA, C_MB = C_IF + 16, C_IF + 16 + D


def units():
    u = [("ada", n) for n in range(8)]
    ada = iter(range(8, 24))

    def z(kind, n, with_ada=True):
        for i in range(n):
            u.append((kind, i))
            if with_ada and kind not in ("gmb",) or (with_ada and i < 2):
                k = next(ada, None)
                if k is not None:
                    u.append(("ada", k))

    for i in range(2):
        u.append(("ga", i))
        u.append(("a", i))
        u.append(("ada", next(ada)))
    for kind, n in (("v", 2), ("k", 2), ("q", 2), ("gma", 4), ("o", 2)):
        z(kind, n)
    for i in range(4):
        u.append(("gmb", i))
        k = next(ada, None)
        if k is not None:
            u.append(("ada", k))
    u += [("wc", 0), ("wm", 0), ("wc", 1), ("wm", 1)]
    u += [("wo", i) for i in range(4)]
    return u


UNITS = units()
G0 = len(UNITS)
WCOL = {"a": C_A, "ga": C_GA, "q": C_Q, "k": C_K, "v": C_V, "o": C_O, "gma": C_MA, "gmb": C_MB}
ZKINDS = tuple(WCOL)


def psum_tiles():
    out, by_unit = [], []
    for kind, i in UNITS:
        mine = []
        if kind == "ada":
            mine = [("ada", i)]
        elif kind in ZKINDS:
            mine = [(kind, 2 * i), (kind, 2 * i + 1)]
            if kind == "v" and i == 0:
                mine = [("gate", 0)] + mine
        by_unit.append([(len(out) + n, *m) for n, m in enumerate(mine)])
        out += mine
    return out, by_unit


TILES, TILES_OF = psum_tiles()
TILE_AT = {m: n for n, m in enumerate(TILES)}
UNIT_AT = {m: n for n, m in enumerate(UNITS)}


def chunk_order(first):
    return [0, 1, 2, 3, 4] if first == 0 else [0, 4, 3, 2, 1]


def build(nc, a, out):
    top = ExitStack()
    block_stack = ExitStack()

    def sem(name):
        return top.enter_context(nc.semaphore(name))

    def keep(name, shape, dt=F32):
        return top.enter_context(nc.sbuf_tensor(name, shape, dt))

    mod_d = nc.dram_tensor("mod_d", [4, 4 * D], F32, kind="Internal").ap()
    h2_d = nc.dram_tensor("h2_d", [T, D], F32, kind="Internal").ap()
    y_d = nc.dram_tensor("y_d", [NS * CAP, D], F32, kind="Internal").ap()

    ident = keep("ident", [P, P])
    identb = keep("identb", [P, P], BF16)
    ones = keep("ones", [P, P])
    onesb = keep("onesb", [P, P], BF16)
    mask = keep("mask", [P, 2, P], BF16)
    vcol = keep("vcol", [P, NV])
    taps = keep("taps", [P, CK * CT])
    cs = keep("cs", [P, 16])
    cst = keep("cst", [P, KT, 4], F32R)
    sel4 = keep("sel4", [4, 2])
    modrow = keep("modrow", [4, 256])
    mod1 = keep("mod1", [P, 16, 2])
    sh1 = keep("sh1", [P, KT, 2])
    sc1 = keep("sc1", [P, KT, 2])
    gbias = keep("gbias", [64, 4])
    m0 = keep("m0", [64, 1])
    rms = keep("rms", [P, 32])
    bqs = keep("bqs", [P, CT])
    lgs = keep("lgs", [P, CT])
    raw = keep("raw", [P, NRAW, CH])
    wh0 = keep("wh0", [P, 3, CH], F32R)
    wl0 = keep("wl0", [P, 3, CH], F32R)

    K = 1024
    spans = []

    def place(name, at, shape, dt=F32):
        with ExitStack() as s:
            if at:
                s.enter_context(nc.sbuf_tensor(f"gap_{name}", [P, int(at)], mybir.dt.uint8))
            t = s.enter_context(nc.sbuf_tensor(name, shape, dt))
        return t

    hh = place("hh", 0, [P, KT, T], F32R)
    hl = place("hl", 20 * K, [P, KT, T], F32R)
    qt = place("qt", 40 * K, [P, H, T])
    kt = place("kt", 50 * K, [P, H, T])
    ktok = place("ktok", 60 * K, [P, H, NT, HD])
    VT0 = 70 * K
    vtok = place("vtok", VT0, [P, H, NT, HD + 1])
    SG0 = 80 * K + 256
    sga = place("sga", SG0, [P, KT, T])
    CV0 = 100 * K + 256
    conv = place("conv", CV0, [P, 5, UW + 2])
    SM0 = 115 * K + 768
    rrow = place("rrow", SM0, [64, T])
    tokg = place("tokg", SM0 + 2560, [P, 3, NT, 8])
    decay = place("decay", SM0 + 3072, [P, 8, NT])
    wt = place("wt", SM0 + 3328, [P, 2, P])
    pt = place("pt", SM0 + 4352, [P, 2, P])
    kw = place("kw", SM0 + 5376, [P, 2, P])
    st = place("st", SM0 + 6400, [P, T])
    cn = place("cn", SM0 + 8960, [P, 2, HD + 1])
    inter = place("inter", SM0 + 8960 + 1056, [P, HD + 1])
    num = place("num", SM0 + 8960 + 1056 + 544, [P, NT, HD + 1])
    dn = place("dn", SM0 + 8960 + 1056 + 544 + 2592, [P, 3, NT])
    cn0 = place("cn0", SM0 + 13248, [P, 2, HD + 1])
    cout = place("cout", SM0 + 13248 + 1056, [P, HD + 1])
    gsum = place("gsum", SM0 + 13248 + 1056 + 544, [64, 2])
    mprev = place("mprev", SM0 + 13248 + 1056 + 576, [64, NT])
    mend = place("mend", SM0 + 13248 + 1056 + 608, [64, 1])
    hf = place("hf", CV0 + 3 * 4 * (UW + 2), [P, NT, HD])
    lnm = place("lnm", SM0, [P, YW])
    lnr = place("lnr", SM0 + 3072, [P, YW])
    lsq = place("lsq", SM0 + 6144, [P, 2, YW])
    hsq = place("hsq", 50 * K, [P, H * NT, HD])
    hrs = place("hrs", SM0 + 12288, [P, 3, H * NT])
    junk = place("junk", SG0, [P, NT, D])
    x5 = place("x5", 40 * K, [P, NT, D])
    vrow = place("vrow", 60 * K, [NV, P])
    drow = place("drow", 61 * K, [CK * CT, P])
    wgr = place("wgr", 62 * K, [P, KT, 16])
    wgh = place("wgh", 63 * K, [P, KT, P], F32R)
    wgl = place("wgl", 67 * K, [P, KT, P], F32R)
    xt = place("xt", SG0, [P, KT, T])
    sgt = place("sgt", 40 * K, [P, 2, T])
    at = place("at", 45 * K, [P, 2, T])
    vt = place("vt", SG0, [P, 2, T])
    gz = place("gz", SG0 + 5 * K, [P, 6, T])
    sgb = place("sgb", 40 * K, [P, KT, T])
    hmt = place("hmt", VT0, [P, H, T])
    ml = place("ml", 40 * K, [P, KT, T], F32R)
    mh = place("mh", SG0, [P, KT, T], F32R)
    mrg = place("mrg", SM0, [P, 2, 2, T])
    x2 = place("x2", 0, [P, NT, D])
    mk = place("mk", 20 * K, [5, 2, D])
    g2n = place("g2n", 28 * K, [P, D])
    tmp = place("tmp", 126 * K, [P, 2, 256])
    bg1 = place("bg1", 60 * K, [P, 2, D])
    bsh = place("bsh", 68 * K, [P, 2, D])
    bsc = place("bsc", CV0, [P, 2, D])
    R0 = CV0 + 8 * K
    lg = place("lg", R0, [P, NT, 20])
    wr = place("wr", R0 + 512, [P, KT, 20])
    rb = place("rb", R0 + 1536, [P, 20])
    iota = place("iota", R0 + 2 * K, [P, P])
    upper = place("upper", R0 + 2560, [P, P], BF16)
    wgt = place("wgt", R0 + 3 * K, [P, NT, 2])
    row_i = place("row_i", R0 + 3 * K + 64, [P, NT, 2], I32)
    slot_i = place("slot_i", R0 + 3 * K + 128, [P, NS], I32)
    expert_i = place("expert_i", R0 + 4 * K + 640, [P, NS], I32)
    pairs_i = place("pairs_i", R0 + 4 * K + 768, [P, 1], I32)
    sel5 = place("sel5", R0 + 3 * K + 320, [5, 2, P])
    h2t = place("h2t", 40 * K, [P, 2, KT, P])
    r1 = place("r1", 48 * K, [P, 20, NT * NE])
    oa = place("oa", 56 * K, [P, 2, NT, P], BF16)
    ob = place("ob", 59 * K, [P, 2, NT, 2, NS], BF16)
    obh = place("obh", 62 * K, [P, NT, NS])
    orow = place("orow", 64 * K, [P, NS - NE, NE])
    picks = place("picks", 65 * K, [P, NT, NE], BF16)
    h2 = place("h2", 20 * K, [P, NT, D])
    scol = place("scol", R0 + 4 * K + 512, [5, 2])
    tokcol = place("tokcol", R0 + 4 * K + 576, [P, 1])
    wh1 = place("wh1", 20 * K, [P, 3, CH], F32R)
    wl1 = place("wl1", 44 * K, [P, 3, CH], F32R)
    xh = place("xh", 68 * K, [P, 2, KT, P], F32R)
    xl = place("xl", 76 * K, [P, 2, KT, P], F32R)
    xg = place("xg", 84 * K, [P, 2, D])
    yy = place("yy", 92 * K, [P, 2, D])
    sil = place("sil", CV0, [P, DE])
    act_ = place("act", CV0 + K, [P, DE])
    slot_b = place("slot_b", CV0 + 4 * K, [P, 2], I32)
    ah = place("ah", CV0 + 2 * K, [P, 2, P], F32R)
    al = place("al", CV0 + 3 * K, [P, 2, P], F32R)
    tick = place("tick", CV0 + 4 * K + 64, [P, 3], I32)
    bg2 = place("bg2", R0 + 5 * K, [P, 2, D])
    gfb = place("gfb", R0 + 13 * K, [P, D])
    ya = place("ya", 20 * K, [P, NT, D])
    yb = place("yb", 40 * K, [P, NT, D])
    yo = place("yo", 60 * K, [P, NT, D])
    fsq = place("fsq", 84 * K, [P, D])
    hsqr = place("hsqr", 76 * K, [P, D])
    plane = lambda n, w: r1[:, n, 0:NT * w].rearrange("p (t w) -> p t w", w=w)
    rexp = [plane(0, NG), plane(1, 1)]

    psum = top.enter_context(nc.psum_tensor("psum", [P, 8, 512], F32))
    flat = psum[:, :, :].rearrange("p b n -> p (b n)")

    x_in, vec_in, gw_in, late_in = sem("x_in"), sem("vec_in"), sem("gw_in"), sem("late_in")
    state_in = [sem(f"state_in{i}") for i in range(2)]
    raw_in = [sem(f"raw_in{i}") for i in range(NRAW)]
    consts = sem("consts")
    late_consts = sem("late_consts")
    hi_done = sem("hi_done")
    lo_done = sem("lo_done")
    z_done = sem("z_done")
    z_free = sem("z_free")
    act_step = sem("act_step")
    dve_step = sem("dve_step")
    pe_start, cols_done = sem("pe_start"), sem("cols_done")
    x_ss, x_inv, x_rstd, x_scaled = sem("x_ss"), sem("x_inv"), sem("x_rstd"), sem("x_scaled")
    xt_turned, xt_free = sem("xt_turned"), sem("xt_free")
    cs_done, cst_hi, cst_lo = sem("cs_done"), sem("cst_hi"), sem("cst_lo")
    gate_in, wg_hi, wg_lo = sem("gate_in"), sem("wg_hi"), sem("wg_lo")
    tiny_done = sem("tiny_done")
    mod_st = sem("mod_st")
    h_hi, h_lo = sem("h_hi"), sem("h_lo")
    h_mod = sem("h_mod")
    u_done = sem("u_done")
    turn_done, turn_free = sem("turn_done"), sem("turn_free")
    gsum_done = sem("gsum_done")
    gate_abs, gate_ln, gate_max = sem("gate_abs"), sem("gate_ln"), sem("gate_max")
    gate_rows, gate_pe, gate_tables = sem("gate_rows"), sem("gate_pe"), sem("gate_tables")
    r_done = sem("r_done")
    st_done, st_free = sem("st_done"), sem("st_free")
    w_done = sem("w_done")
    p_done = sem("p_done")
    mm_done = sem("mm_done")
    t_done = sem("t_done")
    num_done = sem("num_done")
    cout_st, m_st = sem("cout_st"), sem("m_st")
    hn_inv, hn_rstd, hn_scaled, hn_pe, hmt_done = (
        sem(n) for n in ("hn_inv", "hn_rstd", "hn_scaled", "hn_pe", "hmt_done"))
    o_done = sem("o_done")
    conv_step, ln_pe, ln_cent, ln_sq, ln_inv, ln_rstd, ln_norm, ln_y = (
        sem(n) for n in ("conv_step", "ln_pe", "ln_cent", "ln_sq", "ln_inv", "ln_rstd", "ln_norm", "ln_y"))
    sga_done = sem("sga_done")
    b_hi, b_lo = sem("b_hi"), sem("b_lo")
    ab_done, ab_free = sem("ab_done"), sem("ab_free")
    m_sum, m_hi, m_lo = sem("m_sum"), sem("m_hi"), sem("m_lo")
    gb_in = [sem(f"gb_in{i}") for i in range(2)]
    gb_pe, gb_free, gb_dve = sem("gb_pe"), sem("gb_free"), sem("gb_dve")
    bsc_done = sem("bsc_done")
    x2_in, x2_done = sem("x2_in"), sem("x2_done")
    wo_done, wo_free = sem("wo_done"), sem("wo_free")
    h2_ss, h2_inv, h2_rstd, h2_dve, h2_pe, h2_ev, lg_done, lg_free = (
        sem(n) for n in ("h2_ss", "h2_inv", "h2_rstd", "h2_dve", "h2_pe", "h2_ev", "lg_done", "lg_free"))
    h2_st = sem("h2_st")
    rt_x, rt_exp, rt_pe = sem("rt_x"), sem("rt_exp"), sem("rt_pe")
    picked, hots, tables = sem("picked"), sem("hots"), sem("tables")
    e_hi, e_lo, d_hi, d_lo, e_used = (sem(n) for n in ("e_hi", "e_lo", "d_hi", "d_lo", "e_used"))
    slot_set = sem("slot_set")
    xg_in = [sem(f"xg_in{i}") for i in range(2)]
    xt_done, x_hi, x_lo = sem("xt_done"), sem("x_hi"), sem("x_lo")
    gu_done, sil_done, act_done, at_done, a_hi, a_lo, dn_done = (
        sem(n) for n in ("gu_done", "sil_done", "act_done", "at_done", "a_hi", "a_lo", "dn_done"))
    y_act, y_dve = sem("y_act"), sem("y_dve")
    y_st = [sem(f"y_st{i}") for i in range(2)]
    yg_in = [sem(f"yg_in{i}") for i in range(NT)]
    f_scaled, f_both, f_gated, f_sum, f_ss, f_inv, f_rstd, f_out = (
        sem(n) for n in ("f_scaled", "f_both", "f_gated", "f_sum", "f_ss", "f_inv", "f_rstd", "f_out"))
    f_st = sem("f_st")

    VROWS = [(V_CTX, a["c_ctx"]), (V_C, a["c"][0]), (V_G1, a["norm1_g"][0]),
             (V_BSH, a["b_ada"][0, 0:2 * D]), (V_BA, a["b_in"][0, C_A:C_Q]), (V_BQ, a["b_in"][0, C_Q:C_IF]),
             (V_BMA, a["b_in"][0, C_MA:C_MB + D]), (V_BDW, a["b_dw"][0]), (V_LG, a["conv_ln_g"][0]),
             (V_LB, a["conv_ln_b"][0]), (V_HN, a["mlstm_hn_g"][0])]

    def wsrc(kind, i):
        if kind == "ada":
            return a["w_ada"][0, :, i * 256:(i + 1) * 256].rearrange("(k p) n -> p k n", p=P)
        if kind in WCOL:
            c = WCOL[kind] + i * 256
            return a["w_in"][0, :, c:c + 256].rearrange("(k p) n -> p k n", p=P)
        if kind in ("wc", "wm"):
            w = a["w_conv_out" if kind == "wc" else "w_mlstm_out"]
            return w[0, :, i * 512:(i + 1) * 512].rearrange("(k p) n -> p k n", p=P)
        return a["w_o"][0, :, i * 256:(i + 1) * 256].rearrange("(k p) n -> p k n", p=P)

    def chunk(t, slot, rows):
        return t[:, slot, :].rearrange("p (k n) -> p k n", k=rows)

    def lat(plane, width):
        return conv[:, plane, width:width + ROWS * PITCH].rearrange("p (r w) -> p r w", w=PITCH)[:, :, 0:GW]

    def accp(c):
        return 4 if c == 0 else c - 1

    CHAINS = [(h, d) for h in range(H) for d in range(2)]
    hooks = {}
    def raw_owner(g):
        return (g - G0) % 3

    def raw_landed(eng, g):
        eng.wait_ge(raw_in[g % NRAW], 16 * (g // NRAW + 1))

    VEC_IN = 16 * (len(VROWS) + 1)
    GATE_IN = 16 * 8 + 32

    def chunk_used(eng, g):
        kind, i = UNITS[g]
        if TILES_OF[g]:
            eng.wait_ge(z_done, TILES_OF[g][-1][0] + 1)
        elif kind in ("wc", "wm"):
            eng.wait_ge(ab_done, 8 * (i + 1))
        else:
            eng.wait_ge(wo_done, NT * (i + 1))

    def split_matmuls(pe, dst, pairs):
        n = 3 * len(pairs)
        k = 0
        for lh, ll, rh, rl in pairs:
            for left, right in ((lh, rh), (lh, rl), (ll, rh)):
                mm = pe.matmul(dst, left, right, start=(k == 0), stop=(k == n - 1))
                k += 1
        return mm

    def load_mod(eng, j):
        if j >= 2:
            eng.wait_ge(gb_pe, 4 * (j - 1))
        eng.dma_start(mk[0:4, j % 2, :], mod_d[:, j * D:(j + 1) * D]).then_inc(gb_in[j % 2], 16)
        eng.dma_start(mk[4:5, j % 2, :], a["b_ada"][0:1, (j + 2) * D:(j + 3) * D]).then_inc(gb_in[j % 2], 16)

    def h2_out(act, t):
        act.wait_ge(h2_dve, t + 1)
        act.dma_start(h2_d[t * P:(t + 1) * P, :], h2[:, t, :]).then_inc(h2_st, 16)
        for n in range(t, NS - NE, NT):
            act.dma_start(y_d[(NE + n) * CAP:(NE + n + 1) * CAP, :], h2[:, t, :]).then_inc(y_st[n % 2], 16)
        if t >= 2:
            act.wait_ge(lg_done, t - 1)
        for q in range(2):
            act.wait_ge(h2_pe, 2 * t + q + 1)
            act.activation(h2t[:, t % 2, 4 * q:4 * q + 4, :],
                           psum[:, (2 * t + q) % 4, :].rearrange("p (k n) -> p k n", k=4), ACT.Copy).then_inc(h2_ev, 1)

    def routing(dve, then):
        four = lambda n: r1[:, n, 0:80].rearrange("p (t g e) -> p t g e", t=NT, g=NG)
        full = lambda n: r1[:, n, 0:80].rearrange("p (t e) -> p t e", t=NT)
        col = lambda n: r1[:, n, 0:NT]
        over = lambda ap, w: ap.unsqueeze(2).to_broadcast([P, NT, w])
        desc = r1[:, 19, 0:NG]
        then(dve.tensor_scalar(desc, iota[:, 0:NG], -1.0, float(NG), MUL, ADD))

        def first_max(src, top, hot, t1, t2):
            then(dve.tensor_reduce(top, src, AX, MAX))
            then(dve.tensor_tensor(t1, src, over(top, NG), ALU.is_ge))
            then(dve.tensor_tensor(t1, t1, desc.unsqueeze(1).to_broadcast([P, NT, NG]), MUL))
            then(dve.tensor_reduce(t2, t1, AX, MAX))
            then(dve.tensor_tensor(hot, t1, over(t2, NG), ALU.is_equal))

        gl, el = lg[:, :, 0:NG], lg[:, :, NG:20].rearrange("p t (g e) -> p t g e", g=NG)
        first_max(gl, col(2), plane(3, NG), plane(4, NG), col(5))
        dve.tensor_tensor(rexp[0], gl, over(col(2), NG), SUB).then_inc(rt_x, 1)
        then(dve.tensor_tensor(four(6), el, plane(3, NG).unsqueeze(3).to_broadcast([P, NT, NG, GE]), MUL))
        then(dve.tensor_reduce(plane(7, GE), four(6).rearrange("p t g e -> p t e g"), AX, ADD))
        first_max(plane(7, GE), col(8), plane(9, GE), plane(4, GE), col(5))
        then(dve.scalar_tensor_tensor(out=plane(10, GE), in0=plane(9, GE), scalar=NEG, in1=plane(7, GE), op0=MUL, op1=ADD))
        first_max(plane(10, GE), col(11), plane(12, GE), plane(4, GE), col(5))
        dve.tensor_tensor(r1[:, 1, 0:NT], col(11), col(8), SUB).then_inc(rt_x, 1)
        for n, hot in ((13, 9), (14, 12)):
            then(dve.tensor_tensor(four(n), plane(3, NG).unsqueeze(3).to_broadcast([P, NT, NG, GE]),
                                   plane(hot, GE).unsqueeze(2).to_broadcast([P, NT, NG, GE]), MUL))
        dve.tensor_tensor(picks[:, :, :], full(13), full(14), ADD).then_inc(picked, 1)
        dve.wait_ge(rt_exp, 2)
        then(dve.tensor_reduce(col(5), rexp[0], AX, ADD))
        then(dve.reciprocal(col(5), col(5)))
        then(dve.tensor_scalar(col(4), r1[:, 1, 0:NT], 1.0, None, ADD))
        then(dve.reciprocal(col(4), col(4)))
        then(dve.tensor_tensor(wgt[:, :, 0], col(4), col(5), MUL))
        then(dve.tensor_tensor(wgt[:, :, 1], wgt[:, :, 0], r1[:, 1, 0:NT], MUL))
        dve.wait_ge(rt_pe, 1)
        pos, q, cnt, ov, incl, base, blk, s = full(2), full(6), r1[:, 7, 0:NE], r1[:, 8, 0:NE], r1[:, 9, 0:NE], r1[:, 10, 0:NE], full(11), full(12)
        then(dve.tensor_copy(pos, psum[:, 5, 0:NT * NE].rearrange("p (t e) -> p t e", t=NT)))
        then(dve.tensor_copy(cnt, psum[:, 5, NT * NE:(NT + 1) * NE]))
        then(dve.tensor_scalar(q, pos, float(CAP), None, ALU.is_ge))
        then(dve.tensor_scalar(ov, cnt, float(CAP), None, ALU.is_gt))
        for k in range(2, -(-T // CAP)):
            then(dve.scalar_tensor_tensor(out=q, in0=pos, scalar=float(k * CAP), in1=q, op0=ALU.is_ge, op1=ADD))
            then(dve.scalar_tensor_tensor(out=ov, in0=cnt, scalar=float(k * CAP), in1=ov, op0=ALU.is_gt, op1=ADD))
        then(dve.tensor_tensor_scan(incl, ones[:, 0:NE], ov, 0.0, MUL, ADD))
        then(dve.tensor_tensor(base, incl, ov, SUB))
        then(dve.scalar_tensor_tensor(out=base, in0=base, scalar=float(NE - 1), in1=iota[:, 0:NE], op0=ADD, op1=SUB))
        wide = lambda ap: ap.unsqueeze(1).to_broadcast([P, NT, NE])
        then(dve.tensor_tensor(blk, q, wide(base), ADD))
        then(dve.tensor_scalar(full(15), q, 0.0, None, ALU.is_gt))
        then(dve.tensor_tensor(blk, blk, full(15), MUL))
        then(dve.tensor_tensor(blk, blk, wide(iota[:, 0:NE]), ADD))
        then(dve.scalar_tensor_tensor(out=s, in0=q, scalar=-float(CAP), in1=pos, op0=MUL, op1=ADD))
        for i, hot in enumerate((13, 14)):
            then(dve.tensor_tensor(full(15), full(hot), blk, MUL))
            then(dve.tensor_reduce(col(16), full(15), AX, ADD))
            then(dve.tensor_tensor(full(15), full(hot), s, MUL))
            then(dve.tensor_reduce(col(17), full(15), AX, ADD))
            then(dve.scalar_tensor_tensor(out=col(18), in0=col(16), scalar=float(CAP), in1=col(17), op0=MUL, op1=ADD))
            then(dve.tensor_copy(row_i[:, :, i], col(18)))
            then(dve.tensor_tensor(oa[:, i, :, :], iota[:, :].unsqueeze(1).to_broadcast([P, NT, P]), over(col(17), P),
                                   ALU.is_equal))
            then(dve.tensor_tensor(obh[:, :, :], iota[:, 0:NS].unsqueeze(1).to_broadcast([P, NT, NS]), over(col(16), NS),
                                   ALU.is_equal))
            then(dve.tensor_scalar(ob[:, i, :, 0, :], obh[:, :, :], tokcol[:, :], None, MUL))
            ins = dve.tensor_tensor(ob[:, i, :, 1, :], obh[:, :, :], over(iota[:, 0:NT], NS), MUL)
            if i == 0:
                then(ins)
        ins.then_inc(hots, 1)
        dve.wait_ge(hots, 1)
        over_e = r1[:, 17, 0:NS - NE]
        then(dve.tensor_tensor(orow[:, :, :], iota[:, 0:NS - NE].unsqueeze(2).to_broadcast([P, NS - NE, NE]),
                               incl.unsqueeze(1).to_broadcast([P, NS - NE, NE]), ALU.is_ge))
        then(dve.tensor_reduce(over_e, orow[:, :, :], AX, ADD))
        then(dve.tensor_scalar(over_e, over_e, float(NE - 1), None, MIN))
        dve.tensor_copy(expert_i[:, 0:NE], iota[:, 0:NE])
        dve.tensor_copy(expert_i[:, NE:NS], over_e)
        odds, pairs = r1[:, 18, 0:(NS - NE) // 2], r1[:, 18, 8:9]
        then(dve.tensor_scalar(odds, iota[:, 0:NS - NE:2], incl[:, NE - 1:NE], None, ALU.is_lt))
        then(dve.tensor_reduce(pairs, odds, AX, ADD))
        dve.tensor_copy(pairs_i[:, :], pairs)
        dve.wait_ge(rt_pe, 2)
        then(dve.tensor_copy(r1[:, 16, 0:2 * NS], psum[:, 6, 0:2 * NS]))
        then(dve.scalar_tensor_tensor(out=r1[:, 17, 0:NS], in0=r1[:, 16, NS:2 * NS], scalar=float(P), in1=r1[:, 16, 0:NS],
                                      op0=MUL, op1=ADD))
        dve.tensor_copy(slot_i[:, :], r1[:, 17, 0:NS]).then_inc(tables, 1)

    def pair_count(eng):
        eng.wait_ge(tables, 1)
        return eng.value_load(pairs_i[0:1, 0:1], min_val=0, max_val=(NS - NE) // 2) + NE // 2

    def over_pairs(eng, pairs, body):
        body(0, True, False)
        with eng.Fori(1, pairs - 1) as j:
            body(j, False, False)
        body(pairs - 1, False, True)

    def experts_pool(pool):
        pool.wait_ge(h2_st, 16 * NT)
        pairs = pair_count(pool)

        def carry(n, ap):
            pool.tensor_tensor(tick[:, n:n + 1], ap, ap, ADD)

        def gather(j, s, count):
            pool.tensor_copy(slot_b[:, s:s + 1], slot_i[:, bass.ds(count, 1)]).then_inc(slot_set, 1)
            pool.wait_ge(slot_set, count + 1)
            carry(0, slot_b[:, s:s + 1])
            pool.indirect_dma_start(out=xg[:, s, :], out_offset=None, in_=h2_d,
                                    in_offset=bass.IndirectOffsetOnAxis(ap=slot_b[:, s:s + 1], axis=0),
                                    bounds_check=T - 1).then_inc(xg_in[s], 16)

        def body(j, first, last):
            for s in range(2):
                b = 2 * j + s
                if not last:
                    pool.wait_ge(xt_done, 2 * b + 2)
                    carry(1, slot_i[:, 0:1])
                    gather(j + 1, s, b + 2)
                pool.wait_ge(d_hi, b + 1)
                pool.tensor_tensor((wl0, wl1)[s][:, 2, :], raw[:, (G0 + 2) % NRAW, :],
                                   (wh0, wh1)[s][:, 2, :].bitcast(F32), SUB).then_inc(d_lo, 1)

        gather(0, 0, 0)
        gather(0, 1, 1)
        over_pairs(pool, pairs, body)
        for i in range(2):
            pool.wait_ge(y_st[i], 16 * (pairs + FILL))
        carry(2, row_i[:, 0, 0:1])
        for t in range(NT):
            for i, buf in enumerate((ya, yb)):
                pool.indirect_dma_start(out=buf[:, t, :], out_offset=None, in_=y_d,
                                        in_offset=bass.IndirectOffsetOnAxis(ap=row_i[:, t, i:i + 1], axis=0),
                                        bounds_check=NS * CAP - 1).then_inc(yg_in[t], 16)

    block = top.enter_context(nc.Block())

    @block.sync
    def _(sp):
        for t in range(NT):
            src = a["x_prompt"][0] if t == 0 else a["x_sample"][0, (t - 1) * P:t * P, :]
            sp.dma_start(x5[:, t, :], src).then_inc(x_in, 16)
        for g, (kind, i) in enumerate(UNITS):
            if g >= NRAW:
                sp.wait_ge(lo_done, g - NRAW + 1)
            src = wsrc(kind, i)
            sp.dma_start(chunk(raw, g % NRAW, src.shape[1]), src).then_inc(raw_in[g % NRAW], 16)
        def block_weights(b, pick):
            for c, name in enumerate(("w_e_gate", "w_e_up", "w_e_down")):
                g = G0 + c
                if isinstance(b, int) and b == 0:
                    sp.wait_ge(lo_done, g - NRAW + 1)
                elif c == 2:
                    sp.wait_ge(d_lo, b)
                else:
                    sp.wait_ge(e_lo, 2 * b + c - 1)
                src = pick(a[name])
                sp.dma_start(chunk(raw, g % NRAW, src.shape[1]), src).then_inc(raw_in[g % NRAW], 16)

        for b in range(2):
            block_weights(b, lambda w: w[0, b, :, :].rearrange("(k p) n -> p k n", p=P))
        pairs = pair_count(sp)
        with sp.Fori(1, pairs) as j:
            for s in range(2):
                e = sp.value_load(expert_i[0:1, bass.ds(2 * j + s, 1)], min_val=0, max_val=NE - 1)
                block_weights(2 * j + s, lambda w: w[0, bass.ds(e, 1), :, :].rearrange("a (k p) n -> p (a k) n", p=P))

    @block.gpsimd
    def _(pool):
        pool.memset(ident[:, :], 0.0).then_inc(consts, 1)
        pool.memset(identb[:, :], 0.0).then_inc(consts, 1)
        pool.memset(ones[:, :], 1.0).then_inc(consts, 1)
        pool.memset(onesb[:, :], 1.0).then_inc(consts, 1)
        pool.memset(mask[:, :, :], 0.0).then_inc(consts, 1)
        pool.memset(conv[:, :, :], 0.0).then_inc(consts, 1)
        pool.memset(wgh[:, :, :].bitcast(F32), 0.0).then_inc(consts, 1)
        pool.memset(wgl[:, :, :].bitcast(F32), 0.0).then_inc(consts, 1)
        pool.memset(gbias[:, :], 0.0).then_inc(consts, 1)
        pool.memset(m0[:, :], 0.0).then_inc(consts, 1)
        pool.wait_ge(consts, 10)
        for t in (ident, identb):
            pool.affine_select(out=t[:, :], in_=t[:, :], compare_op=ALU.not_equal, fill=1.0, base=0,
                               pattern=[[-1, P]], channel_multiplier=1).then_inc(consts, 1)
        pool.affine_select(out=mask[:, 0, :], in_=mask[:, 0, :], compare_op=ALU.is_ge, fill=NEG, base=0,
                           pattern=[[1, P]], channel_multiplier=-1).then_inc(consts, 1)
        pool.affine_select(out=mask[:, 1, :], in_=mask[:, 1, :], compare_op=ALU.is_ge, fill=NEG, base=0,
                           pattern=[[-1, P]], channel_multiplier=1).then_inc(consts, 1)
        for g in range(G0):
            if g == UNIT_AT["v", 0] - 1:
                pool.wait_ge(h_lo, KT)
                pool.memset(gz[0:64, 5, :], 1.0).then_inc(consts, 1)
                pool.wait_ge(consts, 15)
                pool.memset(gz[0:32, 5, 0:T:P], 0.0).then_inc(consts, 1)
                pool.memset(gz[32:64, 5, P - 1:T:P], 0.0).then_inc(consts, 1)
                pool.wait_ge(consts, 17)
            pool.wait_ge(hi_done, g + 1)
            pool.tensor_tensor(wl0[:, g % 3, :], raw[:, g % NRAW, :], wh0[:, g % 3, :].bitcast(F32),
                               SUB).then_inc(lo_done, 1)
        experts_pool(pool)

    @block.tensor
    def _(pe):
        def turn(dst, src, n=P):
            return pe.transpose(dst, src, ident[0:n, 0:n])

        pe.wait_ge(consts, 14)
        pe.wait_ge(vec_in, VEC_IN)
        turn(psum[:, 4, 0:NV], vrow[:, :], NV)
        turn(psum[:, 4, 128:128 + CK * CT], drow[:, :], CK * CT).then_inc(pe_start, 1)
        for t in range(NT):
            pe.wait_ge(x_scaled, t + 1)
            for q in range(2):
                n = 2 * t + q
                if n >= 4:
                    pe.wait_ge(xt_free, n - 3)
                for k in range(4):
                    mm = turn(psum[:, n % 4, k * P:(k + 1) * P], x5[:, t, (4 * q + k) * P:(4 * q + k + 1) * P])
                mm.then_inc(xt_turned, 1)
        pe.wait_ge(xt_free, 2 * NT)
        pe.wait_ge(cst_lo, 1)

        def tiny(n):
            pe.wait_ge(z_free, TILE_AT["ada", n] + 1)
            for j in range(2):
                mm = pe.matmul(psum[:, 6, 4 * n + 2 * j:4 * n + 2 * j + 2], modrow[:, j * P:(j + 1) * P], sel4[:, :],
                               start=True, stop=True)
            mm.then_inc(tiny_done, 1)

        def open_tile(tile):
            if tile >= 2:
                pe.wait_ge(z_free, tile - 1)
            return 2 * (tile % 2)

        def gemm(tile, wh, wl, hook=None):
            p = open_tile(tile)
            for k in range(KT):
                pe.wait_ge(h_lo, k + 1)
                for x, (w, r) in enumerate(((wh(k), hh), (wh(k), hl), (wl(k), hh))):
                    for q in range(2):
                        mm = pe.matmul(psum[:, p + q, 0:HALF], w, r[:, k, q * HALF:(q + 1) * HALF],
                                       start=(k == 0 and x == 0), stop=(k == KT - 1 and x == 2))
                if hook:
                    hook(k)
            mm.then_inc(z_done, 1)

        def turn_tokens(kind, h):
            pe.wait_ge(z_free, TILE_AT[kind, h] + 1)
            n = h if kind == "v" else H + h
            if n:
                pe.wait_ge(turn_free, n)
            src = vt[:, h % 2, :] if kind == "v" else kt[:, h, :]
            for t in range(NT):
                mm = turn(flat[:, 4 * 512 + t * P:4 * 512 + (t + 1) * P], src[:, t * P:(t + 1) * P])
            mm.then_inc(turn_done, 1)

        def gates_turn():
            pe.wait_ge(gate_rows, 1)
            pe.wait_ge(turn_free, 2 * H)
            for t in range(NT):
                turn(flat[:, 4 * 512 + t * P:4 * 512 + (t + 1) * P], gz[:, 4, t * P:(t + 1) * P])
            for t in range(NT):
                turn(psum[:, 6, t * 64:(t + 1) * 64], gz[0:64, 3, t * P:(t + 1) * P], 64)
            for ci, (h, d) in enumerate(CHAINS):
                col = 64 + 32 * d + h
                mm = pe.matmul(psum[:, 7, ci * NT:(ci + 1) * NT], ident[64:128, col:col + 1].to_broadcast([64, P]),
                               gz[64:128, 4, (0 if d else P - 1):T:P], start=True, stop=True)
            mm.then_inc(gate_pe, 1)

        def exponents(ci):
            h, d = CHAINS[ci]
            if ci:
                pe.wait_ge(w_done, NT * ci)
            row = ident[0:64, 32 * d + h:32 * d + h + 1].to_broadcast([64, P])
            pe.matmul(psum[:, 4, :], row, rrow[:, P:T], start=True, stop=False)
            pe.matmul(psum[:, 4, :], identb[:, :], mask[:, d:d + 1, :].to_broadcast([P, 4, P]), start=False, stop=True)
            pe.matmul(psum[:, 5, 0:P], row, rrow[:, 0:P], start=True, stop=False)
            pe.matmul(psum[:, 5, 0:P], identb[:, :], mask[:, d, :], start=False, stop=True).then_inc(r_done, 1)

        def scores(ci):
            h, _ = CHAINS[ci]
            if ci:
                pe.wait_ge(num_done, NT * ci)
            for t in range(NT):
                mm = pe.matmul(flat[:, 6 * 512 + t * P:6 * 512 + (t + 1) * P], kt[:, h, t * P:(t + 1) * P],
                               qt[:, h, t * P:(t + 1) * P], start=True, stop=True)
            mm.then_inc(st_done, 1)

        def step(ci, i):
            h, d = CHAINS[ci]
            n = NT * ci + i
            c = chunk_order(d)[i]
            pe.wait_ge(p_done, n + 1)
            if n:
                pe.wait_ge(num_done, n)
            mm = pe.matmul(psum[:, 6, 0:HD + 1], pt[:, n % 2, :], vtok[:, h, c, :], start=True, stop=True)
            if i < NT - 1:
                mm = pe.matmul(psum[:, 6, 256:256 + HD + 1], kw[:, n % 2, :], vtok[:, h, c, :], start=True, stop=True)
            if i:
                if i == 1:
                    pe.wait_ge(state_in[ci % 2], 32 * (ci // 2 + 1))
                state = cn0[:, ci % 2, :] if i == 1 else cn[:, i % 2, :]
                mm = pe.matmul(psum[:, 7, 0:HD + 1], qt[:, h, c * P:(c + 1) * P], state, start=True, stop=True)
            mm.then_inc(mm_done, 1)

        def chain_hook(ci):
            def run(k):
                if k == 0:
                    exponents(ci)
                    if CHAINS[ci][1] == 0:
                        scores(ci)
                elif k >= 3:
                    step(ci, k - 3)
            return run

        def heads_turn():
            pe.wait_ge(hn_scaled, 1)
            pe.wait_ge(num_done, NT * len(CHAINS))
            for h in range(H):
                if h:
                    pe.wait_ge(hmt_done, h)
                for t in range(NT):
                    mm = turn(flat[:, 6 * 512 + t * P:6 * 512 + (t + 1) * P], ktok[:, h, t, :])
                mm.then_inc(hn_pe, 1)

        def channel_sums(n):
            for c in range(CT):
                if n == 0:
                    pe.wait_ge(conv_step, CK * CT)
                    src = conv[:, accp(c), 0:YW]
                else:
                    pe.wait_ge(ln_sq, c + 1)
                    src = lsq[:, c % 2, :]
                for q in range(2):
                    mm = pe.matmul(psum[:, 4 + q, 0:YW // 2], ones[:, :], src[:, q * (YW // 2):(q + 1) * (YW // 2)],
                                   start=(c == 0), stop=(c == CT - 1))
                if n == 1:
                    mm.then_inc(ln_pe, 1)
            if n == 0:
                mm.then_inc(ln_pe, 1)

        for g, (kind, i) in enumerate(UNITS):
            if kind in ("wc", "wm", "wo"):
                continue
            pe.wait_ge(lo_done, g + 1)
            hi, lo = wh0[:, g % 3, :], wl0[:, g % 3, :]
            if kind == "v" and i == 0:
                pe.wait_ge(wg_lo, 4)
                gemm(TILE_AT["gate", 0], lambda k: wgh[:, k, :], lambda k: wgl[:, k, :])
            if kind == "ada":
                tile = TILE_AT[kind, i]
                p = open_tile(tile)
                for k in range(KT):
                    for j, w in enumerate((hi, lo)):
                        mm = pe.matmul(psum[0:4, p, 0:256], cst[:, k, :], w[:, k * 256:(k + 1) * 256],
                                       start=(k == 0 and j == 0), stop=(k == KT - 1 and j == 1))
                mm.then_inc(z_done, 1)
                if 1 <= i < 8:
                    tiny(i - 1)
                if i == 7:
                    tiny(7)
            else:
                for j in range(2):
                    n = 2 * i + j
                    hook = chain_hook(n) if kind == "gma" else None
                    if kind == "gma" and n == 0:
                        gates_turn()
                        pe.wait_ge(gate_tables, 1)
                    w = lambda t: (lambda k: t[:, k * 256 + j * P:k * 256 + (j + 1) * P])
                    gemm(TILE_AT[kind, n], w(hi), w(lo), hook)
                    if kind in ("v", "k") and n:
                        turn_tokens(kind, n - 1)
                    if (kind, n) == ("k", 0):
                        turn_tokens("v", H - 1)
                    if (kind, n) == ("q", 0):
                        turn_tokens("k", H - 1)
                    if (kind, n) == ("o", 1):
                        heads_turn()
                    if (kind, n) == ("o", 3):
                        channel_sums(0)
                    if (kind, n) == ("gmb", 1):
                        channel_sums(1)

        for half in range(2):
            g = UNIT_AT["wc", half]
            pe.wait_ge(lo_done, g + 2)
            pe.wait_ge(b_lo, 8)
            for m in range(4):
                for br in range(2):
                    n = 8 * half + 2 * m + br
                    if n >= 2:
                        pe.wait_ge(ab_free, n - 1)
                    else:
                        pe.wait_ge(z_free, len(TILES))
                    p = 2 * (n % 2)
                    slot = (g + br) % 3
                    for k in range(4):
                        cols = slice(k * 512 + m * P, k * 512 + (m + 1) * P)
                        hi, lo = wh0[:, slot, cols], wl0[:, slot, cols]
                        for x, (w, r) in enumerate(((hi, hh), (hi, hl), (lo, hh))):
                            for q in range(2):
                                mm = pe.matmul(psum[:, p + q, 0:HALF], w, r[:, 4 * br + k, q * HALF:(q + 1) * HALF],
                                               start=(k == 0 and x == 0), stop=(k == 3 and x == 2))
                    mm.then_inc(ab_done, 1)

        def broadcast(j):
            pe.wait_ge(gb_in[j % 2], 32 * (j // 2 + 1))
            pe.wait_ge(gb_dve, 1)
            if j:
                pe.wait_ge(gb_free, 4 * j)
            for v in range(2):
                for q in range(2):
                    pe.matmul(psum[:, 4 + 2 * v + q, :], sel5[:, v, :], mk[:, j % 2, q * 512:(q + 1) * 512],
                              start=True, stop=True).then_inc(gb_pe, 1)

        for j in range(4):
            broadcast(j)
        for i in range(4):
            g = UNIT_AT["wo", i]
            pe.wait_ge(lo_done, g + 1)
            for t in range(NT):
                n = NT * i + t
                if n >= 4:
                    pe.wait_ge(wo_free, n - 3)
                elif n < 2:
                    pe.wait_ge(ab_free, 16)
                for k in range(KT):
                    if i == 0 and t == 0:
                        pe.wait_ge(m_lo, k + 1)
                    l_hi, l_lo = mh[:, k, t * P:(t + 1) * P], ml[:, k, t * P:(t + 1) * P]
                    w_hi, w_lo = (w[:, g % 3, k * 256:(k + 1) * 256] for w in (wh0, wl0))
                    for x, (l, r) in enumerate(((l_hi, w_hi), (l_hi, w_lo), (l_lo, w_hi))):
                        mm = pe.matmul(psum[:, n % 4, 0:256], l, r, start=(k == 0 and x == 0),
                                       stop=(k == KT - 1 and x == 2))
                mm.then_inc(wo_done, 1)
        for t in range(NT):
            pe.wait_ge(h2_dve, t + 1)
            for q in range(2):
                n = 2 * t + q
                if n >= 4:
                    pe.wait_ge(h2_ev, n - 3)
                elif n == 0:
                    pe.wait_ge(wo_free, 4 * NT)
                for k in range(4):
                    mm = turn(psum[:, n % 4, k * P:(k + 1) * P], h2[:, t, (4 * q + k) * P:(4 * q + k + 1) * P])
                mm.then_inc(h2_pe, 1)
            pe.wait_ge(h2_ev, 2 * t + 2)
            if t == 0:
                pe.wait_ge(gb_free, 16)
            else:
                pe.wait_ge(lg_free, t)
            for k in range(KT):
                mm = pe.matmul(psum[:, 4, 0:20], h2t[:, t % 2, k, :], wr[:, k, :], start=(k == 0), stop=(k == KT - 1))
            mm.then_inc(lg_done, 1)
        pe.wait_ge(picked, 1)
        for t in range(NT):
            for s in range(t):
                pe.matmul(psum[:, 5, t * NE:(t + 1) * NE], onesb[:, :], picks[:, s, :], start=(s == 0), stop=False)
            pe.matmul(psum[:, 5, t * NE:(t + 1) * NE], upper[:, :], picks[:, t, :], start=(t == 0), stop=True)
        for t in range(NT):
            mm = pe.matmul(psum[:, 5, NT * NE:(NT + 1) * NE], onesb[:, :], picks[:, t, :], start=(t == 0),
                           stop=(t == NT - 1))
        mm.then_inc(rt_pe, 1)
        pe.wait_ge(hots, 1)
        for n in range(2 * NT):
            mm = pe.matmul(psum[:, 6, 0:2 * NS], oa[:, n // NT, n % NT, :], ob[:, n // NT, n % NT, :, :],
                           start=(n == 0), stop=(n == 2 * NT - 1))
        mm.then_inc(rt_pe, 1)

        def turn_x(j, s, b):
            pe.wait_ge(xg_in[s], 16 * j + 16)
            for q in range(2):
                if not (isinstance(b, int) and b == 0):
                    pe.wait_ge(x_lo, 2 * b + q - 1)
                for k in range(4):
                    mm = turn(psum[:, 2 + q, k * P:(k + 1) * P], xg[:, s, (4 * q + k) * P:(4 * q + k + 1) * P])
                mm.then_inc(xt_done, 1)

        def turn_act(b, first=False):
            pe.wait_ge(act_done, b + 1)
            if not first:
                pe.wait_ge(a_lo, b)
            for j in range(2):
                mm = turn(psum[:, 4, j * P:(j + 1) * P], act_[:, j * P:(j + 1) * P])
            mm.then_inc(at_done, 1)

        def down(s, b, first=False):
            wh, wl = (wh0, wh1)[s], (wl0, wl1)[s]
            pe.wait_ge(a_lo, b + 1)
            pe.wait_ge(d_lo, b + 1)
            if not first:
                pe.wait_ge(y_act, b)
                pe.wait_ge(y_dve, b)
            for q in range(2):
                cols = lambda w, j: w[:, 2, j * D + q * 512:j * D + (q + 1) * 512]
                mm = split_matmuls(pe, psum[:, 5 + q, :],
                                   [(ah[:, j, :], al[:, j, :], cols(wh, j), cols(wl, j)) for j in range(2)])
            mm.then_inc(e_used, 1)

        pe.wait_ge(h2_ev, 2 * NT)
        pe.wait_ge(gb_free, 16)
        turn_x(0, 0, 0)
        pairs = pair_count(pe)

        def body(j, first, last):
            for s in range(2):
                b = 2 * j + s
                start = first and s == 0
                if not start:
                    turn_act(b - 1, first and s == 1)
                if not (last and s == 1):
                    turn_x(j + s, 1 - s, b + 1)
                wh, wl = (wh0, wh1)[s], (wl0, wl1)[s]
                pe.wait_ge(e_lo, 2 * b + 2)
                pe.wait_ge(x_lo, 2 * b + 2)
                both = lambda w, k: w[:, 0:2, k * DE:(k + 1) * DE]
                split_matmuls(pe, psum[:, s, :], [(xh[:, s, k, :], xl[:, s, k, :], both(wh, k), both(wl, k))
                                                  for k in range(KT)]).then_inc(gu_done, 1)
                if not start:
                    down(1 - s, b - 1, first and s == 1)

        over_pairs(pe, pairs, body)
        turn_act(2 * pairs - 1)
        down(1, 2 * pairs - 1)

    @block.scalar
    def _(act):
        def raw_hi(g):
            raw_landed(act, g)
            if g >= 3:
                chunk_used(act, g - 3)
            act.activation(wh0[:, g % 3, :], raw[:, g % NRAW, :], ACT.Copy).then_inc(hi_done, 1)

        pair = lambda tile, rows=slice(0, P): psum[rows, 2 * (tile % 2):2 * (tile % 2) + 2, 0:HALF]
        halves = lambda ap: ap.rearrange("p (q n) -> p q n", q=2)

        for row, src in VROWS:
            n = src.shape[0] // P
            act.dma_start(vrow[row:row + n, :], src.rearrange("(r p) -> r p", p=P)).then_inc(vec_in, 16)
        act.dma_start(drow[:, :], a["w_dw"][0].rearrange("k (c p) -> (k c) p", p=P)).then_inc(vec_in, 16)
        act.dma_start(wgr[:, :, :], a["w_in"][0, :, C_IF:C_MA].rearrange("(k p) n -> p k n", p=P)).then_inc(gw_in, 16)
        act.wait_ge(consts, 10)
        for d in range(2):
            for f in range(2):
                rows = slice(32 * d, 32 * d + H)
                c = C_IF + 8 * d + 4 * f
                act.dma_start(gbias[rows, 2 * f:2 * f + 1], a["b_in"][0, c:c + H].rearrange("(h o) -> h o", o=1)).then_inc(gate_in, 16)
                act.dma_start(gbias[rows, 2 * f + 1:2 * f + 2], a["b_gates"][0, d, f].rearrange("(h o) -> h o", o=1)).then_inc(gate_in, 16)
            act.dma_start(m0[rows, :], a["state_m"][0, 0, d].rearrange("(h o) -> h o", o=1)).then_inc(gate_in, 16)
        act.wait_ge(x_in, 16 * NT)
        for t in range(NT):
            act.activation(junk[:, t, :], x5[:, t, :], ACT.Square, accum_out=rms[:, t:t + 1]).then_inc(x_ss, 1)
        act.wait_ge(x_inv, 1)
        act.activation(rms[:, 8:8 + NT], rms[:, 8:8 + NT], ACT.Sqrt).then_inc(x_rstd, 1)
        act.wait_ge(cols_done, 1)
        act.activation(cs[:, :], vcol[:, 0:16], ACT.Silu).then_inc(cs_done, 1)
        act.wait_ge(cs_done, 1)
        act.activation(cst[:, :, 0:2], cs[:, :].rearrange("p (v k) -> p k v", v=2), ACT.Copy).then_inc(cst_hi, 1)
        raw_hi(0)
        raw_hi(1)
        for n in range(2 * NT):
            t, q = n // 2, n % 2
            act.wait_ge(xt_turned, n + 1)
            act.activation(xt[:, 4 * q:4 * q + 4, t * P:(t + 1) * P], psum[:, n % 4, :].rearrange("p (k n) -> p k n", k=4),
                           ACT.Copy).then_inc(xt_free, 1)
        act.wait_ge(gw_in, 16)
        for d in range(2):
            for f in range(2):
                act.activation(wgh[:, :, 64 * f + 32 * d:64 * f + 32 * d + H], wgr[:, :, 8 * d + 4 * f:8 * d + 4 * f + H],
                               ACT.Copy).then_inc(wg_hi, 1)

        def load_state(ci):
            h, d = CHAINS[ci]
            if ci >= 2:
                act.wait_ge(num_done, NT * (ci - 2) + 2)
            act.dma_start(cn0[:, ci % 2, 0:HD], a["state_C"][0, 0, d, h]).then_inc(state_in[ci % 2], 16)
            act.dma_start(cn0[:, ci % 2, HD:HD + 1], a["state_n"][0, 0, d, h].rearrange("(p o) -> p o", o=1)).then_inc(state_in[ci % 2], 16)

        def turned(kind, h):
            n = h if kind == "v" else H + h
            act.wait_ge(turn_done, n + 1)
            src = flat[:, 4 * 512:4 * 512 + T].rearrange("p (t n) -> p t n", t=NT)
            dst = vtok[:, h, :, 0:HD] if kind == "v" else ktok[:, h, :, :]
            act.activation(dst, src, ACT.Copy).then_inc(turn_free, 1)

        def gates():
            act.wait_ge(gate_abs, 1)
            act.activation(gz[0:64, 2, :], gz[0:64, 2, :], ACT.Exp, scale=-1.0).then_inc(act_step, 1)
            act.wait_ge(act_step, 1)
            act.activation(gz[0:64, 2, :], gz[0:64, 2, :], ACT.Ln, bias=1.0).then_inc(gate_ln, 1)

        def gates2():
            act.wait_ge(gate_max, 1)
            for d in range(2):
                act.dma_start(out["new_m"][0, 0, d].rearrange("(h o) -> h o", o=1),
                              mend[32 * d:32 * d + H, :]).then_inc(m_st, 16)
            act.activation(gz[64:128, 4, :], gz[0:64, 1, :], ACT.Exp)
            act.activation(gz[0:64, 3, :], gz[0:64, 3, :], ACT.Exp, scale=-1.0).then_inc(gate_rows, 1)

        def chain(ci):
            h, d = CHAINS[ci]
            order = chunk_order(d)
            col = 4 * d + h

            def weights(i):
                n, c = NT * ci + i, order[i]
                if n >= 2:
                    act.wait_ge(p_done, n - 1)
                src = psum[:, 4, (c - 1) * P:c * P] if c else psum[:, 5, 0:P]
                act.activation(wt[:, n % 2, :], src, ACT.Exp, bias=tokg[:, 0, c, col:col + 1]).then_inc(w_done, 1)

            if ci + 1 < len(CHAINS):
                load_state(ci + 1)
            act.wait_ge(r_done, ci + 1)
            if d == 0:
                act.wait_ge(st_done, h + 1)
                if h:
                    act.wait_ge(p_done, 2 * NT * h)
                act.activation(st[:, :], flat[:, 6 * 512:6 * 512 + T], ACT.Copy).then_inc(st_free, 1)
            weights(0)
            weights(1)
            for i in range(NT):
                n, c = NT * ci + i, order[i]
                if i:
                    act.wait_ge(mm_done, n + 1)
                    act.wait_ge(num_done, n)
                    if i == 1:
                        act.dma_start(out["new_C"][0, 0, d, h], cout[:, 0:HD]).then_inc(cout_st, 16)
                        act.dma_start(out["new_n"][0, 0, d, h].rearrange("(p o) -> p o", o=1),
                                      cout[:, HD:HD + 1]).then_inc(cout_st, 16)
                    act.activation(inter[:, :], psum[:, 7, 0:HD + 1], ACT.Copy,
                                   scale=tokg[:, 1, c, col:col + 1]).then_inc(t_done, 1)
                if i + 2 < NT:
                    weights(i + 2)

        def evacuate(tile, kind, i):
            if kind == "gma":
                if i == 0:
                    load_state(0)
                    act.wait_ge(gate_tables, 1)
                chain(i)
            act.wait_ge(z_done, tile + 1)
            bias = lambda base: vcol[:, base + i:base + i + 1]

            def z(dst, func, base, **more):
                act.activation(halves(dst), pair(tile), func, bias=bias(base), **more).then_inc(z_free, 1)

            if kind == "ada":
                if 1 <= i <= 8:
                    act.wait_ge(tiny_done, i)
                elif i:
                    act.wait_ge(mod_st, 16 * (i - 8))
                act.activation(modrow[:, :], psum[0:4, 2 * (tile % 2), 0:256], ACT.Copy).then_inc(z_free, 1)
                if i >= 8:
                    act.wait_ge(z_free, tile + 1)
                    act.dma_start(mod_d[:, (i - 8) * 256:(i - 7) * 256], modrow[:, :]).then_inc(mod_st, 16)
            elif kind == "ga":
                if i >= 2:
                    act.wait_ge(u_done, i - 1)
                z(sgt[:, i % 2, :], ACT.Sigmoid, V_BGA)
            elif kind == "a":
                z(at[:, i % 2, :], ACT.Identity, V_BA)
            elif kind == "gate":
                act.wait_ge(h_lo, KT)
                act.wait_ge(gsum_done, 1)
                act.activation(halves(gz[0:64, 0, :]), pair(tile, slice(0, 64)), ACT.Identity, bias=gsum[:, 0:1])
                act.activation(halves(gz[0:64, 1, :]), pair(tile, slice(64, P)), ACT.Identity,
                               bias=gsum[:, 1:2]).then_inc(z_free, 1)
                act.activation(vtok[:, :, :, HD], ones[:, 0:H * NT].rearrange("p (h t) -> p h t", h=H), ACT.Copy)
            elif kind == "v":
                if i >= 2:
                    act.wait_ge(turn_done, i - 1)
                z(vt[:, i % 2, :], ACT.Identity, V_BV)
                if i:
                    turned("v", i - 1)
            elif kind == "k":
                z(kt[:, i, :], ACT.Identity, V_BK)
                turned("k", i - 1) if i else turned("v", H - 1)
                if i == 0:
                    gates()
            elif kind == "q":
                act.wait_ge(u_done, CT)
                act.activation(halves(qt[:, i, :]), pair(tile), ACT.Identity, bias=bqs[:, i:i + 1],
                               scale=QS).then_inc(z_free, 1)
                if i == 0:
                    turned("k", H - 1)
                    gates2()
            elif kind == "gma":
                z(sga[:, i, :], ACT.Identity, V_BMA)
            elif kind == "o":
                if i >= 2:
                    act.wait_ge(o_done, i - 1)
                z(sgt[:, i % 2, :], ACT.Sigmoid, V_BO)
                if i == 1:
                    act.wait_ge(hn_inv, 1)
                    act.activation(hrs[:, 1, :], hrs[:, 1, :], ACT.Sqrt).then_inc(hn_rstd, 1)
                    for h in range(H):
                        act.wait_ge(hn_pe, h + 1)
                        act.activation(hmt[:, h, :], flat[:, 6 * 512:6 * 512 + T], ACT.Copy,
                                       scale=vcol[:, V_HN + h:V_HN + h + 1]).then_inc(hmt_done, 1)
                if i == 3:
                    act.activation(sga[:, :, :], sga[:, :, :], ACT.Sigmoid).then_inc(sga_done, 1)
            elif kind == "gmb":
                act.wait_ge(o_done, H)
                z(sgb[:, i, :], ACT.Sigmoid, V_BMB)
                if i == 0:
                    act.wait_ge(ln_cent, CT)
                    for c in range(CT):
                        if c >= 2:
                            act.wait_ge(ln_pe, c)
                        act.activation(lsq[:, c % 2, :], conv[:, accp(c), 0:YW], ACT.Square).then_inc(ln_sq, 1)
                if i == 3:
                    act.wait_ge(ln_inv, 1)
                    act.activation(lnr[:, :], lnr[:, :], ACT.Sqrt).then_inc(ln_rstd, 1)
                    for c in range(CT):
                        act.wait_ge(ln_norm, c + 1)
                        act.activation(conv[:, accp(c), 0:YW], conv[:, accp(c), 0:YW], ACT.Silu,
                                       bias=vcol[:, V_LB + c:V_LB + c + 1], scale=vcol[:, V_LG + c:V_LG + c + 1]).then_inc(ln_y, 1)

        for g, (kind, i) in enumerate(UNITS):
            if g + 2 < G0 and kind != "wm":
                raw_hi(g + 2)
            for tile, k, n in TILES_OF[g]:
                evacuate(tile, k, n)
            if (kind, i) == ("ada", 7):
                for k in range(KT):
                    act.wait_ge(h_mod, k + 1)
                    act.activation(hh[:, k, :], xt[:, k, :], ACT.Copy).then_inc(h_hi, 1)
            if (kind, i) == ("wc", 0):
                act.wait_ge(ln_y, CT)
                act.wait_ge(o_done, H)
                act.wait_ge(z_done, len(TILES))
                for c in range(CT):
                    act.activation(hh[:, c, 0:TP], conv[:, accp(c), 0:TP], ACT.Copy)
                    act.activation(hh[:, c, TP:T].rearrange("p (r w) -> p r w", w=GW), lat(accp(c), U1 - U0), ACT.Copy).then_inc(b_hi, 1)
                for h in range(H):
                    act.activation(hh[:, CT + h, :], hmt[:, h, :], ACT.Copy).then_inc(b_hi, 1)
            if kind == "wc":
                for m in range(4 * i, 4 * i + 4):
                    act.wait_ge(m_sum, m + 1)
                    act.activation(mh[:, m, :], mrg[:, m % 2, 0, :], ACT.Copy).then_inc(m_hi, 1)
                if i == 1:
                    act.wait_ge(ab_done, 16)
                    act.wait_ge(m_lo, KT)
                    act.wait_ge(mod_st, 16 * 16)
                    for j in range(2):
                        load_mod(act, j)
                    for t in range(NT):
                        src = a["x_prompt"][0] if t == 0 else a["x_sample"][0, (t - 1) * P:t * P, :]
                        act.dma_start(x2[:, t, :], src).then_inc(x2_in, 16)
                    act.dma_start(g2n[:, :], a["norm2_g"][0:1, :].to_broadcast([P, D])).then_inc(late_in, 16)
                    act.dma_start(gfb[:, :], a["norm_final_g"].rearrange("(o n) -> o n", o=1).to_broadcast([P, D])).then_inc(late_in, 16)
                    act.dma_start(wr[:, :, 0:NG], a["w_rg"][0].rearrange("(k p) n -> p k n", p=P)).then_inc(late_in, 16)
                    act.dma_start(wr[:, :, NG:20], a["w_re"][0].rearrange("(k p) n -> p k n", p=P)).then_inc(late_in, 16)
                    act.dma_start(rb[:, 0:NG], a["b_rg"][0:1, :].to_broadcast([P, NG])).then_inc(late_in, 16)
                    act.dma_start(rb[:, NG:20], a["b_re"][0:1, :].to_broadcast([P, NE])).then_inc(late_in, 16)
                raw_hi(g + 3)
            if (kind, i) == ("wm", 1):
                for j, dst in enumerate((bg1, bsh, bsc, bg2)):
                    for n in range(4):
                        act.wait_ge(gb_pe, 4 * j + n + 1)
                        act.activation(dst[:, n // 2, (n % 2) * 512:(n % 2 + 1) * 512], psum[:, 4 + n, :], ACT.Copy,
                                       bias=1.0 if j == 2 else 0.0).then_inc(gb_free, 1)
                    if j < 2:
                        load_mod(act, j + 2)
        for t in range(NT):
            act.wait_ge(x2_done, t + 1)
            act.activation(hsqr[:, :], x2[:, t, :], ACT.Square, accum_out=rms[:, 16 + t:17 + t]).then_inc(h2_ss, 1)
            act.wait_ge(h2_inv, t + 1)
            act.activation(rms[:, 24 + t:25 + t], rms[:, 24 + t:25 + t], ACT.Sqrt).then_inc(h2_rstd, 1)
        for t in range(NT):
            h2_out(act, t)
        for n in range(2):
            act.wait_ge(rt_x, n + 1)
            src = rexp[n]
            act.activation(src, src, ACT.Exp).then_inc(rt_exp, 1)

        def w_hi(s, j, b, c, first=False):
            g = G0 + c
            act.wait_ge(raw_in[g % NRAW], 16 * (g // NRAW + 1) + 16 * b)
            if not first and c < 2:
                act.wait_ge(gu_done, b - 1)
            elif not first:
                act.wait_ge(e_used, b - 1)
            act.activation((wh0, wh1)[s][:, c, :], raw[:, g % NRAW, :], ACT.Copy).then_inc(d_hi if c == 2 else e_hi, 1)

        def x_high(s, b, q, first=False):
            act.wait_ge(xt_done, 2 * b + q + 1)
            if not first:
                act.wait_ge(gu_done, b - 1)
            act.activation(xh[:, s, 4 * q:4 * q + 4, :], psum[:, 2 + q, :].rearrange("p (k n) -> p k n", k=4),
                           ACT.Copy).then_inc(x_hi, 1)

        def a_high(b, first=False):
            act.wait_ge(at_done, b + 1)
            if not first:
                act.wait_ge(e_used, b)
            act.activation(ah[:, :, :], psum[:, 4, 0:DE].rearrange("p (j n) -> p j n", j=2), ACT.Copy).then_inc(a_hi, 1)

        def y_left(s, j, b, first=False):
            act.wait_ge(e_used, b + 1)
            if not first:
                act.wait_ge(y_st[s], 16 * (j + FILL))
            act.activation(yy[:, s, 0:512], psum[:, 5, :], ACT.Copy).then_inc(y_act, 1)

        def store_y(s, b):
            act.wait_ge(y_act, b + 1)
            act.wait_ge(y_dve, b + 1)
            act.dma_start(y_d[bass.ds(b * CAP, CAP), :], yy[:, s, :]).then_inc(y_st[s], 16)

        act.wait_ge(wo_done, 4 * NT)
        for c in range(3):
            w_hi(0, 0, 0, c, True)
        for q in range(2):
            x_high(0, 0, q, True)
        act.wait_ge(h2_st, 16 * NT)
        act.wait_ge(y_st[0], 16 * FILL)
        act.wait_ge(y_st[1], 16 * FILL)
        pairs = pair_count(act)

        def body(j, first, last):
            for s in range(2):
                b = 2 * j + s
                start = first and s == 0
                if not start:
                    a_high(b - 1, first)
                if not (last and s == 1):
                    for q in range(2):
                        x_high(1 - s, b + 1, q, start)
                if not first:
                    store_y(s, b - 2)
                if not start:
                    w_hi(s, j, b, 2, first)
                if not (last and s == 1):
                    for c in range(2):
                        w_hi(1 - s, j + s, b + 1, c, start)
                act.wait_ge(gu_done, b + 1)
                if not start:
                    act.wait_ge(act_done, b)
                act.activation(sil[:, :], psum[:, s, 0:DE], ACT.Silu).then_inc(sil_done, 1)
                if not start:
                    y_left(1 - s, j if s else j - 1, b - 1, first)

        over_pairs(act, pairs, body)
        a_high(2 * pairs - 1)
        store_y(0, 2 * pairs - 2)
        y_left(1, pairs - 1, 2 * pairs - 1)
        store_y(1, 2 * pairs - 1)
        for t in range(NT + 1):
            if t < NT:
                act.wait_ge(yg_in[t], 32)
                act.activation(ya[:, t, :], ya[:, t, :], ACT.Copy, scale=wgt[:, t, 0:1]).then_inc(f_scaled, 1)
            if t:
                n = t - 1
                act.wait_ge(f_sum, n + 1)
                act.activation(fsq[:, :], yo[:, n, :], ACT.Square, accum_out=rms[:, n:n + 1]).then_inc(f_ss, 1)
                act.wait_ge(f_inv, n + 1)
                act.activation(rms[:, 8 + n:9 + n], rms[:, 8 + n:9 + n], ACT.Sqrt).then_inc(f_rstd, 1)
        for t in range(NT):
            act.wait_ge(f_out, t + 1)
            dst = out["y_prompt"][0] if t == 0 else out["y_sample"][0, (t - 1) * P:t * P, :]
            act.dma_start(dst, yo[:, t, :]).then_inc(f_st, 16)
        act.wait_ge(f_st, 16 * NT)
        act.wait_ge(cout_st, 32 * len(CHAINS))
        act.wait_ge(m_st, 32)

    @block.vector
    def _(dve):
        steps = [0]

        def then(ins):
            steps[0] += 1
            ins.then_inc(dve_step, 1)
            dve.wait_ge(dve_step, steps[0])

        dve.wait_ge(consts, 14)
        then(dve.tensor_tensor(sel4[:, :], ident[0:4, 0:2], ident[0:4, 2:4], ADD))
        dve.wait_ge(pe_start, 1)
        dve.tensor_copy(vcol[:, :], psum[:, 4, 0:NV])
        dve.tensor_copy(taps[:, :], psum[:, 4, 128:128 + CK * CT]).then_inc(cols_done, 1)
        dve.wait_ge(cols_done, 1)
        dve.tensor_scalar(bqs[:, :], vcol[:, V_BQ:V_BQ + CT], QS, None, MUL)
        dve.wait_ge(gate_in, GATE_IN)
        dve.tensor_tensor(gsum[:, :], gbias[:, 0:4:2], gbias[:, 1:4:2], ADD).then_inc(gsum_done, 1)
        dve.wait_ge(x_ss, NT)
        then(dve.tensor_scalar(rms[:, 8:8 + NT], rms[:, 0:NT], 1.0 / D, EPS, MUL, ADD))
        dve.reciprocal(rms[:, 8:8 + NT], rms[:, 8:8 + NT]).then_inc(x_inv, 1)
        dve.wait_ge(x_rstd, 1)
        for t in range(NT):
            dve.tensor_scalar(x5[:, t, :], x5[:, t, :], rms[:, 8 + t:9 + t], None, MUL).then_inc(x_scaled, 1)
        dve.wait_ge(cst_hi, 1)
        dve.tensor_tensor(cst[:, :, 2:4], cs[:, :].rearrange("p (v k) -> p k v", v=2), cst[:, :, 0:2].bitcast(F32),
                          SUB).then_inc(cst_lo, 1)
        dve.wait_ge(wg_hi, 4)
        for d in range(2):
            for f in range(2):
                dst = slice(64 * f + 32 * d, 64 * f + 32 * d + H)
                dve.tensor_tensor(wgl[:, :, dst], wgr[:, :, 8 * d + 4 * f:8 * d + 4 * f + H],
                                  wgh[:, :, dst].bitcast(F32), SUB).then_inc(wg_lo, 1)
        dve.wait_ge(tiny_done, 8)
        then(dve.tensor_copy(mod1[:, :, :], psum[:, 6, 0:32].rearrange("p (k v) -> p k v", v=2)))
        for v in range(2):
            then(dve.tensor_tensor(sh1[:, :, v], mod1[:, 0:KT, v], vcol[:, V_BSH:V_BSH + KT], ADD))
            then(dve.tensor_tensor(sc1[:, :, v], mod1[:, KT:2 * KT, v], vcol[:, V_BSC:V_BSC + KT], ADD))
            then(dve.scalar_tensor_tensor(out=sc1[:, :, v], in0=sc1[:, :, v], scalar=1.0, in1=vcol[:, V_G1:V_G1 + KT],
                                          op0=ADD, op1=MUL))
        dve.wait_ge(xt_free, 2 * NT)
        for k in range(KT):
            for v, cols in ((0, slice(0, TP)), (1, slice(TP, T))):
                ins = dve.tensor_scalar(xt[:, k, cols], xt[:, k, cols], sc1[:, k, v:v + 1], sh1[:, k, v:v + 1], MUL, ADD)
            ins.then_inc(h_mod, 1)
            dve.wait_ge(h_hi, k + 1)
            dve.tensor_tensor(hl[:, k, :], xt[:, k, :], hh[:, k, :].bitcast(F32), SUB).then_inc(h_lo, 1)

        def conv_input(c):
            dve.wait_ge(z_free, TILE_AT["a", c] + 1)
            dve.tensor_tensor(conv[:, c, U0:U0 + TP], at[:, c % 2, 0:TP], sgt[:, c % 2, 0:TP], MUL)
            dve.tensor_tensor(lat(c, U1), at[:, c % 2, TP:T].rearrange("p (r w) -> p r w", w=GW),
                              sgt[:, c % 2, TP:T].rearrange("p (r w) -> p r w", w=GW), MUL).then_inc(u_done, 1)

        taken = [0]

        def conv_taps(tiles, first, last):
            for c in tiles:
                for k in range(first, last):
                    acc, src = conv[:, accp(c), 0:YW], conv[:, c, k:k + YW]
                    w = taps[:, k * CT + c:k * CT + c + 1]
                    if taken[0]:
                        dve.wait_ge(conv_step, taken[0])
                    if k == 0:
                        ins = dve.tensor_scalar(acc, src, w, vcol[:, V_BDW + c:V_BDW + c + 1], MUL, ADD)
                    else:
                        ins = dve.scalar_tensor_tensor(out=acc, in0=src, scalar=w, in1=acc, op0=MUL, op1=ADD)
                    taken[0] += 1
                    ins.then_inc(conv_step, 1)

        for c in range(2):
            conv_input(c)
        dve.wait_ge(u_done, 2)
        conv_taps((0,), 0, 16)
        conv_input(2)
        conv_input(3)
        conv_taps((0,), 16, CK)
        conv_taps((1,), 0, CK)
        dve.wait_ge(z_free, TILE_AT["gate", 0] + 1)
        dve.scalar_tensor_tensor(out=gz[0:64, 2, :], in0=gz[0:64, 1, :], scalar=-1.0, in1=gz[0:64, 1, :], op0=MUL,
                                 op1=MAX).then_inc(gate_abs, 1)
        dve.wait_ge(u_done, CT)
        conv_taps((2,), 0, CK)
        dve.wait_ge(gate_ln, 1)
        dve.wait_ge(consts, 17)
        then(dve.scalar_tensor_tensor(out=gz[0:64, 1, :], in0=gz[0:64, 1, :], scalar=0.0, in1=gz[0:64, 2, :], op0=MIN,
                                      op1=SUB))
        fwd = lambda n, a0, a1: gz[0:32, n, a0:a1]
        bwd = lambda n, a0, a1: gz[32:64, n, a1 - 1:(a0 - 1 if a0 else None):-1]
        for dirn in (fwd, bwd):
            dve.tensor_tensor_scan(dirn(2, 0, T), dirn(5, 0, T), dirn(1, 0, T), 0.0, MUL, ADD)
            dve.tensor_tensor_scan(dirn(3, 0, TP), dirn(1, 0, TP), dirn(0, 0, TP), 0.0, ADD, MAX)
            start = m0[0:32, :] if dirn is fwd else m0[32:64, :]
            ins = dve.tensor_tensor_scan(dirn(3, TP, T), dirn(1, TP, T), dirn(0, TP, T), start, ADD, MAX)
        then(ins)
        dve.tensor_tensor(gz[0:64, 4, :], gz[0:64, 0, :], gz[0:64, 2, :], SUB)
        dve.memset(mprev[:, :], 0.0)
        then(dve.tensor_tensor(rrow[:, :], gz[0:64, 2, :], gz[0:64, 3, :], SUB))
        dve.tensor_copy(mprev[0:32, 1:2], m0[0:32, :])
        dve.tensor_copy(mprev[32:64, NT - 1:NT], m0[32:64, :])
        dve.tensor_copy(mprev[0:32, 2:NT], gz[0:32, 3, 2 * P - 1:T - P:P])
        dve.tensor_copy(mprev[32:64, 1:NT - 1], gz[32:64, 3, 2 * P:T:P])
        dve.tensor_copy(mend[0:32, :], gz[0:32, 3, P - 1:P])
        then(dve.tensor_copy(mend[32:64, :], gz[32:64, 3, 0:1]))
        dve.tensor_tensor(gz[0:64, 1, :].rearrange("p (t n) -> p t n", t=NT), rrow[:, :].rearrange("p (t n) -> p t n", t=NT),
                          mprev[:, :].unsqueeze(2).to_broadcast([64, NT, P]), ADD).then_inc(gate_max, 1)
        conv_taps((3,), 0, CK)
        dve.wait_ge(conv_step, taken[0])
        dve.wait_ge(gate_pe, 1)
        turned = flat[:, 4 * 512:4 * 512 + T].rearrange("p (t n) -> p t n", t=NT)
        em = psum[:, 6, 0:NT * 64].rearrange("p (t n) -> p t n", t=NT)
        for d in range(2):
            cols = slice(4 * d, 4 * d + H)
            dve.tensor_copy(tokg[:, 0, :, cols], turned[:, :, 32 * d:32 * d + H])
            dve.tensor_copy(tokg[:, 1, :, cols], turned[:, :, 64 + 32 * d:64 + 32 * d + H])
            dve.tensor_copy(tokg[:, 2, :, cols], em[:, :, 32 * d:32 * d + H])
        dve.tensor_copy(decay[:, :, :], psum[:, 7, 0:8 * NT].rearrange("p (c t) -> p c t", t=NT)).then_inc(gate_tables, 1)
        dve.wait_ge(gate_tables, 1)

        NSTEP = NT * len(CHAINS)
        where = [(ci, i, chunk_order(CHAINS[ci][1])[i]) for ci in range(len(CHAINS)) for i in range(NT)]

        def weigh(n):
            ci, i, c = where[n]
            h, d = CHAINS[ci]
            dve.wait_ge(w_done, n + 1)
            dve.wait_ge(st_free, h + 1)
            if n >= 2:
                dve.wait_ge(mm_done, n - 1)
            last = 0 if d else P - 1
            ins = dve.tensor_tensor(pt[:, n % 2, :], st[:, c * P:(c + 1) * P], wt[:, n % 2, :], MUL)
            if i < NT - 1:
                ins = dve.tensor_scalar(kw[:, n % 2, :], ktok[:, h, c, :], wt[:, n % 2, last:last + 1], None, MUL)
            ins.then_inc(p_done, 1)

        for n in range(NSTEP):
            ci, i, c = where[n]
            h, d = CHAINS[ci]
            if i == 0:
                weigh(n)
            if i < NT - 1:
                weigh(n + 1)
            dve.wait_ge(mm_done, n + 1)
            upd = psum[:, 6, 256:256 + HD + 1]
            if i == 0:
                if ci:
                    dve.wait_ge(cout_st, 32 * ci)
                dve.tensor_copy(num[:, c, :], psum[:, 6, 0:HD + 1])
                dve.tensor_copy(cout[:, :], upd).then_inc(num_done, 1)
            else:
                dve.wait_ge(t_done, (NT - 1) * ci + i)
                ins = dve.tensor_tensor(num[:, c, :], psum[:, 6, 0:HD + 1], inter[:, :], ADD)
                if i < NT - 1:
                    before = cn0[:, ci % 2, :] if i == 1 else cn[:, i % 2, :]
                    ins = dve.scalar_tensor_tensor(out=cn[:, (i + 1) % 2, :], in0=before,
                                                   scalar=decay[:, ci, c:c + 1], in1=upd, op0=MUL, op1=ADD)
                ins.then_inc(num_done, 1)
            if i == NT - 1:
                dve.wait_ge(num_done, n + 1)
                den = num[:, :, HD]
                then(dve.scalar_tensor_tensor(out=dn[:, 0, :], in0=den, scalar=-1.0, in1=den, op0=MUL, op1=MAX))
                then(dve.tensor_tensor(dn[:, 1, :], dn[:, 0, :], tokg[:, 2, :, 4 * d + h], MAX))
                then(dve.reciprocal(dn[:, 2, :], dn[:, 1, :]))
                if d == 0:
                    then(dve.tensor_tensor(hf[:, :, :], num[:, :, 0:HD], dn[:, 2, :].unsqueeze(2).to_broadcast([P, NT, HD]), MUL))
                else:
                    for t in range(NT):
                        ins = dve.scalar_tensor_tensor(out=ktok[:, h, t, :], in0=num[:, t, 0:HD], scalar=dn[:, 2, t:t + 1],
                                                       in1=hf[:, t, :], op0=MUL, op1=ADD)
                    then(ins)
        heads = ktok[:, :, :, :].rearrange("p h t n -> p (h t) n")
        dve.wait_ge(mm_done, NSTEP)
        then(dve.tensor_tensor(hsq[:, :, :], heads, heads, MUL))
        then(dve.tensor_reduce(hrs[:, 0, :], hsq[:, :, :], AX, ADD))
        then(dve.tensor_scalar(hrs[:, 0, :], hrs[:, 0, :], 1.0 / HD, EPS, MUL, ADD))
        dve.reciprocal(hrs[:, 1, :], hrs[:, 0, :]).then_inc(hn_inv, 1)
        dve.wait_ge(hn_rstd, 1)
        dve.tensor_tensor(heads, heads, hrs[:, 1, :].unsqueeze(2).to_broadcast([P, H * NT, HD]), MUL).then_inc(hn_scaled, 1)
        for h in range(H):
            dve.wait_ge(hmt_done, H)
            dve.wait_ge(z_free, TILE_AT["o", h] + 1)
            dve.tensor_tensor(hmt[:, h, :], hmt[:, h, :], sgt[:, h % 2, :], MUL).then_inc(o_done, 1)
        dve.wait_ge(ln_pe, 1)
        sums = psum[:, 4:6, 0:YW // 2]
        two = lambda t: t.rearrange("p (q n) -> p q n", q=2)
        then(dve.tensor_scalar(two(lnm[:, :]), sums, 1.0 / DI, None, MUL))
        for c in range(CT):
            dve.tensor_tensor(conv[:, accp(c), 0:YW], conv[:, accp(c), 0:YW], lnm[:, :], SUB).then_inc(ln_cent, 1)
        dve.wait_ge(ln_pe, 1 + CT)
        then(dve.tensor_scalar(two(lnr[:, :]), sums, 1.0 / DI, EPS, MUL, ADD))
        dve.reciprocal(lnr[:, :], lnr[:, :]).then_inc(ln_inv, 1)
        dve.wait_ge(ln_rstd, 1)
        for c in range(CT):
            dve.tensor_tensor(conv[:, accp(c), 0:YW], conv[:, accp(c), 0:YW], lnr[:, :], MUL).then_inc(ln_norm, 1)
        for c in range(CT):
            dve.wait_ge(b_hi, c + 1)
            dve.tensor_tensor(hl[:, c, 0:TP], conv[:, accp(c), 0:TP], hh[:, c, 0:TP].bitcast(F32), SUB)
            dve.tensor_tensor(hl[:, c, TP:T].rearrange("p (r w) -> p r w", w=GW), lat(accp(c), U1 - U0),
                              hh[:, c, TP:T].bitcast(F32).rearrange("p (r w) -> p r w", w=GW), SUB).then_inc(b_lo, 1)
        for h in range(H):
            dve.wait_ge(b_hi, CT + h + 1)
            dve.tensor_tensor(hl[:, CT + h, :], hmt[:, h, :], hh[:, CT + h, :].bitcast(F32), SUB).then_inc(b_lo, 1)
        dve.wait_ge(sga_done, 1)

        def merged_low(m):
            dve.wait_ge(m_hi, m + 1)
            dve.tensor_tensor(ml[:, m, :], mrg[:, m % 2, 0, :], mh[:, m, :].bitcast(F32), SUB).then_inc(m_lo, 1)

        for m in range(KT):
            if m >= 2:
                merged_low(m - 2)
            for br, gate in enumerate((sga, sgb)):
                n = 2 * m + br
                if m >= 2 and br == 0:
                    dve.wait_ge(m_lo, m - 1)
                dve.wait_ge(ab_done, n + 1)
                dve.tensor_tensor(two(mrg[:, m % 2, br, :]), psum[:, 2 * (n % 2):2 * (n % 2) + 2, 0:HALF],
                                  two(gate[:, m, :]), MUL).then_inc(ab_free, 1)
            dve.wait_ge(ab_free, 2 * m + 2)
            dve.tensor_tensor(mrg[:, m % 2, 0, :], mrg[:, m % 2, 0, :], mrg[:, m % 2, 1, :], ADD).then_inc(m_sum, 1)
        merged_low(KT - 2)
        merged_low(KT - 1)
        for v in range(2):
            then(dve.tensor_tensor(scol[:, v:v + 1], ident[0:5, v:v + 1], ident[0:5, v + 2:v + 3], ADD))
            then(dve.tensor_tensor(scol[:, v:v + 1], scol[:, v:v + 1], ident[0:5, 4:5], ADD))
            ins = dve.tensor_scalar(sel5[:, v, :], ones[0:5, :], scol[:, v:v + 1], None, MUL)
        ins.then_inc(gb_dve, 1)
        dve.wait_ge(gb_free, 12)
        dve.wait_ge(late_in, 16 * 6)
        for v in range(2):
            ins = dve.tensor_tensor(bsc[:, v, :], bsc[:, v, :], g2n[:, :], MUL)
        then(ins)
        then(dve.tensor_tensor_scan(iota[:, :], ones[:, :], ones[:, :], -1.0, MUL, ADD))
        then(dve.tensor_tensor(tmp[:, 0, 0:P], ident[:, :], iota[:, :], MUL))
        then(dve.tensor_reduce(tokcol[:, :], tmp[:, 0, 0:P], AX, ADD))
        then(dve.tensor_scalar(upper[:, :], iota[:, :], tokcol[:, :], None, ALU.is_gt))
        dve.wait_ge(x2_in, 16 * NT)
        def add_mixed(n):
            i, t = n // NT, n % NT
            v, cols = min(t, 1), slice(i * 256, (i + 1) * 256)
            dve.wait_ge(wo_done, n + 1)
            dve.tensor_tensor(tmp[:, n % 2, :], psum[:, n % 4, 0:256], bg1[:, v, cols], MUL).then_inc(wo_free, 1)
            dve.wait_ge(wo_free, n + 1)
            ins = dve.tensor_tensor(x2[:, t, cols], x2[:, t, cols], tmp[:, n % 2, :], ADD)
            ins.then_inc(x2_done if i == 3 else dve_step, 1)
            if i < 3:
                steps[0] += 1

        for n in range(3 * NT):
            add_mixed(n)
        for t in range(NT + 1):
            if t < NT:
                add_mixed(3 * NT + t)
            if t:
                m = t - 1
                v = min(m, 1)
                dve.wait_ge(h2_ss, m + 1)
                then(dve.tensor_scalar(rms[:, 24 + m:25 + m], rms[:, 16 + m:17 + m], 1.0 / D, EPS, MUL, ADD))
                dve.reciprocal(rms[:, 24 + m:25 + m], rms[:, 24 + m:25 + m]).then_inc(h2_inv, 1)
                dve.wait_ge(h2_rstd, m + 1)
                then(dve.scalar_tensor_tensor(out=h2[:, m, :], in0=x2[:, m, :], scalar=rms[:, 24 + m:25 + m],
                                              in1=bsc[:, v, :], op0=MUL, op1=MUL))
                dve.tensor_tensor(h2[:, m, :], h2[:, m, :], bsh[:, v, :], ADD).then_inc(h2_dve, 1)
        for t in range(NT):
            dve.wait_ge(lg_done, t + 1)
            dve.tensor_tensor(lg[:, t, :], psum[:, 4, 0:20], rb[:, :], ADD).then_inc(lg_free, 1)
        routing(dve, then)
        def w_lo(s, b, c):
            g = G0 + c
            dve.wait_ge(e_hi, 2 * b + c + 1)
            dve.tensor_tensor((wl0, wl1)[s][:, c, :], raw[:, g % NRAW, :], (wh0, wh1)[s][:, c, :].bitcast(F32),
                              SUB).then_inc(e_lo, 1)

        def x_low(s, b, q):
            dve.wait_ge(x_hi, 2 * b + q + 1)
            dve.tensor_tensor(xl[:, s, 4 * q:4 * q + 4, :], psum[:, 2 + q, :].rearrange("p (k n) -> p k n", k=4),
                              xh[:, s, 4 * q:4 * q + 4, :].bitcast(F32), SUB).then_inc(x_lo, 1)

        def a_low(b):
            dve.wait_ge(a_hi, b + 1)
            dve.tensor_tensor(al[:, :, :], psum[:, 4, 0:DE].rearrange("p (j n) -> p j n", j=2), ah[:, :, :].bitcast(F32),
                              SUB).then_inc(a_lo, 1)

        def y_right(s, j, b, first=False):
            dve.wait_ge(e_used, b + 1)
            if not first:
                dve.wait_ge(y_st[s], 16 * (j + FILL))
            dve.tensor_copy(yy[:, s, 512:D], psum[:, 6, :]).then_inc(y_dve, 1)

        w_lo(0, 0, 0)
        w_lo(0, 0, 1)
        x_low(0, 0, 0)
        x_low(0, 0, 1)
        pairs = pair_count(dve)

        def body(j, first, last):
            for s in range(2):
                b = 2 * j + s
                start = first and s == 0
                if not start:
                    a_low(b - 1)
                if not (last and s == 1):
                    for q in range(2):
                        x_low(1 - s, b + 1, q)
                    for c in range(2):
                        w_lo(1 - s, b + 1, c)
                dve.wait_ge(sil_done, b + 1)
                if not start:
                    dve.wait_ge(at_done, b)
                dve.tensor_tensor(act_[:, :], psum[:, s, DE:2 * DE], sil[:, :], MUL).then_inc(act_done, 1)
                if not start:
                    y_right(1 - s, j if s else j - 1, b - 1, first)

        over_pairs(dve, pairs, body)
        a_low(2 * pairs - 1)
        y_right(1, pairs - 1, 2 * pairs - 1)
        for t in range(NT + 1):
            if t < NT:
                v = min(t, 1)
                dve.wait_ge(f_scaled, t + 1)
                dve.scalar_tensor_tensor(out=yo[:, t, :], in0=yb[:, t, :], scalar=wgt[:, t, 1:2], in1=ya[:, t, :],
                                         op0=MUL, op1=ADD).then_inc(f_both, 1)
                dve.wait_ge(f_both, t + 1)
                dve.tensor_tensor(yo[:, t, :], yo[:, t, :], bg2[:, v, :], MUL).then_inc(f_gated, 1)
                dve.wait_ge(f_gated, t + 1)
                dve.tensor_tensor(yo[:, t, :], yo[:, t, :], x2[:, t, :], ADD).then_inc(f_sum, 1)
            if t:
                n = t - 1
                dve.wait_ge(f_ss, n + 1)
                then(dve.tensor_scalar(rms[:, 8 + n:9 + n], rms[:, n:n + 1], 1.0 / D, EPS, MUL, ADD))
                dve.reciprocal(rms[:, 8 + n:9 + n], rms[:, 8 + n:9 + n]).then_inc(f_inv, 1)
                dve.wait_ge(f_rstd, n + 1)
                dve.scalar_tensor_tensor(out=yo[:, n, :], in0=yo[:, n, :], scalar=rms[:, 8 + n:9 + n], in1=gfb[:, :],
                                         op0=MUL, op1=MUL).then_inc(f_out, 1)

    top.close()


_INS = ["x_prompt", "x_sample", "state_C", "state_n", "state_m", "c", "c_ctx", "norm1_g", "w_ada", "b_ada", "w_in", "b_in",
        "b_gates", "w_dw", "b_dw", "conv_ln_g", "conv_ln_b", "w_conv_out", "mlstm_hn_g", "w_mlstm_out", "w_o", "norm2_g",
        "w_rg", "b_rg", "w_re", "b_re", "w_e_gate", "w_e_up", "w_e_down", "norm_final_g"]
_OUTS = [("y_prompt", (1, TP, D)), ("y_sample", (1, TL, D)), ("new_C", (1, 1, 2, H, HD, HD)), ("new_n", (1, 1, 2, H, HD)),
         ("new_m", (1, 1, 2, H))]


def kernel(**inputs):
    import numpy as np
    import concourse.bacc as bacc
    from concourse.bass_utils import run_bass_kernel_spmd

    nc = bacc.Bacc("TRN2", target_bir_lowering=False, num_devices=1)
    arrays, a, out = {}, {}, {}
    for name in _INS:
        x = np.ascontiguousarray(inputs[name])
        arrays[f"in_{name}"] = x
        a[name] = nc.dram_tensor(f"in_{name}", x.shape, mybir.dt.from_np(x.dtype), kind="ExternalInput").ap()
    for name, shape in _OUTS:
        out[name] = nc.dram_tensor(f"out_{name}", shape, F32, kind="ExternalOutput").ap()
    build(nc, a, out)
    r = run_bass_kernel_spmd(nc, [arrays], core_ids=[0])
    return tuple(r.results[0][f"out_{name}"] for name, _ in _OUTS)
```

```python
from contextlib import ExitStack

import concourse.bass as bass
from concourse import mybir

P = 128
D = 1024
KT = D // P
TP, TL = 128, 512
T = TP + TL
NT = T // P
HALF = T // 2
H, HD = 4, 128
DI = H * HD
CT = DI // P
CK = 31
PADW = CK // 2
GW = 64
ROWS = TL // GW
PITCH = GW + PADW
U0 = PADW
U1 = PADW + TP + PADW
UW = U1 + ROWS * PITCH
YW = UW - 2 * PADW
NE, GE, NG = 16, 4, 4
DE = 256
CAP = P
OVER = 9
NB = NE + OVER
NS = NB + NB % 2
FILL = (NS - NE) // 2
CH = 2048
RING = 4
NRAW_ADA = 8
EPS = 1e-6
QS = HD ** -0.5
NEG = -1e30

F32, F32R, BF16, I32 = mybir.dt.float32, mybir.dt.float32r, mybir.dt.bfloat16, mybir.dt.int32
ALU = mybir.AluOpType
ACT = mybir.ActivationFunctionType
AX = mybir.AxisListType.X
MUL, ADD, SUB, MAX, MIN = ALU.mult, ALU.add, ALU.subtract, ALU.max, ALU.min

V_CTX, V_C, V_G1, V_BSH, V_BSC, V_BA, V_BGA, V_BQ, V_BK, V_BV, V_BO, V_BMA, V_BMB, V_BDW, V_LG, V_LB, V_HN, NV = (
    0, 8, 16, 24, 32, 40, 44, 48, 52, 56, 60, 64, 72, 80, 84, 88, 92, 96)

C_A, C_GA, C_Q, C_K, C_V, C_O, C_IF = 0, 512, 1024, 1536, 2048, 2560, 3072
C_MA, C_MB = C_IF + 16, C_IF + 16 + D


def units():
    u = [("ada", 4 * (n % 2) + n // 2) for n in range(NRAW_ADA)]
    ada = iter(range(8, 24))

    def z(kind, n, with_ada=True):
        for i in range(n):
            u.append((kind, i))
            if with_ada and kind not in ("gmb",) or (with_ada and i < 2):
                k = next(ada, None)
                if k is not None:
                    u.append(("ada", k))

    for i in range(2):
        u.append(("ga", i))
        u.append(("a", i))
        u.append(("ada", next(ada)))
    for kind, n in (("v", 2), ("k", 2), ("q", 2), ("gma", 4), ("o", 2)):
        z(kind, n)
    for i in range(4):
        u.append(("gmb", i))
        k = next(ada, None)
        if k is not None:
            u.append(("ada", k))
    u += [("wc", 0), ("wm", 0), ("wc", 1), ("wm", 1)]
    u += [("wo", i) for i in range(4)]
    return u


UNITS = units()
G0 = len(UNITS)
WCOL = {"a": C_A, "ga": C_GA, "q": C_Q, "k": C_K, "v": C_V, "o": C_O, "gma": C_MA, "gmb": C_MB}
ZKINDS = tuple(WCOL)


def psum_tiles():
    out, by_unit = [], []
    for kind, i in UNITS:
        mine = []
        if kind == "ada":
            mine = [("ada", i)]
        elif kind in ZKINDS:
            mine = [(kind, 2 * i), (kind, 2 * i + 1)]
            if kind == "v" and i == 0:
                mine = [("gate", 0)] + mine
        by_unit.append([(len(out) + n, *m) for n, m in enumerate(mine)])
        out += mine
    return out, by_unit


INPUT_AT = {2: (0, 1), 3: (2, 3), 4: (4,)}
TILES, TILES_OF = psum_tiles()
TILE_AT = {m: n for n, m in enumerate(TILES)}
UNIT_AT = {m: n for n, m in enumerate(UNITS)}


def chunk_order(first):
    return [0, 1, 2, 3, 4] if first == 0 else [0, 4, 3, 2, 1]


def build(nc, a, out):
    top = ExitStack()
    block_stack = ExitStack()

    def sem(name):
        return top.enter_context(nc.semaphore(name))

    def keep(name, shape, dt=F32):
        return top.enter_context(nc.sbuf_tensor(name, shape, dt))

    mod_d = nc.dram_tensor("mod_d", [4, 4 * D], F32, kind="Internal").ap()
    h2_d = nc.dram_tensor("h2_d", [T, D], F32, kind="Internal").ap()
    mod2_d = nc.dram_tensor("mod2_d", [2, 4 * D], F32, kind="Internal").ap()
    y_d = nc.dram_tensor("y_d", [NS * CAP, D], F32, kind="Internal").ap()

    ident = keep("ident", [P, P])
    identb = keep("identb", [P, P], BF16)
    ones = keep("ones", [P, P])
    onesb = keep("onesb", [P, P], BF16)
    mask = keep("mask", [P, 2, P], BF16)
    vcol = keep("vcol", [P, NV])
    taps = keep("taps", [P, CK * CT])
    cs = keep("cs", [P, 16])
    cst = keep("cst", [P, KT, 4], F32R)
    modrow = keep("modrow", [4, 256])
    sh1 = keep("sh1", [P, KT, 2])
    sc1 = keep("sc1", [P, KT, 2])
    gbias = keep("gbias", [64, 4])
    m0 = keep("m0", [64, 1])
    rms = keep("rms", [P, 32])
    bqs = keep("bqs", [P, CT])
    lgs = keep("lgs", [P, CT])

    K = 1024
    spans = []

    def place(name, at, shape, dt=F32):
        with ExitStack() as s:
            if at:
                s.enter_context(nc.sbuf_tensor(f"gap_{name}", [P, int(at)], mybir.dt.uint8))
            t = s.enter_context(nc.sbuf_tensor(name, shape, dt))
        return t

    w_h = place("w_h", 138 * K, [P, RING, CH], F32R)
    w_l = place("w_l", 170 * K, [P, RING, CH], F32R)
    w_raw = place("w_raw", 170 * K, [P, RING, CH])

    hh = place("hh", 0, [P, KT, T], F32R)
    hl = place("hl", 20 * K, [P, KT, T], F32R)
    qt = place("qt", 40 * K, [P, H, T])
    kt = place("kt", 50 * K, [P, H, T])
    ktok = place("ktok", 60 * K, [P, H, NT, HD])
    VT0 = 70 * K
    vtok = place("vtok", VT0, [P, H, NT, HD + 1])
    SG0 = 80 * K + 256
    sga = place("sga", SG0, [P, KT, T])
    CV0 = 100 * K + 256
    conv = place("conv", CV0, [P, 6, UW + 2])
    SM0 = 119 * K
    rrow = place("rrow", SM0, [64, T])
    tokg = place("tokg", SM0 + 2560, [P, 3, NT, 8])
    decay = place("decay", SM0 + 3072, [P, 8, NT])
    wt = place("wt", SM0 + 3328, [P, 2, P])
    pt = place("pt", SM0 + 4352, [P, 2, P])
    kw = place("kw", SM0 + 5376, [P, 2, P])
    st = place("st", SM0 + 6400, [P, T])
    cn = place("cn", SM0 + 8960, [P, 2, HD + 1])
    inter = place("inter", SM0 + 8960 + 1056, [P, HD + 1])
    num = place("num", SM0 + 8960 + 1056 + 544, [P, NT, HD + 1])
    dn = place("dn", SM0 + 8960 + 1056 + 544 + 2592, [P, 3, NT])
    cn0 = place("cn0", SM0 + 13248, [P, 2, HD + 1])
    cout = place("cout", SM0 + 13248 + 1056, [P, HD + 1])
    gsum = place("gsum", SM0 + 13248 + 1056 + 544, [64, 2])
    mprev = place("mprev", SM0 + 13248 + 1056 + 576, [64, NT])
    mend = place("mend", SM0 + 13248 + 1056 + 608, [64, 1])
    hf = place("hf", 134 * K, [P, NT, HD])
    lnm = place("lnm", SM0, [P, YW])
    lnr = place("lnr", SM0 + 3072, [P, YW])
    lsq = place("lsq", SM0 + 6144, [P, 2, YW])
    hsq = place("hsq", 50 * K, [P, H * NT, HD])
    hrs = place("hrs", SM0 + 12288, [P, 3, H * NT])
    junk = place("junk", SG0, [P, NT, D])
    x5 = place("x5", 40 * K, [P, NT, D])
    vrow = place("vrow", 60 * K, [NV, P])
    drow = place("drow", 61 * K, [CK * CT, P])
    wgr = place("wgr", 62 * K, [P, KT, 16])
    wgh = place("wgh", 63 * K, [P, KT, P], F32R)
    wgl = place("wgl", 67 * K, [P, KT, P], F32R)
    xt = place("xt", SG0, [P, KT, T])
    sgt = place("sgt", 40 * K, [P, 2, T])
    at = place("at", 45 * K, [P, 2, T])
    vt = place("vt", SG0, [P, 2, T])
    gz = place("gz", SG0 + 5 * K, [P, 6, T])
    sgb = place("sgb", 40 * K, [P, KT, T])
    hmt = place("hmt", VT0, [P, H, T])
    ml = place("ml", 40 * K, [P, KT, T], F32R)
    mh = place("mh", SG0, [P, KT, T], F32R)
    mrg = place("mrg", SM0, [P, 2, 2, T])
    x2 = place("x2", 0, [P, NT, D])
    mrow = place("mrow", 137 * K, [P, 4, 4 * D // P])
    mbias = place("mbias", 137 * K + 512, [P, 4 * D // P])
    mg2 = place("mg2", 137 * K + 640, [P, 4 * D // P])
    tmp = place("tmp", 125 * K + 256, [P, 2, 256])
    lgt = place("lgt", 127 * K + 256, [20, NT, P])
    bg1 = place("bg1", 60 * K, [P, 2, D])
    bsh = place("bsh", 68 * K, [P, 2, D])
    bsc = place("bsc", CV0, [P, 2, D])
    R0 = CV0 + 8 * K
    lg = place("lg", R0, [P, NT, 20])
    wr = place("wr", R0 + 512, [P, KT, 20])
    rb = place("rb", R0 + 1536, [P, 20])
    iota = place("iota", R0 + 2 * K, [P, P])
    upper = place("upper", R0 + 2560, [P, P], BF16)
    wgt = place("wgt", R0 + 3 * K, [P, NT, 2])
    row_i = place("row_i", R0 + 3 * K + 64, [P, NT, 2], I32)
    slot_i = place("slot_i", R0 + 3 * K + 128, [P, NS], I32)
    expert_i = place("expert_i", R0 + 4 * K + 640, [P, NS], I32)
    pairs_i = place("pairs_i", R0 + 4 * K + 768, [P, 1], I32)
    h2t = place("h2t", 130 * K, [P, 2, KT, P])
    r1 = place("r1", 48 * K, [P, 20, NT * NE])
    oa = place("oa", 56 * K, [P, 2, NT, P], BF16)
    ob = place("ob", 59 * K, [P, 2, NT, 2, NS], BF16)
    obh = place("obh", 62 * K, [P, 2, NT, NS])
    orow = place("orow", 64 * K, [P, NS - NE, NE])
    picks = place("picks", 65 * K, [P, NT, NE], BF16)
    h2 = place("h2", 20 * K, [P, NT, D])
    tokcol = place("tokcol", R0 + 4 * K + 576, [P, 1])
    down_h = place("down_h", 20 * K, [P, 2, CH], F32R)
    down_l = [place("down_l0", 130 * K, [P, 1, CH], F32R), place("down_l1", 36 * K, [P, 1, CH], F32R)]
    down_raw = [place("down_raw0", 130 * K, [P, 1, CH]), place("down_raw1", 36 * K, [P, 1, CH])]
    xh = place("xh", 68 * K, [P, 2, KT, P], F32R)
    xl = place("xl", 76 * K, [P, 2, KT, P], F32R)
    xg = place("xg", 84 * K, [P, 2, D])
    yy = place("yy", 92 * K, [P, 2, D])
    sil = place("sil", CV0, [P, DE])
    act_ = place("act", CV0 + K, [P, DE])
    slot_b = place("slot_b", CV0 + 4 * K, [P, 2], I32)
    ah = place("ah", CV0 + 2 * K, [P, 2, P], F32R)
    al = place("al", CV0 + 3 * K, [P, 2, P], F32R)
    tick = place("tick", CV0 + 4 * K + 64, [P, 3], I32)
    bg2 = place("bg2", R0 + 5 * K, [P, 2, D])
    gfb = place("gfb", R0 + 13 * K, [P, D])
    ya = place("ya", 20 * K, [P, NT, D])
    yb = place("yb", 40 * K, [P, NT, D])
    yo = place("yo", 60 * K, [P, NT, D])
    fsq = place("fsq", 84 * K, [P, D])
    hsqr = place("hsqr", 76 * K, [P, D])
    plane = lambda n, w: r1[:, n, 0:NT * w].rearrange("p (t w) -> p t w", w=w)
    rexp = [plane(0, NG), plane(1, 1)]

    psum = top.enter_context(nc.psum_tensor("psum", [P, 8, 512], F32))
    flat = psum[:, :, :].rearrange("p b n -> p (b n)")

    x_in, vec_in, gw_in, late_in = sem("x_in"), sem("vec_in"), sem("gw_in"), sem("late_in")
    state_in = [sem(f"state_in{i}") for i in range(2)]
    raw_in = [sem(f"raw_in{i}") for i in range(RING)]
    consts = sem("consts")
    late_consts = sem("late_consts")
    down_in = [sem(f"down_in{i}") for i in range(2)]
    hi_done = sem("hi_done")
    lo_done = sem("lo_done")
    z_done = sem("z_done")
    z_free = sem("z_free")
    act_step = sem("act_step")
    dve_step = sem("dve_step")
    pe_start, cols_done = sem("pe_start"), sem("cols_done")
    x_ss, x_inv, x_rstd, x_scaled = sem("x_ss"), sem("x_inv"), sem("x_rstd"), sem("x_scaled")
    xt_turned, xt_free = sem("xt_turned"), sem("xt_free")
    cs_done, cst_hi, cst_lo = sem("cs_done"), sem("cst_hi"), sem("cst_lo")
    gate_in, wg_hi, wg_lo = sem("gate_in"), sem("wg_hi"), sem("wg_lo")
    tiny_done = sem("tiny_done")
    mod_st = sem("mod_st")
    h_hi, h_lo = sem("h_hi"), sem("h_lo")
    h_mod = sem("h_mod")
    u_done = sem("u_done")
    turn_done, turn_free = sem("turn_done"), sem("turn_free")
    gsum_done = sem("gsum_done")
    gate_abs, gate_ln, gate_max = sem("gate_abs"), sem("gate_ln"), sem("gate_max")
    gate_rows, gate_pe, gate_tables = sem("gate_rows"), sem("gate_pe"), sem("gate_tables")
    r_done = sem("r_done")
    st_done, st_free = sem("st_done"), sem("st_free")
    w_done = sem("w_done")
    p_done = sem("p_done")
    mm_done = sem("mm_done")
    t_done = sem("t_done")
    num_done = sem("num_done")
    cout_st, m_st = sem("cout_st"), sem("m_st")
    hn_inv, hn_rstd, hn_scaled, hn_pe, hmt_done = (
        sem(n) for n in ("hn_inv", "hn_rstd", "hn_scaled", "hn_pe", "hmt_done"))
    o_done = sem("o_done")
    conv_step, ln_pe, ln_cent, ln_sq, ln_inv, ln_rstd, ln_norm, ln_y = (
        sem(n) for n in ("conv_step", "ln_pe", "ln_cent", "ln_sq", "ln_inv", "ln_rstd", "ln_norm", "ln_y"))
    sga_done = sem("sga_done")
    b_hi, b_lo = sem("b_hi"), sem("b_lo")
    ab_done, ab_free = sem("ab_done"), sem("ab_free")
    m_sum, m_hi, m_lo = sem("m_sum"), sem("m_hi"), sem("m_lo")
    mrow_in, mrow_done, mod2_st = sem("mrow_in"), sem("mrow_done"), sem("mod2_st")
    mod_in, gate2_in = sem("mod_in"), sem("gate2_in")
    lgt_pe, lgt_done = sem("lgt_pe"), sem("lgt_done")
    x2_in, x2_done = sem("x2_in"), sem("x2_done")
    wo_done, wo_free = sem("wo_done"), sem("wo_free")
    h2_ss, h2_inv, h2_rstd, h2_dve, h2_pe, h2_ev, lg_done, lg_free = (
        sem(n) for n in ("h2_ss", "h2_inv", "h2_rstd", "h2_dve", "h2_pe", "h2_ev", "lg_done", "lg_free"))
    h2_st = sem("h2_st")
    rt_x, rt_exp, rt_pe = sem("rt_x"), sem("rt_exp"), sem("rt_pe")
    picked, hots, tables = sem("picked"), sem("hots"), sem("tables")
    e_hi, e_lo, d_hi, d_lo, e_used = (sem(n) for n in ("e_hi", "e_lo", "d_hi", "d_lo", "e_used"))
    slot_set = sem("slot_set")
    xg_in = [sem(f"xg_in{i}") for i in range(2)]
    xt_done, x_hi, x_lo = sem("xt_done"), sem("x_hi"), sem("x_lo")
    gu_done, sil_done, act_done, at_done, a_hi, a_lo, dn_done = (
        sem(n) for n in ("gu_done", "sil_done", "act_done", "at_done", "a_hi", "a_lo", "dn_done"))
    y_act, y_dve = sem("y_act"), sem("y_dve")
    y_st = [sem(f"y_st{i}") for i in range(2)]
    yg_in = [sem(f"yg_in{i}") for i in range(NT)]
    f_scaled, f_both, f_gated, f_sum, f_ss, f_inv, f_rstd, f_out = (
        sem(n) for n in ("f_scaled", "f_both", "f_gated", "f_sum", "f_ss", "f_inv", "f_rstd", "f_out"))
    f_st = sem("f_st")

    VROWS = [(V_CTX, a["c_ctx"]), (V_C, a["c"][0]), (V_G1, a["norm1_g"][0]),
             (V_BSH, a["b_ada"][0, 0:2 * D]), (V_BA, a["b_in"][0, C_A:C_Q]), (V_BQ, a["b_in"][0, C_Q:C_IF]),
             (V_BMA, a["b_in"][0, C_MA:C_MB + D]), (V_BDW, a["b_dw"][0]), (V_LG, a["conv_ln_g"][0]),
             (V_LB, a["conv_ln_b"][0]), (V_HN, a["mlstm_hn_g"][0])]

    def wsrc(kind, i):
        if kind == "ada":
            return a["w_ada"][0, :, i * 256:(i + 1) * 256].rearrange("(k p) n -> p k n", p=P)
        if kind in WCOL:
            c = WCOL[kind] + i * 256
            return a["w_in"][0, :, c:c + 256].rearrange("(k p) n -> p k n", p=P)
        if kind in ("wc", "wm"):
            w = a["w_conv_out" if kind == "wc" else "w_mlstm_out"]
            return w[0, :, i * 512:(i + 1) * 512].rearrange("(k p) n -> p k n", p=P)
        return a["w_o"][0, :, i * 256:(i + 1) * 256].rearrange("(k p) n -> p k n", p=P)

    def chunk(t, slot, rows):
        return t[:, slot, :].rearrange("p (k n) -> p k n", k=rows)

    def lat(plane, width):
        return conv[:, plane, width:width + ROWS * PITCH].rearrange("p (r w) -> p r w", w=PITCH)[:, :, 0:GW]

    def accp(c):
        return (4, 5, 0, 1)[c]

    CHAINS = [(h, d) for h in range(H) for d in range(2)]
    hooks = {}
    def raw_landed(eng, g):
        eng.wait_ge(raw_in[g % RING], 16 * (g // RING + 1))

    VEC_IN = 16 * (len(VROWS) + 1)
    GATE_IN = 16 * 8 + 32

    def chunk_used(eng, g):
        kind, i = UNITS[g]
        if TILES_OF[g]:
            eng.wait_ge(z_done, TILES_OF[g][-1][0] + 1)
        elif kind in ("wc", "wm"):
            eng.wait_ge(ab_done, 8 * (i + 1))
        else:
            eng.wait_ge(wo_done, NT * (i + 1))

    def split_matmuls(pe, dst, pairs):
        n = 3 * len(pairs)
        k = 0
        for lh, ll, rh, rl in pairs:
            for left, right in ((lh, rh), (lh, rl), (ll, rh)):
                mm = pe.matmul(dst, left, right, start=(k == 0), stop=(k == n - 1))
                k += 1
        return mm

    def load_mod(eng, j, dst, landed):
        for v in range(2):
            eng.dma_start(dst[:, v, :], mod2_d[v:v + 1, j * D:(j + 1) * D].to_broadcast([P, D])).then_inc(landed, 16)

    def h2_out(act, t):
        act.wait_ge(h2_dve, t + 1)
        act.dma_start(h2_d[t * P:(t + 1) * P, :], h2[:, t, :]).then_inc(h2_st, 16)
        for n in range(t, NS - NE, NT):
            act.dma_start(y_d[(NE + n) * CAP:(NE + n + 1) * CAP, :], h2[:, t, :]).then_inc(y_st[n % 2], 16)
        if t >= 2:
            act.wait_ge(lgt_pe, t - 1)
        for q in range(2):
            act.wait_ge(h2_pe, 2 * t + q + 1)
            act.activation(h2t[:, t % 2, 4 * q:4 * q + 4, :],
                           psum[:, 5 + q, :].rearrange("p (k n) -> p k n", k=4), ACT.Copy).then_inc(h2_ev, 1)

    def logits_out(act, t):
        act.wait_ge(lgt_pe, t + 1)
        act.activation(lgt[:, t, :], psum[0:20, 4, 0:P], ACT.Copy).then_inc(lgt_done, 1)

    def routing(dve, then):
        four = lambda n: r1[:, n, 0:80].rearrange("p (t g e) -> p t g e", t=NT, g=NG)
        full = lambda n: r1[:, n, 0:80].rearrange("p (t e) -> p t e", t=NT)
        col = lambda n: r1[:, n, 0:NT]
        over = lambda ap, w: ap.unsqueeze(2).to_broadcast([P, NT, w])
        desc = r1[:, 19, 0:NG]
        then(dve.tensor_scalar(desc, iota[:, 0:NG], -1.0, float(NG), MUL, ADD))

        def first_max(src, top, hot, t1, t2):
            then(dve.tensor_reduce(top, src, AX, MAX))
            then(dve.tensor_tensor(t1, src, over(top, NG), ALU.is_ge))
            then(dve.tensor_tensor(t1, t1, desc.unsqueeze(1).to_broadcast([P, NT, NG]), MUL))
            then(dve.tensor_reduce(t2, t1, AX, MAX))
            then(dve.tensor_tensor(hot, t1, over(t2, NG), ALU.is_equal))

        gl, el = lg[:, :, 0:NG], lg[:, :, NG:20].rearrange("p t (g e) -> p t g e", g=NG)
        first_max(gl, col(2), plane(3, NG), plane(4, NG), col(5))
        dve.tensor_tensor(rexp[0], gl, over(col(2), NG), SUB).then_inc(rt_x, 1)
        then(dve.tensor_tensor(four(6), el, plane(3, NG).unsqueeze(3).to_broadcast([P, NT, NG, GE]), MUL))
        then(dve.tensor_reduce(plane(7, GE), four(6).rearrange("p t g e -> p t e g"), AX, ADD))
        first_max(plane(7, GE), col(8), plane(9, GE), plane(4, GE), col(5))
        then(dve.scalar_tensor_tensor(out=plane(10, GE), in0=plane(9, GE), scalar=NEG, in1=plane(7, GE), op0=MUL, op1=ADD))
        first_max(plane(10, GE), col(11), plane(12, GE), plane(4, GE), col(5))
        dve.tensor_tensor(r1[:, 1, 0:NT], col(11), col(8), SUB).then_inc(rt_x, 1)
        for n, hot in ((13, 9), (14, 12)):
            then(dve.tensor_tensor(four(n), plane(3, NG).unsqueeze(3).to_broadcast([P, NT, NG, GE]),
                                   plane(hot, GE).unsqueeze(2).to_broadcast([P, NT, NG, GE]), MUL))
        dve.tensor_tensor(picks[:, :, :], full(13), full(14), ADD).then_inc(picked, 1)
        dve.wait_ge(rt_pe, 1)
        rf = r1[:, :, :].rearrange("p a b -> p (a b)")
        W = NT * NE
        pc, qc = rf[:, 6 * W:7 * W + NE], rf[:, 8 * W:9 * W + NE]
        tok = lambda ap: ap[:, 0:W].rearrange("p (t e) -> p t e", t=NT)
        pos, q, ov = tok(pc), tok(qc), qc[:, W:W + NE]
        incl, base, blk, place_in = r1[:, 10, 0:NE], r1[:, 10, NE:2 * NE], full(11), full(12)
        then(dve.tensor_copy(pc, psum[:, 5, 0:W + NE]))
        then(dve.tensor_scalar(pc[:, W:W + NE], pc[:, W:W + NE], -1.0, None, ADD))
        then(dve.tensor_scalar(qc, pc, float(CAP), None, ALU.is_ge))
        for k in range(2, -(-T // CAP)):
            then(dve.scalar_tensor_tensor(out=qc, in0=pc, scalar=float(k * CAP), in1=qc, op0=ALU.is_ge, op1=ADD))
        then(dve.tensor_tensor_scan(incl, ones[:, 0:NE], ov, 0.0, MUL, ADD))
        then(dve.tensor_tensor(base, incl, ov, SUB))
        then(dve.scalar_tensor_tensor(out=base, in0=base, scalar=float(NE - 1), in1=iota[:, 0:NE], op0=ADD, op1=SUB))
        wide = lambda ap: ap.unsqueeze(1).to_broadcast([P, NT, NE])
        then(dve.tensor_tensor(blk, q, wide(base), ADD))
        then(dve.scalar_tensor_tensor(out=blk, in0=q, scalar=0.0, in1=blk, op0=ALU.is_gt, op1=MUL))
        then(dve.tensor_tensor(blk, blk, wide(iota[:, 0:NE]), ADD))
        then(dve.scalar_tensor_tensor(out=place_in, in0=q, scalar=-float(CAP), in1=pos, op0=MUL, op1=ADD))
        hots2 = r1[:, 13:15, :].rearrange("p i (t e) -> p i t e", t=NT)
        prod = r1[:, 15:17, :].rearrange("p i (t e) -> p i t e", t=NT)
        both = lambda ap: ap.unsqueeze(1).to_broadcast([P, 2, NT, NE])
        pair_of = lambda n: r1[:, n, 0:2 * NT].rearrange("p (i t) -> p i t", i=2)
        then(dve.tensor_tensor(prod, hots2, both(blk), MUL))
        then(dve.tensor_reduce(pair_of(2), prod, AX, ADD))
        then(dve.tensor_tensor(prod, hots2, both(place_in), MUL))
        then(dve.tensor_reduce(pair_of(4), prod, AX, ADD))
        flat2 = lambda n, w: r1[:, n, 0:2 * NT].unsqueeze(2).to_broadcast([P, 2 * NT, w])
        dve.tensor_tensor(oa[:, :, :, :].rearrange("p i t n -> p (i t) n"), iota[:, :].unsqueeze(1).to_broadcast([P, 2 * NT, P]),
                          flat2(4, P), ALU.is_equal)
        then(dve.tensor_tensor(obh[:, :, :, :].rearrange("p i t n -> p (i t) n"),
                               iota[:, 0:NS].unsqueeze(1).to_broadcast([P, 2 * NT, NS]), flat2(2, NS), ALU.is_equal))
        dve.tensor_scalar(ob[:, :, :, 0, :], obh[:, :, :, :], tokcol[:, :], None, MUL)
        for i in range(2):
            ins = dve.tensor_tensor(ob[:, i, :, 1, :], obh[:, i, :, :], over(iota[:, 0:NT], NS), MUL)
        ins.then_inc(hots, 1)
        then(dve.scalar_tensor_tensor(out=pair_of(6), in0=pair_of(2), scalar=float(CAP), in1=pair_of(4), op0=MUL, op1=ADD))
        dve.tensor_copy(row_i[:, :, :].rearrange("p t i -> p i t"), pair_of(6))
        dve.wait_ge(rt_exp, 2)
        then(dve.tensor_reduce(col(7), rexp[0], AX, ADD))
        then(dve.reciprocal(col(7), col(7)))
        then(dve.tensor_scalar(col(8), r1[:, 1, 0:NT], 1.0, None, ADD))
        then(dve.reciprocal(col(8), col(8)))
        then(dve.tensor_tensor(wgt[:, :, 0], col(7), col(8), MUL))
        then(dve.tensor_tensor(wgt[:, :, 1], wgt[:, :, 0], r1[:, 1, 0:NT], MUL))
        over_e = r1[:, 17, 0:NS - NE]
        then(dve.tensor_tensor(orow[:, :, :], iota[:, 0:NS - NE].unsqueeze(2).to_broadcast([P, NS - NE, NE]),
                               incl.unsqueeze(1).to_broadcast([P, NS - NE, NE]), ALU.is_ge))
        then(dve.tensor_reduce(over_e, orow[:, :, :], AX, ADD))
        then(dve.tensor_scalar(over_e, over_e, float(NE - 1), None, MIN))
        dve.tensor_copy(expert_i[:, 0:NE], iota[:, 0:NE])
        dve.tensor_copy(expert_i[:, NE:NS], over_e)
        odds, pairs = r1[:, 18, 0:(NS - NE) // 2], r1[:, 18, 8:9]
        then(dve.tensor_scalar(odds, iota[:, 0:NS - NE:2], incl[:, NE - 1:NE], None, ALU.is_lt))
        then(dve.tensor_reduce(pairs, odds, AX, ADD))
        dve.tensor_copy(pairs_i[:, :], pairs)
        dve.wait_ge(rt_pe, 2)
        then(dve.tensor_copy(r1[:, 16, 0:2 * NS], psum[:, 6, 0:2 * NS]))
        then(dve.scalar_tensor_tensor(out=r1[:, 17, 0:NS], in0=r1[:, 16, NS:2 * NS], scalar=float(P), in1=r1[:, 16, 0:NS],
                                      op0=MUL, op1=ADD))
        dve.tensor_copy(slot_i[:, :], r1[:, 17, 0:NS]).then_inc(tables, 1)

    def pair_count(eng):
        eng.wait_ge(tables, 1)
        return eng.value_load(pairs_i[0:1, 0:1], min_val=0, max_val=(NS - NE) // 2) + NE // 2

    def over_pairs(eng, pairs, body):
        body(0, True, False)
        with eng.Fori(1, pairs - 1) as j:
            body(j, False, False)
        body(pairs - 1, False, True)

    def experts_pool(pool):
        for c in range(2):
            pool.wait_ge(e_hi, c + 1)
            pool.tensor_tensor(w_l[:, c, :], w_raw[:, c, :], w_h[:, c, :].bitcast(F32), SUB).then_inc(e_lo, 1)
        pool.wait_ge(h2_st, 16 * NT)
        pairs = pair_count(pool)

        def carry(n, ap):
            pool.tensor_tensor(tick[:, n:n + 1], ap, ap, ADD)

        def gather(j, s, count):
            pool.tensor_copy(slot_b[:, s:s + 1], slot_i[:, bass.ds(count, 1)]).then_inc(slot_set, 1)
            pool.wait_ge(slot_set, count + 1)
            carry(0, slot_b[:, s:s + 1])
            pool.indirect_dma_start(out=xg[:, s, :], out_offset=None, in_=h2_d,
                                    in_offset=bass.IndirectOffsetOnAxis(ap=slot_b[:, s:s + 1], axis=0),
                                    bounds_check=T - 1).then_inc(xg_in[s], 16)

        def body(j, first, last):
            for s in range(2):
                b = 2 * j + s
                if not last:
                    pool.wait_ge(xt_done, 2 * b + 2)
                    carry(1, slot_i[:, 0:1])
                    gather(j + 1, s, b + 2)
                pool.wait_ge(d_hi, b + 1)
                pool.tensor_tensor(down_l[s][:, 0, :], down_raw[s][:, 0, :], down_h[:, s, :].bitcast(F32),
                                   SUB).then_inc(d_lo, 1)

        gather(0, 0, 0)
        gather(0, 1, 1)
        over_pairs(pool, pairs, body)
        for i in range(2):
            pool.wait_ge(y_st[i], 16 * (pairs + FILL))
        carry(2, row_i[:, 0, 0:1])
        for t in range(NT):
            for i, buf in enumerate((ya, yb)):
                pool.indirect_dma_start(out=buf[:, t, :], out_offset=None, in_=y_d,
                                        in_offset=bass.IndirectOffsetOnAxis(ap=row_i[:, t, i:i + 1], axis=0),
                                        bounds_check=NS * CAP - 1).then_inc(yg_in[t], 16)
        for t in range(NT):
            pool.wait_ge(f_gated, t + 1)
            pool.tensor_tensor(yo[:, t, :], yo[:, t, :], x2[:, t, :], ADD).then_inc(f_sum, 1)

    block = top.enter_context(nc.Block())

    @block.sync
    def _(sp):
        for g, (kind, i) in enumerate(UNITS):
            if g >= RING:
                chunk_used(sp, g - RING)
            src = wsrc(kind, i)
            sp.dma_start(chunk(w_raw, g % RING, src.shape[1]), src).then_inc(raw_in[g % RING], 16)
        def gate_up(s, b, pick, first):
            for c, name in enumerate(("w_e_gate", "w_e_up")):
                slot = 2 * s + c
                if first:
                    chunk_used(sp, G0 - RING + slot)
                else:
                    sp.wait_ge(gu_done, b - 1)
                sp.dma_start(chunk(w_raw, slot, KT), pick(a[name])).then_inc(raw_in[slot], 16)

        def down_weights(s, b, pick, first):
            if not first:
                sp.wait_ge(e_used, b - 1)
            sp.dma_start(chunk(down_raw[s], 0, 2), pick(a["w_e_down"])).then_inc(down_in[s], 16)

        def own(b):
            return lambda w: w[0, b, :, :].rearrange("(k p) n -> p k n", p=P)

        def by_table(b):
            e = sp.value_load(expert_i[0:1, bass.ds(b, 1)], min_val=0, max_val=NE - 1)
            return lambda w: w[0, bass.ds(e, 1), :, :].rearrange("a (k p) n -> p (a k) n", p=P)

        for b in range(2):
            gate_up(b, b, own(b), True)
        pairs = pair_count(sp)
        sp.wait_ge(h2_st, 16 * NT)
        sp.wait_ge(y_st[0], 16 * FILL)
        sp.wait_ge(y_st[1], 16 * FILL)
        down_weights(0, 0, own(0), True)
        gate_up(0, 2, own(2), False)
        down_weights(1, 1, own(1), True)
        gate_up(1, 3, own(3), False)
        down_weights(0, 2, own(2), False)
        with sp.Fori(2, pairs) as j:
            for s in range(2):
                b = 2 * j + s
                gate_up(s, b, by_table(b), False)
                down_weights(1 - s, b - 1, by_table(b - 1), False)
        down_weights(1, 2 * pairs - 1, by_table(2 * pairs - 1), False)

    @block.gpsimd
    def _(pool):
        def diagonal(t):
            pool.affine_select(out=t[:, :], in_=t[:, :], compare_op=ALU.not_equal, fill=1.0, base=0,
                               pattern=[[-1, P]], channel_multiplier=1).then_inc(consts, 1)

        pool.memset(ident[:, :], 0.0).then_inc(consts, 1)
        pool.wait_ge(consts, 1)
        diagonal(ident)
        pool.memset(gbias[:, :], 0.0).then_inc(consts, 1)
        pool.memset(m0[:, :], 0.0).then_inc(consts, 1)
        pool.memset(wgh[:, :, :].bitcast(F32), 0.0).then_inc(consts, 1)
        pool.memset(wgl[:, :, :].bitcast(F32), 0.0).then_inc(consts, 1)
        pool.memset(ones[:, :], 1.0).then_inc(consts, 1)
        pool.memset(onesb[:, :], 1.0).then_inc(consts, 1)
        pool.memset(identb[:, :], 0.0).then_inc(consts, 1)
        pool.memset(mask[:, :, :], 0.0).then_inc(consts, 1)
        pool.memset(conv[:, :, :], 0.0).then_inc(consts, 1)
        pool.wait_ge(consts, 11)
        diagonal(identb)
        pool.affine_select(out=mask[:, 0, :], in_=mask[:, 0, :], compare_op=ALU.is_ge, fill=NEG, base=0,
                           pattern=[[1, P]], channel_multiplier=-1).then_inc(consts, 1)
        pool.affine_select(out=mask[:, 1, :], in_=mask[:, 1, :], compare_op=ALU.is_ge, fill=NEG, base=0,
                           pattern=[[-1, P]], channel_multiplier=1).then_inc(consts, 1)
        for g in range(NRAW_ADA, G0):
            if g == UNIT_AT["v", 0] - 1:
                pool.wait_ge(h_lo, KT)
                pool.memset(gz[0:64, 5, :], 1.0).then_inc(consts, 1)
                pool.wait_ge(consts, 15)
                pool.memset(gz[0:32, 5, 0:T:P], 0.0).then_inc(consts, 1)
                pool.memset(gz[32:64, 5, P - 1:T:P], 0.0).then_inc(consts, 1)
                pool.wait_ge(consts, 17)
            pool.wait_ge(hi_done, g - NRAW_ADA + 1)
            pool.tensor_tensor(w_l[:, g % RING, :], w_raw[:, g % RING, :], w_h[:, g % RING, :].bitcast(F32),
                               SUB).then_inc(lo_done, 1)
        experts_pool(pool)

    @block.tensor
    def _(pe):
        def turn(dst, src, n=P):
            return pe.transpose(dst, src, ident[0:n, 0:n])

        pe.wait_ge(consts, 2)
        pe.wait_ge(vec_in, VEC_IN)
        turn(psum[:, 4, 0:NV], vrow[:, :], NV)
        turn(psum[:, 4, 128:128 + CK * CT], drow[:, :], CK * CT).then_inc(pe_start, 1)
        pe.wait_ge(cs_done, 1)

        def turn_input(t):
            pe.wait_ge(x_scaled, t + 1)
            for q in range(2):
                n = 2 * t + q
                if n >= 2:
                    pe.wait_ge(xt_free, n - 1)
                for k in range(4):
                    mm = turn(psum[:, 1 + 2 * (n % 2), k * P:(k + 1) * P], x5[:, t, (4 * q + k) * P:(4 * q + k + 1) * P])
                mm.then_inc(xt_turned, 1)

        def tiny(g):
            pe.wait_ge(z_free, g + 1)
            for j in range(2):
                at = 4 * (g % 2) + 2 * j
                mm = pe.matmul(psum[:, 4 + g // 2, at:at + 2], modrow[0:2, j * P:(j + 1) * P], ident[0:2, 0:2],
                               start=True, stop=True)
            mm.then_inc(tiny_done, 1)

        def open_tile(tile):
            if tile >= 2:
                pe.wait_ge(z_free, tile - 1)
            return 2 * (tile % 2)

        def gemm(tile, wh, wl, hook=None):
            p = open_tile(tile)
            for k in range(KT):
                pe.wait_ge(h_lo, k + 1)
                for x, (w, r) in enumerate(((wh(k), hh), (wh(k), hl), (wl(k), hh))):
                    for q in range(2):
                        mm = pe.matmul(psum[:, p + q, 0:HALF], w, r[:, k, q * HALF:(q + 1) * HALF],
                                       start=(k == 0 and x == 0), stop=(k == KT - 1 and x == 2))
                if hook:
                    hook(k)
            mm.then_inc(z_done, 1)

        def turn_tokens(kind, h):
            pe.wait_ge(z_free, TILE_AT[kind, h] + 1)
            n = h if kind == "v" else H + h
            if n:
                pe.wait_ge(turn_free, n)
            src = vt[:, h % 2, :] if kind == "v" else kt[:, h, :]
            for t in range(NT):
                mm = turn(flat[:, 4 * 512 + t * P:4 * 512 + (t + 1) * P], src[:, t * P:(t + 1) * P])
            mm.then_inc(turn_done, 1)

        def gates_turn():
            pe.wait_ge(gate_rows, 1)
            pe.wait_ge(turn_free, 2 * H)
            for t in range(NT):
                turn(flat[:, 4 * 512 + t * P:4 * 512 + (t + 1) * P], gz[:, 4, t * P:(t + 1) * P])
            for t in range(NT):
                turn(psum[:, 6, t * 64:(t + 1) * 64], gz[0:64, 3, t * P:(t + 1) * P], 64)
            for ci, (h, d) in enumerate(CHAINS):
                col = 64 + 32 * d + h
                mm = pe.matmul(psum[:, 7, ci * NT:(ci + 1) * NT], ident[64:128, col:col + 1].to_broadcast([64, P]),
                               gz[64:128, 4, (0 if d else P - 1):T:P], start=True, stop=True)
            mm.then_inc(gate_pe, 1)

        def exponents(ci):
            h, d = CHAINS[ci]
            if ci:
                pe.wait_ge(w_done, NT * ci)
            row = ident[0:64, 32 * d + h:32 * d + h + 1].to_broadcast([64, P])
            pe.matmul(psum[:, 4, :], row, rrow[:, P:T], start=True, stop=False)
            pe.matmul(psum[:, 4, :], identb[:, :], mask[:, d:d + 1, :].to_broadcast([P, 4, P]), start=False, stop=True)
            pe.matmul(psum[:, 5, 0:P], row, rrow[:, 0:P], start=True, stop=False)
            pe.matmul(psum[:, 5, 0:P], identb[:, :], mask[:, d, :], start=False, stop=True).then_inc(r_done, 1)

        def scores(ci):
            h, _ = CHAINS[ci]
            if ci:
                pe.wait_ge(num_done, NT * ci)
            for t in range(NT):
                mm = pe.matmul(flat[:, 6 * 512 + t * P:6 * 512 + (t + 1) * P], kt[:, h, t * P:(t + 1) * P],
                               qt[:, h, t * P:(t + 1) * P], start=True, stop=True)
            mm.then_inc(st_done, 1)

        def step(ci, i):
            h, d = CHAINS[ci]
            n = NT * ci + i
            c = chunk_order(d)[i]
            pe.wait_ge(p_done, n + 1)
            if n:
                pe.wait_ge(num_done, n)
            mm = pe.matmul(psum[:, 6, 0:HD + 1], pt[:, n % 2, :], vtok[:, h, c, :], start=True, stop=True)
            if i < NT - 1:
                mm = pe.matmul(psum[:, 6, 256:256 + HD + 1], kw[:, n % 2, :], vtok[:, h, c, :], start=True, stop=True)
            if i:
                if i == 1:
                    pe.wait_ge(state_in[ci % 2], 32 * (ci // 2 + 1))
                state = cn0[:, ci % 2, :] if i == 1 else cn[:, i % 2, :]
                mm = pe.matmul(psum[:, 7, 0:HD + 1], qt[:, h, c * P:(c + 1) * P], state, start=True, stop=True)
            mm.then_inc(mm_done, 1)

        def chain_hook(ci):
            def run(k):
                if k == 0:
                    exponents(ci)
                    if ci:
                        step(ci - 1, NT - 1)
                elif k == 1 and CHAINS[ci][1] == 0:
                    scores(ci)
                elif k in STEP_AT:
                    step(ci, STEP_AT.index(k))
                if k == KT - 1 and ci == len(CHAINS) - 1:
                    step(ci, NT - 1)
            return run

        def heads_turn():
            pe.wait_ge(hn_scaled, 1)
            pe.wait_ge(num_done, NT * len(CHAINS))
            for h in range(H):
                if h:
                    pe.wait_ge(hmt_done, h)
                for t in range(NT):
                    mm = turn(flat[:, 6 * 512 + t * P:6 * 512 + (t + 1) * P], ktok[:, h, t, :])
                mm.then_inc(hn_pe, 1)

        def channel_sums(n):
            for c in range(CT):
                if n == 0:
                    pe.wait_ge(conv_step, CK * CT)
                    src = conv[:, accp(c), 0:YW]
                else:
                    pe.wait_ge(ln_sq, c + 1)
                    src = lsq[:, c % 2, :]
                for q in range(2):
                    mm = pe.matmul(psum[:, 4 + q, 0:YW // 2], ones[:, :], src[:, q * (YW // 2):(q + 1) * (YW // 2)],
                                   start=(c == 0), stop=(c == CT - 1))
                if n == 1:
                    mm.then_inc(ln_pe, 1)
            if n == 0:
                mm.then_inc(ln_pe, 1)

        STEP_AT = (2, 3, 5, 6)
        for g, (kind, i) in enumerate(UNITS):
            if kind in ("wc", "wm", "wo"):
                continue
            if g < NRAW_ADA:
                p = open_tile(g)
                raw_landed(pe, g)
                for k in range(KT):
                    mm = pe.matmul(psum[0:2, p, 0:256], cs[:, k:16:KT], w_raw[:, g % RING, k * 256:(k + 1) * 256],
                                   start=(k == 0), stop=(k == KT - 1))
                mm.then_inc(z_done, 1)
                if g:
                    tiny(g - 1)
                for t in INPUT_AT.get(g, ()):
                    turn_input(t)
                if g == NRAW_ADA - 1:
                    tiny(g)
                    pe.wait_ge(xt_free, 2 * NT)
                    pe.wait_ge(cst_lo, 1)
                continue
            pe.wait_ge(lo_done, g - NRAW_ADA + 1)
            hi, lo = w_h[:, g % RING, :], w_l[:, g % RING, :]
            if kind == "v" and i == 0:
                pe.wait_ge(wg_lo, 4)
                gemm(TILE_AT["gate", 0], lambda k: wgh[:, k, :], lambda k: wgl[:, k, :])
            if kind == "ada":
                tile = TILE_AT[kind, i]
                p = open_tile(tile)
                for k in range(KT):
                    for j, w in enumerate((hi, lo)):
                        mm = pe.matmul(psum[0:4, p, 0:256], cst[:, k, :], w[:, k * 256:(k + 1) * 256],
                                       start=(k == 0 and j == 0), stop=(k == KT - 1 and j == 1))
                mm.then_inc(z_done, 1)
            else:
                for j in range(2):
                    n = 2 * i + j
                    hook = chain_hook(n) if kind == "gma" else None
                    if kind == "gma" and n == 0:
                        gates_turn()
                        pe.wait_ge(gate_tables, 1)
                    w = lambda t: (lambda k: t[:, k * 256 + j * P:k * 256 + (j + 1) * P])
                    gemm(TILE_AT[kind, n], w(hi), w(lo), hook)
                    if kind in ("v", "k") and n:
                        turn_tokens(kind, n - 1)
                    if (kind, n) == ("k", 0):
                        turn_tokens("v", H - 1)
                    if (kind, n) == ("q", 0):
                        turn_tokens("k", H - 1)
                    if (kind, n) == ("o", 1):
                        heads_turn()
                    if (kind, n) == ("o", 3):
                        channel_sums(0)
                    if (kind, n) == ("gmb", 1):
                        channel_sums(1)

        for half in range(2):
            g = UNIT_AT["wc", half]
            pe.wait_ge(lo_done, g - NRAW_ADA + 2)
            for m in range(4):
                for br in range(2):
                    n = 8 * half + 2 * m + br
                    if n >= 2:
                        pe.wait_ge(ab_free, n - 1)
                    else:
                        pe.wait_ge(z_free, len(TILES))
                    p = 2 * (n % 2)
                    slot = (g + br) % RING
                    for k in range(4):
                        if half == 0 and m == 0:
                            pe.wait_ge(b_lo, 4 * br + k + 1)
                        cols = slice(k * 512 + m * P, k * 512 + (m + 1) * P)
                        hi, lo = w_h[:, slot, cols], w_l[:, slot, cols]
                        for x, (w, r) in enumerate(((hi, hh), (hi, hl), (lo, hh))):
                            for q in range(2):
                                mm = pe.matmul(psum[:, p + q, 0:HALF], w, r[:, 4 * br + k, q * HALF:(q + 1) * HALF],
                                               start=(k == 0 and x == 0), stop=(k == 3 and x == 2))
                    mm.then_inc(ab_done, 1)

        def route(t):
            pe.wait_ge(h2_dve, t + 1)
            for q in range(2):
                if t:
                    pe.wait_ge(h2_ev, 2 * t + q - 1)
                for k in range(4):
                    mm = turn(psum[:, 5 + q, k * P:(k + 1) * P], h2[:, t, (4 * q + k) * P:(4 * q + k + 1) * P])
                mm.then_inc(h2_pe, 1)
            pe.wait_ge(h2_ev, 2 * t + 2)
            pe.wait_ge(late_in, 16 * 5)
            if t:
                pe.wait_ge(lgt_done, t)
            for k in range(KT):
                mm = pe.matmul(psum[0:20, 4, 0:P], wr[:, k, :], h2t[:, t % 2, k, :], start=(k == 0), stop=(k == KT - 1))
            mm.then_inc(lgt_pe, 1)

        for i in range(4):
            g = UNIT_AT["wo", i]
            pe.wait_ge(lo_done, g - NRAW_ADA + 1)
            for t in range(NT):
                n = NT * i + t
                if n >= 4:
                    pe.wait_ge(wo_free, n - 3)
                elif n < 2:
                    pe.wait_ge(ab_free, 16)
                for k in range(KT):
                    if i == 0 and t == 0:
                        pe.wait_ge(m_lo, k + 1)
                    l_hi, l_lo = mh[:, k, t * P:(t + 1) * P], ml[:, k, t * P:(t + 1) * P]
                    w_hi, w_lo = (w[:, g % RING, k * 256:(k + 1) * 256] for w in (w_h, w_l))
                    for x, (l, r) in enumerate(((l_hi, w_hi), (l_hi, w_lo), (l_lo, w_hi))):
                        mm = pe.matmul(psum[:, n % 4, 0:256], l, r, start=(k == 0 and x == 0),
                                       stop=(k == KT - 1 and x == 2))
                mm.then_inc(wo_done, 1)
                if i == 3 and t >= 2:
                    route(t - 2)
        route(NT - 2)
        route(NT - 1)
        pe.wait_ge(lgt_done, NT)
        for t in range(NT):
            mm = turn(psum[:, 7, t * 20:(t + 1) * 20], lgt[:, t, :], 20)
        mm.then_inc(lg_done, 1)
        pe.wait_ge(picked, 1)
        for t in range(NT):
            for s in range(t):
                pe.matmul(psum[:, 5, t * NE:(t + 1) * NE], onesb[:, :], picks[:, s, :], start=(s == 0), stop=False)
            pe.matmul(psum[:, 5, t * NE:(t + 1) * NE], upper[:, :], picks[:, t, :], start=(t == 0), stop=True)
        for t in range(NT):
            mm = pe.matmul(psum[:, 5, NT * NE:(NT + 1) * NE], onesb[:, :], picks[:, t, :], start=(t == 0),
                           stop=(t == NT - 1))
        mm.then_inc(rt_pe, 1)
        pe.wait_ge(hots, 1)
        for n in range(2 * NT):
            mm = pe.matmul(psum[:, 6, 0:2 * NS], oa[:, n // NT, n % NT, :], ob[:, n // NT, n % NT, :, :],
                           start=(n == 0), stop=(n == 2 * NT - 1))
        mm.then_inc(rt_pe, 1)

        def turn_x(j, s, b):
            pe.wait_ge(xg_in[s], 16 * j + 16)
            for q in range(2):
                if not (isinstance(b, int) and b == 0):
                    pe.wait_ge(x_lo, 2 * b + q - 1)
                for k in range(4):
                    mm = turn(psum[:, 2 + q, k * P:(k + 1) * P], xg[:, s, (4 * q + k) * P:(4 * q + k + 1) * P])
                mm.then_inc(xt_done, 1)

        def turn_act(b, first=False):
            pe.wait_ge(act_done, b + 1)
            if not first:
                pe.wait_ge(a_lo, b)
            for j in range(2):
                mm = turn(psum[:, 4, j * P:(j + 1) * P], act_[:, j * P:(j + 1) * P])
            mm.then_inc(at_done, 1)

        def down(s, b, first=False):
            wh, wl = down_h[:, s, :], down_l[s][:, 0, :]
            pe.wait_ge(a_lo, b + 1)
            pe.wait_ge(d_lo, b + 1)
            if not first:
                pe.wait_ge(y_act, b)
                pe.wait_ge(y_dve, b)
            for q in range(2):
                cols = lambda w, j: w[:, j * D + q * 512:j * D + (q + 1) * 512]
                mm = split_matmuls(pe, psum[:, 5 + q, :],
                                   [(ah[:, j, :], al[:, j, :], cols(wh, j), cols(wl, j)) for j in range(2)])
            mm.then_inc(e_used, 1)

        turn_x(0, 0, 0)
        pairs = pair_count(pe)

        def body(j, first, last):
            for s in range(2):
                b = 2 * j + s
                start = first and s == 0
                if not start:
                    turn_act(b - 1, first and s == 1)
                if not (last and s == 1):
                    turn_x(j + s, 1 - s, b + 1)
                wh, wl = w_h[:, 2 * s:2 * s + 2, :], w_l[:, 2 * s:2 * s + 2, :]
                pe.wait_ge(e_lo, 2 * b + 2)
                pe.wait_ge(x_lo, 2 * b + 2)
                both = lambda w, k: w[:, :, k * DE:(k + 1) * DE]
                split_matmuls(pe, psum[:, s, :], [(xh[:, s, k, :], xl[:, s, k, :], both(wh, k), both(wl, k))
                                                  for k in range(KT)]).then_inc(gu_done, 1)
                if not start:
                    down(1 - s, b - 1, first and s == 1)

        over_pairs(pe, pairs, body)
        turn_act(2 * pairs - 1)
        down(1, 2 * pairs - 1)

    @block.scalar
    def _(act):
        def raw_hi(g):
            raw_landed(act, g)
            act.activation(w_h[:, g % RING, :], w_raw[:, g % RING, :], ACT.Copy).then_inc(hi_done, 1)

        pair = lambda tile, rows=slice(0, P): psum[rows, 2 * (tile % 2):2 * (tile % 2) + 2, 0:HALF]
        halves = lambda ap: ap.rearrange("p (q n) -> p q n", q=2)

        for row, src in VROWS:
            n = src.shape[0] // P
            act.dma_start(vrow[row:row + n, :], src.rearrange("(r p) -> r p", p=P)).then_inc(vec_in, 16)
        act.dma_start(drow[:, :], a["w_dw"][0].rearrange("k (c p) -> (k c) p", p=P)).then_inc(vec_in, 16)
        act.dma_start(wgr[:, :, :], a["w_in"][0, :, C_IF:C_MA].rearrange("(k p) n -> p k n", p=P)).then_inc(gw_in, 16)
        for t in range(NT):
            src = a["x_prompt"][0] if t == 0 else a["x_sample"][0, (t - 1) * P:t * P, :]
            act.dma_start(x5[:, t, :], src).then_inc(x_in, 16)
        act.wait_ge(cols_done, 1)
        act.activation(cs[:, :], vcol[:, 0:16], ACT.Silu).then_inc(cs_done, 1)
        act.wait_ge(cs_done, 1)
        act.activation(cst[:, :, 0:2], cs[:, :].rearrange("p (v k) -> p k v", v=2), ACT.Copy).then_inc(cst_hi, 1)
        act.wait_ge(consts, 6)
        for d in range(2):
            for f in range(2):
                rows = slice(32 * d, 32 * d + H)
                c = C_IF + 8 * d + 4 * f
                act.dma_start(gbias[rows, 2 * f:2 * f + 1], a["b_in"][0, c:c + H].rearrange("(h o) -> h o", o=1)).then_inc(gate_in, 16)
                act.dma_start(gbias[rows, 2 * f + 1:2 * f + 2], a["b_gates"][0, d, f].rearrange("(h o) -> h o", o=1)).then_inc(gate_in, 16)
            act.dma_start(m0[rows, :], a["state_m"][0, 0, d].rearrange("(h o) -> h o", o=1)).then_inc(gate_in, 16)
        act.wait_ge(x_in, 16 * NT)
        for t in range(NT):
            act.activation(junk[:, t, :], x5[:, t, :], ACT.Square, accum_out=rms[:, t:t + 1]).then_inc(x_ss, 1)
        act.wait_ge(x_inv, 1)
        act.activation(rms[:, 8:8 + NT], rms[:, 8:8 + NT], ACT.Sqrt).then_inc(x_rstd, 1)
        act.wait_ge(gw_in, 16)
        for d in range(2):
            for f in range(2):
                act.activation(wgh[:, :, 64 * f + 32 * d:64 * f + 32 * d + H], wgr[:, :, 8 * d + 4 * f:8 * d + 4 * f + H],
                               ACT.Copy).then_inc(wg_hi, 1)

        def input_turned(t):
            for q in range(2):
                n = 2 * t + q
                act.wait_ge(xt_turned, n + 1)
                act.activation(xt[:, 4 * q:4 * q + 4, t * P:(t + 1) * P],
                               psum[:, 1 + 2 * (n % 2), :].rearrange("p (k n) -> p k n", k=4), ACT.Copy).then_inc(xt_free, 1)

        def load_state(ci):
            h, d = CHAINS[ci]
            if ci >= 2:
                act.wait_ge(num_done, NT * (ci - 2) + 2)
            act.dma_start(cn0[:, ci % 2, 0:HD], a["state_C"][0, 0, d, h]).then_inc(state_in[ci % 2], 16)
            act.dma_start(cn0[:, ci % 2, HD:HD + 1], a["state_n"][0, 0, d, h].rearrange("(p o) -> p o", o=1)).then_inc(state_in[ci % 2], 16)

        def turned(kind, h):
            n = h if kind == "v" else H + h
            act.wait_ge(turn_done, n + 1)
            src = flat[:, 4 * 512:4 * 512 + T].rearrange("p (t n) -> p t n", t=NT)
            dst = vtok[:, h, :, 0:HD] if kind == "v" else ktok[:, h, :, :]
            act.activation(dst, src, ACT.Copy).then_inc(turn_free, 1)

        def gates():
            act.wait_ge(gate_abs, 1)
            act.activation(gz[0:64, 2, :], gz[0:64, 2, :], ACT.Exp, scale=-1.0).then_inc(act_step, 1)
            act.wait_ge(act_step, 1)
            act.activation(gz[0:64, 2, :], gz[0:64, 2, :], ACT.Ln, bias=1.0).then_inc(gate_ln, 1)

        def gates2():
            act.wait_ge(gate_max, 1)
            for d in range(2):
                act.dma_start(out["new_m"][0, 0, d].rearrange("(h o) -> h o", o=1),
                              mend[32 * d:32 * d + H, :]).then_inc(m_st, 16)
            act.activation(gz[64:128, 4, :], gz[0:64, 1, :], ACT.Exp)
            act.activation(gz[0:64, 3, :], gz[0:64, 3, :], ACT.Exp, scale=-1.0).then_inc(gate_rows, 1)

        def state_share(ci, i):
            h, d = CHAINS[ci]
            n, c, col = NT * ci + i, chunk_order(d)[i], 4 * d + h
            act.wait_ge(mm_done, n + 1)
            act.wait_ge(num_done, n)
            if i == 1:
                act.dma_start(out["new_C"][0, 0, d, h], cout[:, 0:HD]).then_inc(cout_st, 16)
                act.dma_start(out["new_n"][0, 0, d, h].rearrange("(p o) -> p o", o=1),
                              cout[:, HD:HD + 1]).then_inc(cout_st, 16)
            act.activation(inter[:, :], psum[:, 7, 0:HD + 1], ACT.Copy,
                           scale=tokg[:, 1, c, col:col + 1]).then_inc(t_done, 1)

        def chain(ci):
            h, d = CHAINS[ci]
            order = chunk_order(d)
            col = 4 * d + h

            def weights(i):
                n, c = NT * ci + i, order[i]
                if n >= 2:
                    act.wait_ge(p_done, n - 1)
                src = psum[:, 4, (c - 1) * P:c * P] if c else psum[:, 5, 0:P]
                act.activation(wt[:, n % 2, :], src, ACT.Exp, bias=tokg[:, 0, c, col:col + 1]).then_inc(w_done, 1)

            if ci + 1 < len(CHAINS):
                load_state(ci + 1)
            if ci:
                state_share(ci - 1, NT - 1)
            act.wait_ge(r_done, ci + 1)
            weights(0)
            weights(1)
            if d == 0:
                act.wait_ge(st_done, h + 1)
                if h:
                    act.wait_ge(p_done, 2 * NT * h)
                act.activation(st[:, :], flat[:, 6 * 512:6 * 512 + T], ACT.Copy).then_inc(st_free, 1)
            for i in range(NT - 1):
                if i:
                    state_share(ci, i)
                if i + 2 < NT:
                    weights(i + 2)
            if ci == len(CHAINS) - 1:
                state_share(ci, NT - 1)

        def evacuate(tile, kind, i):
            if kind == "gma":
                if i == 0:
                    load_state(0)
                    act.wait_ge(gate_tables, 1)
                chain(i)
            act.wait_ge(z_done, tile + 1)
            bias = lambda base: vcol[:, base + i:base + i + 1]

            def z(dst, func, base, **more):
                act.activation(halves(dst), pair(tile), func, bias=bias(base), **more).then_inc(z_free, 1)

            if kind == "ada":
                if 1 <= tile <= NRAW_ADA:
                    act.wait_ge(tiny_done, tile)
                if i > NRAW_ADA:
                    act.wait_ge(mod_st, 16 * (i - NRAW_ADA))
                rows = slice(0, 2 if i < NRAW_ADA else 4)
                act.activation(modrow[rows, :], psum[rows, 2 * (tile % 2), 0:256], ACT.Copy).then_inc(z_free, 1)
                if i >= 8:
                    act.wait_ge(z_free, tile + 1)
                    act.dma_start(mod_d[:, (i - 8) * 256:(i - 7) * 256], modrow[:, :]).then_inc(mod_st, 16)
            elif kind == "ga":
                if i >= 2:
                    act.wait_ge(u_done, i - 1)
                z(sgt[:, i % 2, :], ACT.Sigmoid, V_BGA)
            elif kind == "a":
                z(at[:, i % 2, :], ACT.Identity, V_BA)
            elif kind == "gate":
                act.wait_ge(h_lo, KT)
                act.wait_ge(gsum_done, 1)
                act.activation(halves(gz[0:64, 0, :]), pair(tile, slice(0, 64)), ACT.Identity, bias=gsum[:, 0:1])
                act.activation(halves(gz[0:64, 1, :]), pair(tile, slice(64, P)), ACT.Identity,
                               bias=gsum[:, 1:2]).then_inc(z_free, 1)
                act.activation(vtok[:, :, :, HD], ones[:, 0:H * NT].rearrange("p (h t) -> p h t", h=H), ACT.Copy)
            elif kind == "v":
                if i >= 2:
                    act.wait_ge(turn_done, i - 1)
                z(vt[:, i % 2, :], ACT.Identity, V_BV)
                if i:
                    turned("v", i - 1)
            elif kind == "k":
                z(kt[:, i, :], ACT.Identity, V_BK)
                turned("k", i - 1) if i else turned("v", H - 1)
                if i == 0:
                    gates()
            elif kind == "q":
                act.wait_ge(u_done, CT)
                act.activation(halves(qt[:, i, :]), pair(tile), ACT.Identity, bias=bqs[:, i:i + 1],
                               scale=QS).then_inc(z_free, 1)
                if i == 0:
                    turned("k", H - 1)
                    gates2()
            elif kind == "gma":
                z(sga[:, i, :], ACT.Identity, V_BMA)
            elif kind == "o":
                if i >= 2:
                    act.wait_ge(o_done, i - 1)
                z(sgt[:, i % 2, :], ACT.Sigmoid, V_BO)
                if i == 1:
                    act.wait_ge(hn_inv, 1)
                    act.activation(hrs[:, 1, :], hrs[:, 1, :], ACT.Sqrt).then_inc(hn_rstd, 1)
                    for h in range(H):
                        act.wait_ge(hn_pe, h + 1)
                        act.activation(hmt[:, h, :], flat[:, 6 * 512:6 * 512 + T], ACT.Copy,
                                       scale=vcol[:, V_HN + h:V_HN + h + 1]).then_inc(hmt_done, 1)
                if i == 3:
                    act.activation(sga[:, :, :], sga[:, :, :], ACT.Sigmoid).then_inc(sga_done, 1)
            elif kind == "gmb":
                act.wait_ge(o_done, H)
                z(sgb[:, i, :], ACT.Sigmoid, V_BMB)
                if i == 0:
                    act.wait_ge(ln_cent, CT)
                    for c in range(CT):
                        if c >= 2:
                            act.wait_ge(ln_pe, c)
                        act.activation(lsq[:, c % 2, :], conv[:, accp(c), 0:YW], ACT.Square).then_inc(ln_sq, 1)
                if i == 3:
                    act.wait_ge(ln_inv, 1)
                    act.activation(lnr[:, :], lnr[:, :], ACT.Sqrt).then_inc(ln_rstd, 1)
                    for c in range(CT):
                        act.wait_ge(ln_norm, c + 1)
                        act.activation(conv[:, accp(c), 0:YW], conv[:, accp(c), 0:YW], ACT.Silu,
                                       bias=vcol[:, V_LB + c:V_LB + c + 1], scale=vcol[:, V_LG + c:V_LG + c + 1]).then_inc(ln_y, 1)

        for g, (kind, i) in enumerate(UNITS):
            if NRAW_ADA <= g + 2 < G0 and kind != "wm":
                raw_hi(g + 2)
            for tile, k, n in TILES_OF[g]:
                evacuate(tile, k, n)
            for t in INPUT_AT.get(g, ()):
                input_turned(t)
            if NRAW_ADA // 2 <= g < NRAW_ADA:
                for k in range(2 * g - NRAW_ADA, 2 * g - NRAW_ADA + 2):
                    act.wait_ge(h_mod, k + 1)
                    act.activation(hh[:, k, :], xt[:, k, :], ACT.Copy).then_inc(h_hi, 1)
            if (kind, i) == ("wc", 0):
                act.wait_ge(mod_st, 16 * 16)
                act.dma_start(mrow[:, :, :], mod_d.rearrange("v (p c) -> p v c", p=P)).then_inc(mrow_in, 16)
                act.dma_start(mbias[:, :], a["b_ada"][0, 2 * D:6 * D].rearrange("(p c) -> p c", p=P)).then_inc(mrow_in, 16)
                act.dma_start(mg2[64:96, :], a["norm2_g"][0].rearrange("(p c) -> p c", p=32)).then_inc(mrow_in, 16)
                act.wait_ge(ln_y, CT)
                act.wait_ge(o_done, H)
                act.wait_ge(z_done, len(TILES))
                for c in range(CT):
                    act.activation(hh[:, c, 0:TP], conv[:, accp(c), 0:TP], ACT.Copy)
                    act.activation(hh[:, c, TP:T].rearrange("p (r w) -> p r w", w=GW), lat(accp(c), U1 - U0), ACT.Copy).then_inc(b_hi, 1)
                for h in range(H):
                    act.activation(hh[:, CT + h, :], hmt[:, h, :], ACT.Copy).then_inc(b_hi, 1)
            if kind == "wc":
                raw_hi(g + 3)
            if (kind, i) == ("wc", 0):
                act.wait_ge(mrow_done, 1)
                act.dma_start(mod2_d.rearrange("v (p c) -> p v c", p=P), mrow[:, 0:2, :]).then_inc(mod2_st, 16)
                act.wait_ge(mod2_st, 16)
                act.wait_ge(b_lo, 8)
                for j, dst in enumerate((bg1, bsh, bsc)):
                    load_mod(act, j, dst, mod_in)
            if kind == "wc":
                for m in range(4 * i, 4 * i + 4):
                    act.wait_ge(m_sum, m + 1)
                    act.activation(mh[:, m, :], mrg[:, m % 2, 0, :], ACT.Copy).then_inc(m_hi, 1)
                if i == 1:
                    act.wait_ge(ab_done, 16)
                    act.wait_ge(m_lo, KT)
                    load_mod(act, 3, bg2, gate2_in)
                    for t in range(NT):
                        src = a["x_prompt"][0] if t == 0 else a["x_sample"][0, (t - 1) * P:t * P, :]
                        act.dma_start(x2[:, t, :], src).then_inc(x2_in, 16)
                    act.dma_start(gfb[:, :], a["norm_final_g"].rearrange("(o n) -> o n", o=1).to_broadcast([P, D])).then_inc(late_in, 16)
                    act.dma_start(wr[:, :, 0:NG], a["w_rg"][0].rearrange("(k p) n -> p k n", p=P)).then_inc(late_in, 16)
                    act.dma_start(wr[:, :, NG:20], a["w_re"][0].rearrange("(k p) n -> p k n", p=P)).then_inc(late_in, 16)
                    act.dma_start(rb[:, 0:NG], a["b_rg"][0:1, :].to_broadcast([P, NG])).then_inc(late_in, 16)
                    act.dma_start(rb[:, NG:20], a["b_re"][0:1, :].to_broadcast([P, NE])).then_inc(late_in, 16)
        def w_hi(s, j, c):
            if c == 2:
                act.wait_ge(down_in[s], 16 * j + 16)
                act.activation(down_h[:, s, :], down_raw[s][:, 0, :], ACT.Copy).then_inc(d_hi, 1)
            else:
                g = G0 + 2 * s + c
                act.wait_ge(raw_in[g % RING], 16 * (g // RING + 1) + 16 * j)
                act.activation(w_h[:, 2 * s + c, :], w_raw[:, 2 * s + c, :], ACT.Copy).then_inc(e_hi, 1)

        for t in range(NT + 2):
            if t < 2:
                w_hi(0, 0, t)
            else:
                if t >= 3:
                    logits_out(act, t - 3)
                h2_out(act, t - 2)
            if t < NT:
                act.wait_ge(x2_done, t + 1)
                act.activation(hsqr[:, :], x2[:, t, :], ACT.Square, accum_out=rms[:, 16 + t:17 + t]).then_inc(h2_ss, 1)
                act.wait_ge(h2_inv, t + 1)
                act.activation(rms[:, 24 + t:25 + t], rms[:, 24 + t:25 + t], ACT.Sqrt).then_inc(h2_rstd, 1)
        logits_out(act, NT - 1)
        for n in range(2):
            act.wait_ge(rt_x, n + 1)
            src = rexp[n]
            act.activation(src, src, ACT.Exp).then_inc(rt_exp, 1)

        def x_high(s, b, q, first=False):
            act.wait_ge(xt_done, 2 * b + q + 1)
            if not first:
                act.wait_ge(gu_done, b - 1)
            act.activation(xh[:, s, 4 * q:4 * q + 4, :], psum[:, 2 + q, :].rearrange("p (k n) -> p k n", k=4),
                           ACT.Copy).then_inc(x_hi, 1)

        def a_high(b, first=False):
            act.wait_ge(at_done, b + 1)
            if not first:
                act.wait_ge(e_used, b)
            act.activation(ah[:, :, :], psum[:, 4, 0:DE].rearrange("p (j n) -> p j n", j=2), ACT.Copy).then_inc(a_hi, 1)

        def y_left(s, j, b, first=False):
            act.wait_ge(e_used, b + 1)
            if not first:
                act.wait_ge(y_st[s], 16 * (j + FILL))
            act.activation(yy[:, s, 0:512], psum[:, 5, :], ACT.Copy).then_inc(y_act, 1)

        def store_y(s, b):
            act.wait_ge(y_act, b + 1)
            act.wait_ge(y_dve, b + 1)
            act.dma_start(y_d[bass.ds(b * CAP, CAP), :], yy[:, s, :]).then_inc(y_st[s], 16)

        for q in range(2):
            x_high(0, 0, q, True)
        act.wait_ge(h2_st, 16 * NT)
        act.wait_ge(y_st[0], 16 * FILL)
        act.wait_ge(y_st[1], 16 * FILL)
        pairs = pair_count(act)

        def body(j, first, last):
            for s in range(2):
                b = 2 * j + s
                start = first and s == 0
                if not start:
                    a_high(b - 1, first)
                if not (last and s == 1):
                    for q in range(2):
                        x_high(1 - s, b + 1, q, start)
                if not first:
                    store_y(s, b - 2)
                if not (last and s == 1):
                    for c in range(2):
                        w_hi(1 - s, j + s, c)
                act.wait_ge(gu_done, b + 1)
                if not start:
                    act.wait_ge(act_done, b)
                act.activation(sil[:, :], psum[:, s, 0:DE], ACT.Silu).then_inc(sil_done, 1)
                w_hi(s, j, 2)
                if not start:
                    y_left(1 - s, j if s else j - 1, b - 1, first)

        over_pairs(act, pairs, body)
        a_high(2 * pairs - 1)
        store_y(0, 2 * pairs - 2)
        y_left(1, pairs - 1, 2 * pairs - 1)
        store_y(1, 2 * pairs - 1)
        for t in range(NT + 1):
            if t < NT:
                act.wait_ge(yg_in[t], 32)
                act.activation(ya[:, t, :], ya[:, t, :], ACT.Copy, scale=wgt[:, t, 0:1]).then_inc(f_scaled, 1)
            if t:
                n = t - 1
                act.wait_ge(f_sum, n + 1)
                act.activation(fsq[:, :], yo[:, n, :], ACT.Square, accum_out=rms[:, n:n + 1]).then_inc(f_ss, 1)
                act.wait_ge(f_inv, n + 1)
                act.activation(rms[:, 8 + n:9 + n], rms[:, 8 + n:9 + n], ACT.Sqrt).then_inc(f_rstd, 1)
        for t in range(NT):
            act.wait_ge(f_out, t + 1)
            dst = out["y_prompt"][0] if t == 0 else out["y_sample"][0, (t - 1) * P:t * P, :]
            act.dma_start(dst, yo[:, t, :]).then_inc(f_st, 16)
        act.wait_ge(f_st, 16 * NT)
        act.wait_ge(cout_st, 32 * len(CHAINS))
        act.wait_ge(m_st, 32)

    @block.vector
    def _(dve):
        steps = [0]

        def then(ins):
            steps[0] += 1
            ins.then_inc(dve_step, 1)
            dve.wait_ge(dve_step, steps[0])

        dve.wait_ge(pe_start, 1)
        dve.tensor_copy(vcol[:, :], psum[:, 4, 0:NV])
        dve.tensor_copy(taps[:, :], psum[:, 4, 128:128 + CK * CT]).then_inc(cols_done, 1)
        dve.wait_ge(cols_done, 1)
        dve.tensor_scalar(bqs[:, :], vcol[:, V_BQ:V_BQ + CT], QS, None, MUL)
        dve.wait_ge(x_ss, NT)
        then(dve.tensor_scalar(rms[:, 8:8 + NT], rms[:, 0:NT], 1.0 / D, EPS, MUL, ADD))
        dve.reciprocal(rms[:, 8:8 + NT], rms[:, 8:8 + NT]).then_inc(x_inv, 1)
        dve.wait_ge(x_rstd, 1)
        for t in range(NT):
            dve.tensor_scalar(x5[:, t, :], x5[:, t, :], rms[:, 8 + t:9 + t], None, MUL).then_inc(x_scaled, 1)
        dve.wait_ge(gate_in, GATE_IN)
        dve.tensor_tensor(gsum[:, :], gbias[:, 0:4:2], gbias[:, 1:4:2], ADD).then_inc(gsum_done, 1)
        dve.wait_ge(cst_hi, 1)
        dve.tensor_tensor(cst[:, :, 2:4], cs[:, :].rearrange("p (v k) -> p k v", v=2), cst[:, :, 0:2].bitcast(F32),
                          SUB).then_inc(cst_lo, 1)
        dve.wait_ge(wg_hi, 4)
        for d in range(2):
            for f in range(2):
                dst = slice(64 * f + 32 * d, 64 * f + 32 * d + H)
                dve.tensor_tensor(wgl[:, :, dst], wgr[:, :, 8 * d + 4 * f:8 * d + 4 * f + H],
                                  wgh[:, :, dst].bitcast(F32), SUB).then_inc(wg_lo, 1)
        dve.wait_ge(xt_free, 2 * NT)
        for k in range(KT):
            if k % 2 == 0:
                i, ks = k // 2, slice(k, k + 2)
                dve.wait_ge(tiny_done, 2 * i + 2)
                vec = lambda base: vcol[:, base + k:base + k + 2].unsqueeze(2).to_broadcast([P, 2, 2])
                mods = psum[:, 4 + i, 0:8].rearrange("p (m k v) -> p m k v", m=2, k=2)
                dve.tensor_tensor(sh1[:, ks, :], mods[:, 0, :, :], vec(V_BSH), ADD)
                then(dve.tensor_tensor(sc1[:, ks, :], mods[:, 1, :, :], vec(V_BSC), ADD))
                then(dve.scalar_tensor_tensor(out=sc1[:, ks, :], in0=sc1[:, ks, :], scalar=1.0, in1=vec(V_G1),
                                              op0=ADD, op1=MUL))
            for v, cols in ((0, slice(0, TP)), (1, slice(TP, T))):
                ins = dve.tensor_scalar(xt[:, k, cols], xt[:, k, cols], sc1[:, k, v:v + 1], sh1[:, k, v:v + 1], MUL, ADD)
            ins.then_inc(h_mod, 1)
            dve.wait_ge(h_hi, k + 1)
            dve.tensor_tensor(hl[:, k, :], xt[:, k, :], hh[:, k, :].bitcast(F32), SUB).then_inc(h_lo, 1)

        def conv_input(c):
            dve.wait_ge(z_free, TILE_AT["a", c] + 1)
            dve.tensor_tensor(conv[:, c, U0:U0 + TP], at[:, c % 2, 0:TP], sgt[:, c % 2, 0:TP], MUL)
            dve.tensor_tensor(lat(c, U1), at[:, c % 2, TP:T].rearrange("p (r w) -> p r w", w=GW),
                              sgt[:, c % 2, TP:T].rearrange("p (r w) -> p r w", w=GW), MUL).then_inc(u_done, 1)

        taken, last_tap = [0], [0] * CT

        def conv_taps(*taps_of):
            for n in range(max(last - first for _, first, last in taps_of)):
                for c, first, last in taps_of:
                    k = first + n
                    if k >= last:
                        continue
                    acc, src = conv[:, accp(c), 0:YW], conv[:, c, k:k + YW]
                    w = taps[:, k * CT + c:k * CT + c + 1]
                    if k == 0:
                        if c >= 2:
                            dve.wait_ge(conv_step, last_tap[c - 2])
                        ins = dve.tensor_scalar(acc, src, w, vcol[:, V_BDW + c:V_BDW + c + 1], MUL, ADD)
                    else:
                        dve.wait_ge(conv_step, last_tap[c])
                        ins = dve.scalar_tensor_tensor(out=acc, in0=src, scalar=w, in1=acc, op0=MUL, op1=ADD)
                    taken[0] += 1
                    last_tap[c] = taken[0]
                    ins.then_inc(conv_step, 1)

        HEAD = 10
        dve.wait_ge(consts, 11)
        conv_input(0)
        dve.wait_ge(u_done, 1)
        conv_taps((0, 0, HEAD))
        conv_input(1)
        dve.wait_ge(u_done, 2)
        conv_taps((0, HEAD, CK), (1, 0, CK - HEAD))
        conv_input(2)
        dve.wait_ge(u_done, 3)
        conv_taps((1, CK - HEAD, CK), (2, 0, HEAD))
        conv_input(3)
        dve.wait_ge(z_free, TILE_AT["gate", 0] + 1)
        dve.scalar_tensor_tensor(out=gz[0:64, 2, :], in0=gz[0:64, 1, :], scalar=-1.0, in1=gz[0:64, 1, :], op0=MUL,
                                 op1=MAX).then_inc(gate_abs, 1)
        dve.wait_ge(u_done, CT)
        conv_taps((2, HEAD, CK), (3, 0, CK - HEAD))
        dve.wait_ge(gate_ln, 1)
        dve.wait_ge(consts, 17)
        then(dve.scalar_tensor_tensor(out=gz[0:64, 1, :], in0=gz[0:64, 1, :], scalar=0.0, in1=gz[0:64, 2, :], op0=MIN,
                                      op1=SUB))
        fwd = lambda n, a0, a1: gz[0:32, n, a0:a1]
        bwd = lambda n, a0, a1: gz[32:64, n, a1 - 1:(a0 - 1 if a0 else None):-1]
        for dirn in (fwd, bwd):
            dve.tensor_tensor_scan(dirn(2, 0, T), dirn(5, 0, T), dirn(1, 0, T), 0.0, MUL, ADD)
            dve.tensor_tensor_scan(dirn(3, 0, TP), dirn(1, 0, TP), dirn(0, 0, TP), 0.0, ADD, MAX)
            start = m0[0:32, :] if dirn is fwd else m0[32:64, :]
            ins = dve.tensor_tensor_scan(dirn(3, TP, T), dirn(1, TP, T), dirn(0, TP, T), start, ADD, MAX)
        then(ins)
        dve.tensor_tensor(gz[0:64, 4, :], gz[0:64, 0, :], gz[0:64, 2, :], SUB)
        dve.memset(mprev[:, :], 0.0)
        then(dve.tensor_tensor(rrow[:, :], gz[0:64, 2, :], gz[0:64, 3, :], SUB))
        dve.tensor_copy(mprev[0:32, 1:2], m0[0:32, :])
        dve.tensor_copy(mprev[32:64, NT - 1:NT], m0[32:64, :])
        dve.tensor_copy(mprev[0:32, 2:NT], gz[0:32, 3, 2 * P - 1:T - P:P])
        dve.tensor_copy(mprev[32:64, 1:NT - 1], gz[32:64, 3, 2 * P:T:P])
        dve.tensor_copy(mend[0:32, :], gz[0:32, 3, P - 1:P])
        then(dve.tensor_copy(mend[32:64, :], gz[32:64, 3, 0:1]))
        dve.tensor_tensor(gz[0:64, 1, :].rearrange("p (t n) -> p t n", t=NT), rrow[:, :].rearrange("p (t n) -> p t n", t=NT),
                          mprev[:, :].unsqueeze(2).to_broadcast([64, NT, P]), ADD).then_inc(gate_max, 1)
        dve.wait_ge(gate_pe, 1)
        turned = flat[:, 4 * 512:4 * 512 + T].rearrange("p (t n) -> p t n", t=NT)
        em = psum[:, 6, 0:NT * 64].rearrange("p (t n) -> p t n", t=NT)
        for d in range(2):
            cols = slice(4 * d, 4 * d + H)
            dve.tensor_copy(tokg[:, 0, :, cols], turned[:, :, 32 * d:32 * d + H])
            dve.tensor_copy(tokg[:, 1, :, cols], turned[:, :, 64 + 32 * d:64 + 32 * d + H])
            dve.tensor_copy(tokg[:, 2, :, cols], em[:, :, 32 * d:32 * d + H])
        dve.tensor_copy(decay[:, :, :], psum[:, 7, 0:8 * NT].rearrange("p (c t) -> p c t", t=NT)).then_inc(gate_tables, 1)
        dve.wait_ge(gate_tables, 1)

        NSTEP = NT * len(CHAINS)
        TAPS_IN = [0]
        for n in range(NSTEP):
            TAPS_IN.append(min(TAPS_IN[-1] + (1 if n % NT else 0), HEAD))
        where = [(ci, i, chunk_order(CHAINS[ci][1])[i]) for ci in range(len(CHAINS)) for i in range(NT)]

        def weigh(n):
            ci, i, c = where[n]
            h, d = CHAINS[ci]
            dve.wait_ge(w_done, n + 1)
            dve.wait_ge(st_free, h + 1)
            if n >= 2:
                dve.wait_ge(mm_done, n - 1)
            last = 0 if d else P - 1
            ins = dve.tensor_tensor(pt[:, n % 2, :], st[:, c * P:(c + 1) * P], wt[:, n % 2, :], MUL)
            if i < NT - 1:
                ins = dve.tensor_scalar(kw[:, n % 2, :], ktok[:, h, c, :], wt[:, n % 2, last:last + 1], None, MUL)
            ins.then_inc(p_done, 1)

        for n in range(NSTEP):
            ci, i, c = where[n]
            h, d = CHAINS[ci]
            if i == 0:
                weigh(n)
            if i < NT - 1:
                weigh(n + 1)
            if TAPS_IN[n + 1] > TAPS_IN[n]:
                for k in range(CK - HEAD + TAPS_IN[n], CK - HEAD + TAPS_IN[n + 1]):
                    conv_taps((3, k, k + 1))
            dve.wait_ge(mm_done, n + 1)
            upd = psum[:, 6, 256:256 + HD + 1]
            if i == 0:
                if ci:
                    dve.wait_ge(cout_st, 32 * ci)
                dve.tensor_copy(num[:, c, :], psum[:, 6, 0:HD + 1])
                dve.tensor_copy(cout[:, :], upd).then_inc(num_done, 1)
            else:
                dve.wait_ge(t_done, (NT - 1) * ci + i)
                ins = dve.tensor_tensor(num[:, c, :], psum[:, 6, 0:HD + 1], inter[:, :], ADD)
                if i < NT - 1:
                    before = cn0[:, ci % 2, :] if i == 1 else cn[:, i % 2, :]
                    ins = dve.scalar_tensor_tensor(out=cn[:, (i + 1) % 2, :], in0=before,
                                                   scalar=decay[:, ci, c:c + 1], in1=upd, op0=MUL, op1=ADD)
                ins.then_inc(num_done, 1)
            if i == NT - 1:
                dve.wait_ge(num_done, n + 1)
                den = num[:, :, HD]
                then(dve.scalar_tensor_tensor(out=dn[:, 0, :], in0=den, scalar=-1.0, in1=den, op0=MUL, op1=MAX))
                then(dve.tensor_tensor(dn[:, 1, :], dn[:, 0, :], tokg[:, 2, :, 4 * d + h], MAX))
                then(dve.reciprocal(dn[:, 2, :], dn[:, 1, :]))
                if d == 0:
                    then(dve.tensor_tensor(hf[:, :, :], num[:, :, 0:HD], dn[:, 2, :].unsqueeze(2).to_broadcast([P, NT, HD]), MUL))
                else:
                    for t in range(NT):
                        ins = dve.scalar_tensor_tensor(out=ktok[:, h, t, :], in0=num[:, t, 0:HD], scalar=dn[:, 2, t:t + 1],
                                                       in1=hf[:, t, :], op0=MUL, op1=ADD)
                    then(ins)
        heads = ktok[:, :, :, :].rearrange("p h t n -> p (h t) n")
        dve.wait_ge(mm_done, NSTEP)
        then(dve.tensor_tensor(hsq[:, :, :], heads, heads, MUL))
        then(dve.tensor_reduce(hrs[:, 0, :], hsq[:, :, :], AX, ADD))
        then(dve.tensor_scalar(hrs[:, 0, :], hrs[:, 0, :], 1.0 / HD, EPS, MUL, ADD))
        dve.reciprocal(hrs[:, 1, :], hrs[:, 0, :]).then_inc(hn_inv, 1)
        dve.wait_ge(hn_rstd, 1)
        dve.tensor_tensor(heads, heads, hrs[:, 1, :].unsqueeze(2).to_broadcast([P, H * NT, HD]), MUL).then_inc(hn_scaled, 1)
        for h in range(H):
            dve.wait_ge(hmt_done, H)
            dve.wait_ge(z_free, TILE_AT["o", h] + 1)
            dve.tensor_tensor(hmt[:, h, :], hmt[:, h, :], sgt[:, h % 2, :], MUL).then_inc(o_done, 1)
        dve.wait_ge(ln_pe, 1)
        sums = psum[:, 4:6, 0:YW // 2]
        two = lambda t: t.rearrange("p (q n) -> p q n", q=2)
        then(dve.tensor_scalar(two(lnm[:, :]), sums, 1.0 / DI, None, MUL))
        for c in range(CT):
            dve.tensor_tensor(conv[:, accp(c), 0:YW], conv[:, accp(c), 0:YW], lnm[:, :], SUB).then_inc(ln_cent, 1)
        dve.wait_ge(ln_pe, 1 + CT)
        then(dve.tensor_scalar(two(lnr[:, :]), sums, 1.0 / DI, EPS, MUL, ADD))
        dve.reciprocal(lnr[:, :], lnr[:, :]).then_inc(ln_inv, 1)
        dve.wait_ge(ln_rstd, 1)
        for c in range(CT):
            dve.tensor_tensor(conv[:, accp(c), 0:YW], conv[:, accp(c), 0:YW], lnr[:, :], MUL).then_inc(ln_norm, 1)
        for c in range(CT):
            dve.wait_ge(b_hi, c + 1)
            dve.tensor_tensor(hl[:, c, 0:TP], conv[:, accp(c), 0:TP], hh[:, c, 0:TP].bitcast(F32), SUB)
            dve.tensor_tensor(hl[:, c, TP:T].rearrange("p (r w) -> p r w", w=GW), lat(accp(c), U1 - U0),
                              hh[:, c, TP:T].bitcast(F32).rearrange("p (r w) -> p r w", w=GW), SUB).then_inc(b_lo, 1)
        for h in range(H):
            dve.wait_ge(b_hi, CT + h + 1)
            dve.tensor_tensor(hl[:, CT + h, :], hmt[:, h, :], hh[:, CT + h, :].bitcast(F32), SUB).then_inc(b_lo, 1)
        dve.wait_ge(mrow_in, 16 * 3)
        then(dve.tensor_tensor(mrow[:, 0:2, :], mrow[:, 0:2, :], mrow[:, 2:4, :], ADD))
        then(dve.tensor_tensor(mrow[:, 0:2, :], mrow[:, 0:2, :], mbias[:, :].unsqueeze(1).to_broadcast([P, 2, 4 * D // P]), ADD))
        dve.scalar_tensor_tensor(out=mrow[64:96, 0:2, :], in0=mrow[64:96, 0:2, :], scalar=1.0,
                                 in1=mg2[64:96, :].unsqueeze(1).to_broadcast([32, 2, 4 * D // P]),
                                 op0=ADD, op1=MUL).then_inc(mrow_done, 1)
        dve.wait_ge(sga_done, 1)

        def merged_low(m):
            dve.wait_ge(m_hi, m + 1)
            dve.tensor_tensor(ml[:, m, :], mrg[:, m % 2, 0, :], mh[:, m, :].bitcast(F32), SUB).then_inc(m_lo, 1)

        for m in range(KT):
            if m >= 2:
                merged_low(m - 2)
            for br, gate in enumerate((sga, sgb)):
                n = 2 * m + br
                if m >= 2 and br == 0:
                    dve.wait_ge(m_lo, m - 1)
                dve.wait_ge(ab_done, n + 1)
                dve.tensor_tensor(two(mrg[:, m % 2, br, :]), psum[:, 2 * (n % 2):2 * (n % 2) + 2, 0:HALF],
                                  two(gate[:, m, :]), MUL).then_inc(ab_free, 1)
            dve.wait_ge(ab_free, 2 * m + 2)
            dve.tensor_tensor(mrg[:, m % 2, 0, :], mrg[:, m % 2, 0, :], mrg[:, m % 2, 1, :], ADD).then_inc(m_sum, 1)
        merged_low(KT - 2)
        merged_low(KT - 1)
        then(dve.tensor_tensor_scan(iota[:, :], ones[:, :], ones[:, :], -1.0, MUL, ADD))
        then(dve.tensor_tensor(tmp[:, 0, 0:P], ident[:, :], iota[:, :], MUL))
        then(dve.tensor_reduce(tokcol[:, :], tmp[:, 0, 0:P], AX, ADD))
        then(dve.tensor_scalar(upper[:, :], iota[:, :], tokcol[:, :], None, ALU.is_gt))
        dve.wait_ge(x2_in, 16 * NT)
        dve.wait_ge(mod_in, 16 * 6)
        def add_mixed(n):
            i, t = n // NT, n % NT
            v, cols = min(t, 1), slice(i * 256, (i + 1) * 256)
            dve.wait_ge(wo_done, n + 1)
            dve.tensor_tensor(tmp[:, n % 2, :], psum[:, n % 4, 0:256], bg1[:, v, cols], MUL).then_inc(wo_free, 1)
            dve.wait_ge(wo_free, n + 1)
            ins = dve.tensor_tensor(x2[:, t, cols], x2[:, t, cols], tmp[:, n % 2, :], ADD)
            ins.then_inc(x2_done if i == 3 else dve_step, 1)
            if i < 3:
                steps[0] += 1

        for n in range(3 * NT):
            add_mixed(n)
        for t in range(NT + 1):
            if t < NT:
                add_mixed(3 * NT + t)
            if t:
                m = t - 1
                v = min(m, 1)
                dve.wait_ge(h2_ss, m + 1)
                then(dve.tensor_scalar(rms[:, 24 + m:25 + m], rms[:, 16 + m:17 + m], 1.0 / D, EPS, MUL, ADD))
                dve.reciprocal(rms[:, 24 + m:25 + m], rms[:, 24 + m:25 + m]).then_inc(h2_inv, 1)
                dve.wait_ge(h2_rstd, m + 1)
                then(dve.scalar_tensor_tensor(out=h2[:, m, :], in0=x2[:, m, :], scalar=rms[:, 24 + m:25 + m],
                                              in1=bsc[:, v, :], op0=MUL, op1=MUL))
                dve.tensor_tensor(h2[:, m, :], h2[:, m, :], bsh[:, v, :], ADD).then_inc(h2_dve, 1)
        def w_lo(s, b, c):
            dve.wait_ge(e_hi, 2 * b + c + 1)
            dve.tensor_tensor(w_l[:, 2 * s + c, :], w_raw[:, 2 * s + c, :], w_h[:, 2 * s + c, :].bitcast(F32),
                              SUB).then_inc(e_lo, 1)

        dve.wait_ge(late_in, 16 * 5)
        dve.wait_ge(lg_done, 1)
        then(dve.tensor_tensor(lg[:, :, :], psum[:, 7, 0:NT * 20].rearrange("p (t n) -> p t n", t=NT),
                               rb[:, :].unsqueeze(1).to_broadcast([P, NT, 20]), ADD))
        routing(dve, then)
        def x_low(s, b, q):
            dve.wait_ge(x_hi, 2 * b + q + 1)
            dve.tensor_tensor(xl[:, s, 4 * q:4 * q + 4, :], psum[:, 2 + q, :].rearrange("p (k n) -> p k n", k=4),
                              xh[:, s, 4 * q:4 * q + 4, :].bitcast(F32), SUB).then_inc(x_lo, 1)

        def a_low(b):
            dve.wait_ge(a_hi, b + 1)
            dve.tensor_tensor(al[:, :, :], psum[:, 4, 0:DE].rearrange("p (j n) -> p j n", j=2), ah[:, :, :].bitcast(F32),
                              SUB).then_inc(a_lo, 1)

        def y_right(s, j, b, first=False):
            dve.wait_ge(e_used, b + 1)
            if not first:
                dve.wait_ge(y_st[s], 16 * (j + FILL))
            dve.tensor_copy(yy[:, s, 512:D], psum[:, 6, :]).then_inc(y_dve, 1)

        x_low(0, 0, 0)
        x_low(0, 0, 1)
        pairs = pair_count(dve)

        def body(j, first, last):
            for s in range(2):
                b = 2 * j + s
                start = first and s == 0
                if not start:
                    a_low(b - 1)
                if not (last and s == 1):
                    for q in range(2):
                        x_low(1 - s, b + 1, q)
                    w_lo(1 - s, b + 1, 0)
                dve.wait_ge(sil_done, b + 1)
                if not start:
                    dve.wait_ge(at_done, b)
                dve.tensor_tensor(act_[:, :], psum[:, s, DE:2 * DE], sil[:, :], MUL).then_inc(act_done, 1)
                if not (last and s == 1):
                    w_lo(1 - s, b + 1, 1)
                if not start:
                    y_right(1 - s, j if s else j - 1, b - 1, first)

        over_pairs(dve, pairs, body)
        a_low(2 * pairs - 1)
        y_right(1, pairs - 1, 2 * pairs - 1)
        dve.wait_ge(gate2_in, 32)
        for t in range(NT + 1):
            if t < NT:
                v = min(t, 1)
                dve.wait_ge(f_scaled, t + 1)
                dve.scalar_tensor_tensor(out=yo[:, t, :], in0=yb[:, t, :], scalar=wgt[:, t, 1:2], in1=ya[:, t, :],
                                         op0=MUL, op1=ADD).then_inc(f_both, 1)
                dve.wait_ge(f_both, t + 1)
                dve.tensor_tensor(yo[:, t, :], yo[:, t, :], bg2[:, v, :], MUL).then_inc(f_gated, 1)
            if t:
                n = t - 1
                dve.wait_ge(f_ss, n + 1)
                then(dve.tensor_scalar(rms[:, 8 + n:9 + n], rms[:, n:n + 1], 1.0 / D, EPS, MUL, ADD))
                dve.reciprocal(rms[:, 8 + n:9 + n], rms[:, 8 + n:9 + n]).then_inc(f_inv, 1)
                dve.wait_ge(f_rstd, n + 1)
                dve.scalar_tensor_tensor(out=yo[:, n, :], in0=yo[:, n, :], scalar=rms[:, 8 + n:9 + n], in1=gfb[:, :],
                                         op0=MUL, op1=MUL).then_inc(f_out, 1)

    top.close()


_INS = ["x_prompt", "x_sample", "state_C", "state_n", "state_m", "c", "c_ctx", "norm1_g", "w_ada", "b_ada", "w_in", "b_in",
        "b_gates", "w_dw", "b_dw", "conv_ln_g", "conv_ln_b", "w_conv_out", "mlstm_hn_g", "w_mlstm_out", "w_o", "norm2_g",
        "w_rg", "b_rg", "w_re", "b_re", "w_e_gate", "w_e_up", "w_e_down", "norm_final_g"]
_OUTS = [("y_prompt", (1, TP, D)), ("y_sample", (1, TL, D)), ("new_C", (1, 1, 2, H, HD, HD)), ("new_n", (1, 1, 2, H, HD)),
         ("new_m", (1, 1, 2, H))]


def kernel(**inputs):
    import numpy as np
    import concourse.bacc as bacc
    from concourse.bass_utils import run_bass_kernel_spmd

    nc = bacc.Bacc("TRN2", target_bir_lowering=False, num_devices=1)
    arrays, a, out = {}, {}, {}
    for name in _INS:
        x = np.ascontiguousarray(inputs[name])
        arrays[f"in_{name}"] = x
        a[name] = nc.dram_tensor(f"in_{name}", x.shape, mybir.dt.from_np(x.dtype), kind="ExternalInput").ap()
    for name, shape in _OUTS:
        out[name] = nc.dram_tensor(f"out_{name}", shape, F32, kind="ExternalOutput").ap()
    build(nc, a, out)
    r = run_bass_kernel_spmd(nc, [arrays], core_ids=[0])
    return tuple(r.results[0][f"out_{name}"] for name, _ in _OUTS)
```
